# Optimizing a Trainium2 kernel written in Bass

```python
import math
import jax, jax.numpy as jnp
from jax import lax
import numpy as np

D_MODEL = 1024
BATCH = 1
SEQ = 256
DEPTH = 1

N_META = 16
EPS = 1e-6
MLA_HEADS = 8
Q_LORA = 384
KV_LORA = 256
QK_NOPE = 64
QK_ROPE = 32
V_DIM = 64
ROPE_BASE = 10000.0
Q_BLOCK = 128
LRU_WIDTH = D_MODEL
LRU_BLOCKS = 8
LRU_BW = LRU_WIDTH // LRU_BLOCKS
CONV_WIDTH = 4
LRU_C = 8.0
N_EXPERTS = 32
TOP_K = 4
D_FF = D_MODEL
SWIGLU_ALPHA = 1.702
SWIGLU_LIMIT = 7.0
EXPERT_BLOCK = 128
OFF_CQ = 0
OFF_CKV = OFF_CQ + Q_LORA
OFF_KR = OFF_CKV + KV_LORA
OFF_RX = OFF_KR + QK_ROPE
OFF_RG = OFF_RX + LRU_WIDTH
OFF_GATE = OFF_RG + LRU_WIDTH
D_IN = OFF_GATE + 2 * D_MODEL

kernel_name = 'hybrid_mla_rglru_moe_meta'

def rms_norm(x, g):
    xf = x.astype(jnp.float32)
    var = jnp.mean(xf * xf, axis=-1, keepdims=True)
    return (xf * lax.rsqrt(var + EPS)).astype(x.dtype) * g

def rope_tables(T, dtype):
    inv = ROPE_BASE ** (-jnp.arange(0, QK_ROPE, 2, dtype=jnp.float32) / QK_ROPE)
    ang = jnp.arange(T, dtype=jnp.float32)[:, None] * inv[None, :]
    return jnp.cos(ang).astype(dtype), jnp.sin(ang).astype(dtype)

def apply_rope(x, cos, sin):
    x1, x2 = jnp.split(x, 2, axis=-1)
    return jnp.concatenate([x1 * cos - x2 * sin, x1 * sin + x2 * cos], axis=-1)

def causal_block_attention(q_nope, q_pe, k_nope, k_pe, v):
    B, T, H, _ = q_nope.shape
    n_blk = -(-T // Q_BLOCK)
    Tp = n_blk * Q_BLOCK
    pad = Tp - T

    def padt(a):
        return jnp.pad(a, [(0, 0), (0, pad)] + [(0, 0)] * (a.ndim - 2))

    q_nope, q_pe, k_nope, k_pe, v = padt(q_nope), padt(q_pe), padt(k_nope), padt(k_pe), padt(v)
    scale = (QK_NOPE + QK_ROPE) ** -0.5
    k_pos = jnp.arange(Tp)

    def one_block(i):
        s = i * Q_BLOCK
        qn = lax.dynamic_slice_in_dim(q_nope, s, Q_BLOCK, axis=1)
        qp = lax.dynamic_slice_in_dim(q_pe, s, Q_BLOCK, axis=1)
        scores = (jnp.einsum('bqhd,bkhd->bhqk', qn, k_nope, preferred_element_type=jnp.float32)
                  + jnp.einsum('bqhr,bkr->bhqk', qp, k_pe, preferred_element_type=jnp.float32))
        q_pos = s + jnp.arange(Q_BLOCK)
        mask = k_pos[None, :] <= q_pos[:, None]
        scores = jnp.where(mask, scores * scale, -jnp.inf)
        p = jax.nn.softmax(scores, axis=-1).astype(v.dtype)
        return jnp.einsum('bhqk,bkhd->bqhd', p, v)

    out = lax.map(one_block, jnp.arange(n_blk))
    out = jnp.moveaxis(out, 0, 1).reshape(B, Tp, H, V_DIM)
    return out[:, :T]

def mla_branch(p_cq, p_ckv, p_kr, q_norm_g, w_uq, kv_norm_g, w_ukv, w_ao, cos, sin):
    B, T, _ = p_cq.shape
    c_q = rms_norm(p_cq, q_norm_g)
    q = (c_q @ w_uq).reshape(B, T, MLA_HEADS, QK_NOPE + QK_ROPE)
    q_nope = q[..., :QK_NOPE]
    q_pe = apply_rope(q[..., QK_NOPE:], cos[:, None, :], sin[:, None, :])
    c_kv = rms_norm(p_ckv, kv_norm_g)
    kv = (c_kv @ w_ukv).reshape(B, T, MLA_HEADS, QK_NOPE + V_DIM)
    k_nope, v = kv[..., :QK_NOPE], kv[..., QK_NOPE:]
    k_pe = apply_rope(p_kr, cos, sin)
    o = causal_block_attention(q_nope, q_pe, k_nope, k_pe, v)
    return o.reshape(B, T, MLA_HEADS * V_DIM) @ w_ao

def rglru_branch(p_rx, p_rg, conv_w, conv_b, w_rg_a, b_rg_a, w_rg_x, b_rg_x, rg_lambda, w_ro):
    B, T, W = p_rx.shape
    xc = lax.conv_general_dilated(p_rx, conv_w[:, None, :], window_strides=(1,),
                                  padding=[(CONV_WIDTH - 1, 0)],
                                  dimension_numbers=('NWC', 'WIO', 'NWC'),
                                  feature_group_count=W) + conv_b
    xb = xc.reshape(B, T, LRU_BLOCKS, LRU_BW)
    r = jax.nn.sigmoid(jnp.einsum('btni,nij->btnj', xb, w_rg_a).reshape(B, T, W) + b_rg_a)
    ig = jax.nn.sigmoid(jnp.einsum('btni,nij->btnj', xb, w_rg_x).reshape(B, T, W) + b_rg_x)
    log_a = (-LRU_C * r.astype(jnp.float32)) * jax.nn.softplus(-rg_lambda.astype(jnp.float32))
    a = jnp.exp(log_a)
    b = jnp.sqrt(-jnp.expm1(2.0 * log_a)) * (ig * xc).astype(jnp.float32)

    def combine(left, right):
        a1, b1 = left
        a2, b2 = right
        return a1 * a2, a2 * b1 + b2

    _, h = lax.associative_scan(combine, (a, b), axis=1)
    y = h.astype(p_rx.dtype) * jax.nn.gelu(p_rg)
    return y @ w_ro

def moe_ffn(xn, w_router, b_router, w_up, b_up, w_down, b_down):
    B, T, D = xn.shape
    xt = xn.reshape(-1, D)
    N = xt.shape[0]
    logits = (xt @ w_router + b_router).astype(jnp.float32)
    top_val, top_idx = lax.top_k(logits, TOP_K)
    gates = jax.nn.softmax(top_val, axis=-1).astype(xn.dtype)
    NK = N * TOP_K
    e_flat = top_idx.reshape(-1)
    order = jnp.argsort(e_flat)
    e_sorted = e_flat[order]
    tok_sorted = order // TOP_K
    counts = jnp.bincount(e_flat, length=N_EXPERTS)
    padded = (counts + EXPERT_BLOCK - 1) // EXPERT_BLOCK * EXPERT_BLOCK
    start = jnp.cumsum(counts) - counts
    pend = jnp.cumsum(padded)
    pstart = pend - padded
    dest = pstart[e_sorted] + (jnp.arange(NK) - start[e_sorted])
    n_blocks = -(-NK // EXPERT_BLOCK) + N_EXPERTS
    P = n_blocks * EXPERT_BLOCK
    x_pad = jnp.zeros((P, D), xt.dtype).at[dest].set(xt[tok_sorted])
    block_e = jnp.minimum(jnp.searchsorted(pend, jnp.arange(n_blocks) * EXPERT_BLOCK, side='right'),
                          N_EXPERTS - 1)

    def expert_block(args):
        xb, e = args
        hdn = xb @ w_up[e] + b_up[e]
        x_glu = jnp.minimum(hdn[:, :D_FF], SWIGLU_LIMIT)
        x_lin = jnp.clip(hdn[:, D_FF:], -SWIGLU_LIMIT, SWIGLU_LIMIT)
        act = x_glu * jax.nn.sigmoid(SWIGLU_ALPHA * x_glu) * (x_lin + 1.0)
        return act @ w_down[e] + b_down[e]

    y_pad = lax.map(expert_block, (x_pad.reshape(n_blocks, EXPERT_BLOCK, D), block_e))
    y_sorted = y_pad.reshape(P, D)[dest]
    g_sorted = gates.reshape(-1)[order]
    y = jnp.zeros_like(xt).at[tok_sorted].add(y_sorted * g_sorted[:, None])
    return y.reshape(B, T, D)

def setup_inputs(seed: int = 0) -> dict:
    key = jax.random.key(seed)
    ks = jax.random.split(key, 32)
    f32 = jnp.float32

    def nrm(k, shape, scale):
        return jax.random.normal(k, shape, f32) * scale

    def gain(k, shape):
        return 1.0 + 0.01 * jax.random.normal(k, shape, f32)

    L = DEPTH
    a0 = jax.random.uniform(ks[13], (L, LRU_WIDTH), f32, 0.9, 0.999)
    return {
        'x': nrm(ks[0], (BATCH, SEQ, D_MODEL), 1.0),
        'meta_tokens': nrm(ks[1], (N_META, D_MODEL), 1.0),
        'norm_mix_g': gain(ks[2], (L, D_MODEL)),
        'w_in': nrm(ks[3], (L, D_MODEL, D_IN), D_MODEL ** -0.5),
        'b_gate': nrm(ks[4], (L, 2 * D_MODEL), 0.02),
        'q_norm_g': gain(ks[5], (L, Q_LORA)),
        'w_uq': nrm(ks[6], (L, Q_LORA, MLA_HEADS * (QK_NOPE + QK_ROPE)), Q_LORA ** -0.5),
        'kv_norm_g': gain(ks[7], (L, KV_LORA)),
        'w_ukv': nrm(ks[8], (L, KV_LORA, MLA_HEADS * (QK_NOPE + V_DIM)), KV_LORA ** -0.5),
        'w_ao': nrm(ks[9], (L, MLA_HEADS * V_DIM, D_MODEL), (MLA_HEADS * V_DIM) ** -0.5),
        'conv_w': nrm(ks[10], (L, CONV_WIDTH, LRU_WIDTH), CONV_WIDTH ** -0.5),
        'conv_b': nrm(ks[11], (L, LRU_WIDTH), 0.02),
        'w_rg_a': nrm(ks[12], (L, LRU_BLOCKS, LRU_BW, LRU_BW), LRU_BW ** -0.5),
        'b_rg_a': nrm(ks[14], (L, LRU_WIDTH), 0.02),
        'w_rg_x': nrm(ks[15], (L, LRU_BLOCKS, LRU_BW, LRU_BW), LRU_BW ** -0.5),
        'b_rg_x': nrm(ks[16], (L, LRU_WIDTH), 0.02),
        'rg_lambda': jnp.log(a0) - jnp.log1p(-a0),
        'w_ro': nrm(ks[17], (L, LRU_WIDTH, D_MODEL), LRU_WIDTH ** -0.5),
        'w_out': nrm(ks[18], (L, D_MODEL, D_MODEL), D_MODEL ** -0.5),
        'norm_ffn_g': gain(ks[19], (L, D_MODEL)),
        'w_router': nrm(ks[20], (L, D_MODEL, N_EXPERTS), D_MODEL ** -0.5),
        'b_router': nrm(ks[21], (L, N_EXPERTS), 0.01),
        'w_up': nrm(ks[22], (L, N_EXPERTS, D_MODEL, 2 * D_FF), D_MODEL ** -0.5),
        'b_up': nrm(ks[23], (L, N_EXPERTS, 2 * D_FF), 0.02),
        'w_down': nrm(ks[24], (L, N_EXPERTS, D_FF, D_MODEL), D_FF ** -0.5),
        'b_down': nrm(ks[25], (L, N_EXPERTS, D_MODEL), 0.02),
        'norm_final_g': gain(ks[26], (D_MODEL,)),
    }

def reference(x, meta_tokens, norm_mix_g, w_in, b_gate, q_norm_g, w_uq, kv_norm_g, w_ukv, w_ao,
              conv_w, conv_b, w_rg_a, b_rg_a, w_rg_x, b_rg_x, rg_lambda, w_ro, w_out,
              norm_ffn_g, w_router, b_router, w_up, b_up, w_down, b_down, norm_final_g):
    B = x.shape[0]
    meta = jnp.broadcast_to(meta_tokens[None].astype(x.dtype), (B, N_META, D_MODEL))
    h = jnp.concatenate([meta, x], axis=1)
    T = h.shape[1]
    cos, sin = rope_tables(T, h.dtype)
    for l in range(DEPTH):
        xn = rms_norm(h, norm_mix_g[l])
        proj = xn @ w_in[l]
        attn = mla_branch(proj[..., OFF_CQ:OFF_CKV], proj[..., OFF_CKV:OFF_KR], proj[..., OFF_KR:OFF_RX],
                          q_norm_g[l], w_uq[l], kv_norm_g[l], w_ukv[l], w_ao[l], cos, sin)
        rec = rglru_branch(proj[..., OFF_RX:OFF_RG], proj[..., OFF_RG:OFF_GATE], conv_w[l], conv_b[l],
                           w_rg_a[l], b_rg_a[l], w_rg_x[l], b_rg_x[l], rg_lambda[l], w_ro[l])
        g = jax.nn.sigmoid(proj[..., OFF_GATE:] + b_gate[l])
        merged = g[..., :D_MODEL] * attn + g[..., D_MODEL:] * rec
        h = h + merged @ w_out[l]
        h = h + moe_ffn(rms_norm(h, norm_ffn_g[l]), w_router[l], b_router[l],
                        w_up[l], b_up[l], w_down[l], b_down[l])
    h = rms_norm(h, norm_final_g)
    return h[:, N_META:]


_drawn_inputs = setup_inputs


def setup_inputs(seed=0):
    import zlib

    import numpy as np

    out = dict(_drawn_inputs(seed))
    spreads = {}
    factors = {'b_gate': 3.245,
     'q_norm_g': 4.503,
     'kv_norm_g': 3.686,
     'b_rg_a': 33.802,
     'b_rg_x': 13.977,
     'b_up': 5.218,
     'b_down': 20.99,
     'norm_final_g': 176.431,
     'conv_b': 3.084,
     'norm_ffn_g': 3.097,
     'b_router': 4.33}
    for name, (base, spread) in spreads.items():
        noise = np.random.default_rng([zlib.crc32(name.encode()), seed]).standard_normal(out[name].shape)
        drawn = base * np.exp(spread * noise) if base else spread * noise
        out[name] = __import__('jax').numpy.asarray(drawn.astype(out[name].dtype))
    for name, factor in factors.items():
        out[name] = (out[name] * factor).astype(out[name].dtype)
    return out
```

```python
import math
from contextlib import ExitStack

import numpy as np

import concourse.bass as bass
from concourse import mybir

F32 = mybir.dt.float32
I32 = mybir.dt.int32
ALU = mybir.AluOpType
ACT = mybir.ActivationFunctionType
AX_X = mybir.AxisListType.X

P = 128
D = 1024
N_META = 16
SEQ = 256
T = SEQ + N_META
EPS = 1e-6
HEADS = 8
Q_LORA, KV_LORA = 384, 256
NOPE, ROPE, VD = 64, 32, 64
QD = NOPE + ROPE
ROPE_BASE = 10000.0
CONV = 4
LRU_C = 8.0
E = 32
TOP_K = 4
F = 1024
ALPHA, LIMIT = 1.702, 7.0
OFF_CQ = 0
OFF_CKV = OFF_CQ + Q_LORA
OFF_KR = OFF_CKV + KV_LORA
OFF_RX = OFF_KR + ROPE
OFF_RG = OFF_RX + D
OFF_GATE = OFF_RG + D
KT = D // P
QT = Q_LORA // P
KVT = KV_LORA // P
TT = SEQ // P
SCALE = (NOPE + ROPE) ** -0.5
GELU_C = math.sqrt(2.0 / math.pi)
MASKED = -3.0e38

SLOTS = 16
SLOT = 2048
CAP = 64
BLOCKS = SEQ // CAP
UNROLL = 4
GROUPS = E // UNROLL
PER_EXPERT = 12
NCOL = E * BLOCKS + UNROLL

VEC_ROWS = [("norm_mix_g", 8), ("q_norm_g", 3), ("kv_norm_g", 2), ("b_gate", 16), ("conv_w", 32),
            ("conv_b", 8), ("b_rg_a", 8), ("b_rg_x", 8), ("rg_lambda", 8)]
VEC_AT = {}
_n = 0
for _name, _rows in VEC_ROWS:
    VEC_AT[_name] = _n
    _n += _rows
NVEC = _n

CA = {}
_n = 0
for _name, _w in (("ident", 128), ("ones", 128), ("mask", 272), ("rot", 32), ("cos", T), ("sin", T)):
    CA[_name] = (_n, _n + _w)
    _n += _w
NCA = _n
CB = {}
_n = 0
for _name, _w in (("upper", 128), ("slot_id", 128), ("pick", NCOL), ("block_base", NCOL)):
    CB[_name] = (_n, _n + _w)
    _n += _w
NCB = _n


def constants():
    a = np.zeros((P, NCA), np.float32)
    a[:, slice(*CA["ident"])] = np.eye(P, dtype=np.float32)
    a[:, slice(*CA["ones"])] = 1.0
    q, k = np.arange(P)[:, None], np.arange(P)[None, :]
    a[:, CA["mask"][0] + 144:CA["mask"][1]] = np.where(k <= q, 0.0, MASKED)
    half = ROPE // 2
    rot = np.zeros((ROPE, ROPE), np.float32)
    for r in range(half):
        rot[r + half, r] = -1.0
        rot[r, r + half] = 1.0
    a[NOPE:QD, slice(*CA["rot"])] = rot
    inv = (np.float32(ROPE_BASE) ** (-np.arange(0, ROPE, 2, dtype=np.float32) / np.float32(ROPE))).astype(np.float32)
    ang = np.arange(T, dtype=np.float32)[:, None] * inv[None, :]
    a[NOPE:QD, slice(*CA["cos"])] = np.tile(np.cos(ang).astype(np.float32).T, (2, 1))
    a[NOPE:QD, slice(*CA["sin"])] = np.tile(np.sin(ang).astype(np.float32).T, (2, 1))
    b = np.zeros((P, NCB), np.float32)
    b[:, slice(*CB["upper"])] = np.triu(np.ones((P, P), np.float32), 1)
    b[:, slice(*CB["slot_id"])] = np.arange(P) % CAP
    n = np.arange(NCOL)
    b[:E, slice(*CB["pick"])] = (n[None, :] % E == np.arange(E)[:, None])
    b[:, slice(*CB["block_base"])] = CAP * (n // E)
    return a, b


def mixer_loads():
    loads = [("in", 0, 256), ("in", 256, 256), ("in", 512, 160), ("in", OFF_RX, 256),
             ("uq", 0, 384), ("uq", 384, 384), ("ukv", 0, 1024), ("in", OFF_RG, 256), ("gates", 0, 2)]
    for p in range(1, 4):
        loads += [("in", OFF_RX + 256 * p, 256), ("in", OFF_RG + 256 * p, 256), ("gates", 2 * p, 2)]
    for h in range(2):
        loads += [("in", OFF_GATE + 512 * h, 256), ("in", OFF_GATE + 512 * h + 256, 256), ("ao", 512 * h, 512)]
    for p in range(4):
        loads += [("in", OFF_GATE + D + 256 * p, 256), ("ro", 256 * p, 256)]
    loads += [("out", 2 * r, 2) for r in range(4)]
    return loads


LOADS = mixer_loads()
M0 = len(LOADS)


def layer(nc, x_in, meta_in, vec_in, ca_in, cb_in, w_in, w_uq, w_ukv, w_ao, w_rg_a, w_rg_x, w_ro, w_out,
          norm_ffn_g, w_router, b_router, w_up, b_up, w_down, b_down, norm_final_g, out):
    with ExitStack() as ctx:
        def sb(name, shape, dt=F32):
            return ctx.enter_context(nc.sbuf_tensor(name, shape, dt))

        def sem(name):
            return ctx.enter_context(nc.semaphore(name))

        ring = sb("ring", [P, SLOTS, SLOT])
        X = sb("X", [P, TT, D])
        ca = sb("ca", [P, NCA])
        vec = sb("vec", [P, NVEC])
        small = sb("small", [P, 160])
        WORK = 16800
        work = sb("work", [P, WORK])
        ps = ctx.enter_context(nc.psum_tensor("ps", [P, 8, 512], F32))

        at = [0]

        def view(n, start=None):
            a = at[0] if start is None else start
            if start is None:
                at[0] += n
            assert a + n <= WORK, (a, n)
            return work[:, a:a + n]

        xnT = view(KT * T).rearrange("p (k t) -> p k t", k=KT)
        qh = view(HEADS * SEQ).rearrange("p (h t) -> p h t", h=HEADS)
        kh = view(HEADS * T).rearrange("p (h t) -> p h t", h=HEADS)
        vtok = view(3 * 512).rearrange("p (k n) -> p k n", k=3)
        cq_at = at[0]
        cq = view(QT * SEQ).rearrange("p (k t) -> p k t", k=QT)
        ckv_at = at[0]
        ckv = view(KVT * T).rearrange("p (k t) -> p k t", k=KVT)
        oT = view(4 * SEQ).rearrange("p (k t) -> p k t", k=4)
        rg_at = at[0]
        rxp = view(2 * (T + 3)).rearrange("p (k t) -> p k t", k=2)
        xc = view(2 * T).rearrange("p (k t) -> p k t", k=2)
        tr = view(2 * T).rearrange("p (k t) -> p k t", k=2)
        ti = view(2 * T).rearrange("p (k t) -> p k t", k=2)
        av = view(2 * T).rearrange("p (k t) -> p k t", k=2)
        th = view(2 * T).rearrange("p (k t) -> p k t", k=2)
        xg = view(2 * SEQ).rearrange("p (k t) -> p k t", k=2)
        ug = view(2 * SEQ).rearrange("p (k t) -> p k t", k=2)
        gel = view(KT * SEQ).rearrange("p (k t) -> p k t", k=KT)
        PT = view(2 * 384, cq_at).rearrange("p (b k q) -> p b k q", b=2, k=3)
        S = view(2 * T, ckv_at).rearrange("p (b t) -> p b t", b=2)
        xs = view(3 * D, rg_at).rearrange("p (k d) -> p k d", k=3)
        metab = view(D, rg_at + 3 * D)
        sqq = view(QT * SEQ, rg_at + 4 * D - 768).rearrange("p (k t) -> p k t", k=QT)
        sqk = view(KVT * T, cq_at + 1312).rearrange("p (k t) -> p k t", k=KVT)
        rq = view(SEQ, rg_at + 1100)
        rk = view(T, rg_at + 1100 + SEQ)
        ropeu = view(2 * SEQ, rg_at + 1700).rearrange("p (k t) -> p k t", k=2)
        m_at = KT * T
        vec_rows = view(P, m_at)[0:NVEC, :]
        mT = view(KT * SEQ, m_at).rearrange("p (k t) -> p k t", k=KT)
        ta = view(4 * SEQ, m_at + 2048).rearrange("p (k t) -> p k t", k=4)

        at[0] = 0
        cb = view(NCB)
        xn2 = view(TT * D).rearrange("p (i d) -> p i d", i=TT)
        gffn = view(D)
        bup = view(2 * F)
        bdn = view(D)
        wr = view(KT * E).rearrange("p (k e) -> p k e", k=KT)
        brt = view(E)
        posm = view(TT * NCOL).rearrange("p (i n) -> p i n", i=TT)
        gate = view(TT * NCOL).rearrange("p (i n) -> p i n", i=TT)
        sel = view(2 * CAP).rearrange("p (b t) -> p b t", b=2)
        pick = view(TT * CAP).rearrange("p (i t) -> p i t", i=TT)
        gpick = view(TT * P).rearrange("p (i t) -> p i t", i=TT)
        gpickT = view(2 * TT * P).rearrange("p (b i t) -> p b i t", b=2, i=TT)
        xe = view(512)
        xeT = view(512).rearrange("p (j t) -> p j t", j=4)
        hg = view(512)
        hl = view(512)
        sg = view(512)
        act_h = view(512)
        actT = view(512).rearrange("p (j t) -> p j t", j=4)
        y = view(512)
        gateT = view(SEQ)
        lg = view(TT * E).rearrange("p (i e) -> p i e", i=TT)
        selm = view(TT * E).rearrange("p (i e) -> p i e", i=TT)
        tmp = view(6 * E).rearrange("p (k e) -> p k e", k=6)
        gfin = view(D)
        xn2T_at = at[0]
        xn2T = view(KT * SEQ).rearrange("p (k t) -> p k t", k=KT)
        sqx = view(TT * D, xn2T_at).rearrange("p (i d) -> p i d", i=TT)
        sqf = sqx
        flag_i = sb("flag_i", [1, 1], I32)

        ident = ca[:, slice(*CA["ident"])]
        ones = ca[:, slice(*CA["ones"])]
        maskc = ca[:, slice(*CA["mask"])]
        rotm = ca[NOPE:QD, slice(*CA["rot"])]
        cosT = ca[NOPE:QD, slice(*CA["cos"])]
        sinT = ca[NOPE:QD, slice(*CA["sin"])]
        upper = cb[:, slice(*CB["upper"])]
        slot_id = cb[:, slice(*CB["slot_id"])]
        pick_e = cb[:, slice(*CB["pick"])]
        block_base = cb[:, slice(*CB["block_base"])]

        def v(name, i):
            c = VEC_AT[name] + i
            return vec[:, c:c + 1]

        sm_n = [0]

        def col(n):
            a = sm_n[0]
            sm_n[0] += n
            assert sm_n[0] <= 160
            return small[:, a:a + n]

        hc = col(8)
        nhc = col(8)
        hba = col(8)
        hbx = col(8)
        hbg = col(16)
        sp = col(32)
        ssx = col(3)
        rsx = col(3)
        mx = col(2)
        nmx = col(2)
        sm = col(2)
        rsm = col(2)
        ss2 = col(2)
        rs2 = col(2)
        top8 = col(16)
        nm1 = col(2)
        ngt = col(2)
        esum = col(2)
        cmax = col(2)
        ssf = col(2)
        rsf = col(2)

        const_in, vec_in_s, x_in_s, meta_in_s, moe_in = (sem(n) for n in
                                                         ("const_in", "vec_in_s", "x_in_s", "meta_in_s", "moe_in"))
        slot_loaded = [sem(f"slot_loaded{s}") for s in range(SLOTS)]
        weights_used = sem("weights_used")
        dve_chain, act_chain = sem("dve_chain"), sem("act_chain")
        vecT_done, vec_ready, softplus_in, sp_exp = sem("vecT_done"), sem("vec_ready"), sem("softplus_in"), sem("sp_exp")
        x_sumsq, x_var, x_std, xs_ready = sem("x_sumsq"), sem("x_var"), sem("x_std"), sem("xs_ready")
        proj_done, proj_read = sem("proj_done"), sem("proj_read")
        lora_sq, lora_sum, lora_var, lora_std, lora_ready = (sem(n) for n in
                                                             ("lora_sq", "lora_sum", "lora_var", "lora_std", "lora_ready"))
        krot_done, qrot_done, rope_ready, rope_read = (sem(n) for n in
                                                       ("krot_done", "qrot_done", "rope_ready", "rope_read"))
        scores_done, rowmax_ready, exp_done, probs_ready = (sem(n) for n in
                                                            ("scores_done", "rowmax_ready", "exp_done", "probs_ready"))
        scores_read, probsT_done, probsT_ready, attn_done, attn_ready = (sem(n) for n in
            ("scores_read", "probsT_done", "probsT_ready", "attn_done", "attn_ready"))
        conv_ready, gelu_arg, gelu_tanh, lru_arg, lru_sqrt, gelu_free, y_ready_s, gates_used = (sem(n) for n in
            ("conv_ready", "gelu_arg", "gelu_tanh", "lru_arg", "lru_sqrt", "gelu_free", "y_ready_s", "gates_used"))
        branch_done, branch_read, h_ready = (sem(n) for n in
                                                       ("branch_done", "branch_read", "h_ready"))
        h_sumsq, h_var, h_std, xn2_ready, xn2T_done, xn2T_ready = (sem(n) for n in
            ("h_sumsq", "h_var", "h_std", "xn2_ready", "xn2T_done", "xn2T_ready"))
        logits_done, gexp_done, mask_ready, pos_done, gate_ready, gateT_done, gateT_ready, bdn_done = (
            sem(n) for n in ("logits_done", "gexp_done", "mask_ready", "pos_done", "gate_ready",
                             "gateT_done", "gateT_ready", "bdn_done"))
        flag_ready = sem("flag_ready")
        route_ready, gather_done, xe_ready, xeT_done, xeT_ready = (sem(n) for n in
            ("route_ready", "gather_done", "xe_ready", "xeT_done", "xeT_ready"))
        gpickT_done, gpickT_ready, hidden_read, glu_ready, sig_done, act_ready = (sem(n) for n in
            ("gpickT_done", "gpickT_ready", "hidden_read", "glu_ready", "sig_done", "act_ready"))
        actT_done, actT_ready, y_ready, scat_done, scat_added = (sem(n) for n in
            ("actT_done", "actT_ready", "y_ready", "scat_done", "scat_added"))
        f_sumsq, f_var, f_std, fin_ready, out_stored = (sem(n) for n in
                                                        ("f_sumsq", "f_var", "f_std", "fin_ready", "out_stored"))

        lru_tanh, last_added, last_scat, xs_read, ssx_set, hc_ready, lin_ready = (sem(n) for n in
            ("lru_tanh", "last_added", "last_scat", "xs_read", "ssx_set", "hc_ready", "lin_ready"))

        block = ctx.enter_context(nc.Block())

        jobs = []
        jobs += [("xT", i) for i in range(KT)]
        jobs += [("cq", i) for i in range(QT)] + [("ckv", i) for i in range(KVT)] + [("kr", 0)]
        jobs += [("rx", 0), ("rx", 1)]
        jobs += [("q", h) for h in range(HEADS)] + [("k", h) for h in range(HEADS)] + [("v", i) for i in range(3)]
        jobs += [("rg", 0), ("rg", 1), ("ra", 0), ("ra", 1), ("ri", 0), ("ri", 1)]
        for p in range(1, 4):
            for kinds in (("rx", "rg"), ("ra", "ri")):
                jobs += [(kind, i) for kind in kinds for i in (2 * p, 2 * p + 1)]
        jobs += [("ga", i) for i in range(4)] + [("ga", i) for i in range(4, 8)]
        jobs += [("gr", i) for i in range(8)]
        JOB = {job: n for n, job in enumerate(jobs)}

        UNITS = [(h, b) for h in range(HEADS) for b in range(TT)]
        NU = len(UNITS)
        step_after = {}
        slots_for_steps = [j for j in jobs if j[0] in ("rx", "rg") and j[1] >= 2] + \
            [("ra", 2), ("ri", 2), ("ra", 4), ("ri", 4), ("ra", 6), ("ri", 6)]
        slots_for_steps.sort(key=lambda j: JOB[j])
        for s in range(NU + 2):
            step_after[slots_for_steps[s]] = s
        assert len(slots_for_steps) >= NU + 2

        def nk(b):
            return N_META + P * (b + 1)

        def ktiles(b):
            return [(t, min(P, nk(b) - P * t)) for t in range(3) if nk(b) > P * t]

        @block.sync
        def _(spe):
            for k in range(3):
                src = x_in[0, P * k:P * k + P, :] if k < 2 else meta_in[:, :]
                if k < 2:
                    spe.dma_start(X[:, k, :], src).then_inc(x_in_s, 16)
                else:
                    spe.dma_start(metab[0:N_META, :], src).then_inc(meta_in_s, 16)
            kview = w_in[0].rearrange("(k p) n -> p k n", p=P)
            for n, (kind, a, w) in enumerate(LOADS):
                s = n % SLOTS
                if n >= SLOTS:
                    spe.wait_ge(weights_used, n - SLOTS + 1)
                if kind == "in":
                    parts = [(KT * w, kview[:, :, a:a + w], KT)]
                elif kind == "ro":
                    parts = [(KT * w, w_ro[0].rearrange("(k p) n -> p k n", p=P)[:, :, a:a + w], KT)]
                elif kind == "uq":
                    parts = [(QT * w, w_uq[0].rearrange("(k p) n -> p k n", p=P)[:, :, a:a + w], QT)]
                elif kind == "ukv":
                    parts = [(KVT * w, w_ukv[0].rearrange("(k p) n -> p k n", p=P), KVT)]
                elif kind == "ao":
                    parts = [(4 * w, w_ao[0].rearrange("(k p) n -> p k n", p=P)[:, :, a:a + w], 4)]
                elif kind == "out":
                    parts = [(2 * D, w_out[0].rearrange("(k p) n -> p k n", p=P)[:, a:a + w, :], 2)]
                else:
                    parts = [(2 * P, w_rg_a[0].rearrange("b i j -> i b j")[:, a:a + w, :], 2),
                             (2 * P, w_rg_x[0].rearrange("b i j -> i b j")[:, a:a + w, :], 2)]
                o = 0
                for width, src, k in parts:
                    spe.dma_start(ring[:, s, o:o + width].rearrange("p (k n) -> p k n", k=k), src)\
                       .then_inc(slot_loaded[s], 16)
                    o += width

            def expert_loads(it, i):
                for u in range(UNROLL):
                    for c in range(PER_EXPERT):
                        m = u * PER_EXPERT + c
                        s = (M0 + m) % SLOTS
                        spe.wait_ge(weights_used, it * (UNROLL * PER_EXPERT) + (M0 + m - SLOTS + 1))
                        if c < KT:
                            src = w_up[0, i * UNROLL + u, P * c:P * c + P, :]
                            dst = ring[:, s, :]
                        else:
                            r = 2 * P * (c - KT)
                            src = w_down[0, i * UNROLL + u, r:r + 2 * P, :].rearrange("(k p) n -> p k n", p=P)
                            dst = ring[:, s, :].rearrange("p (k n) -> p k n", k=2)
                        spe.dma_start(dst, src).then_inc(slot_loaded[s], 16)

            with spe.Fori(0, GROUPS) as it:
                expert_loads(it, it)
            spe.wait_ge(flag_ready, 1)
            over = spe.value_load(flag_i[0:1, 0:1], min_val=0, max_val=1)
            with spe.If(over > 0):
                with spe.Fori(1, BLOCKS) as j:
                    with spe.Fori(0, GROUPS) as i:
                        expert_loads(j * GROUPS + i, i)
            for i in range(TT):
                spe.wait_ge(fin_ready, i + 1)
                spe.dma_start(out[0, P * i:P * i + P, :], X[:, i, :]).then_inc(out_stored, 16)
            spe.wait_ge(out_stored, 16 * TT)

        @block.gpsimd
        def _(pool):
            pool.dma_start(ca[:, :], ca_in[:, :]).then_inc(const_in, 16)
            pool.dma_start(vec_rows, vec_in[:, :]).then_inc(vec_in_s, 16)
            pool.wait_ge(h_ready, TT)
            pool.dma_start(gffn, norm_ffn_g[0:1, :].broadcast_to([P, D])).then_inc(moe_in, 16)
            pool.dma_start(wr, w_router[0].rearrange("(k p) e -> p k e", p=P)).then_inc(moe_in, 16)
            pool.dma_start(brt[0:1, :], b_router[0:1, :]).then_inc(moe_in, 16)
            pool.dma_start(cb, cb_in[:, :]).then_inc(moe_in, 16)
            pool.dma_start(bup[0:E, :], b_up[0]).then_inc(moe_in, 16)
            pool.dma_start(bdn[0:E, :], b_down[0]).then_inc(moe_in, 16)
            pool.dma_start(gfin, norm_final_g.rearrange("(a d) -> a d", a=1).broadcast_to([P, D])).then_inc(moe_in, 16)

        @block.tensor
        def _(pe):
            owed = [0]

            def settle(ins):
                if owed[0]:
                    ins.then_inc(weights_used, owed[0])
                    owed[0] = 0

            def slot_of(n):
                return n % SLOTS

            def wait_load(n):
                s = slot_of(n)
                total = sum(32 if LOADS[m][0] == "gates" else 16 for m in range(s, n + 1, SLOTS))
                pe.wait_ge(slot_loaded[s], total)

            def wslot(n, k):
                return ring[:, slot_of(n), :].rearrange("p (k n) -> p k n", k=k)

            load_at = {}
            for n, (kind, a, w) in enumerate(LOADS):
                load_at[(kind, a)] = n

            def begin(job):
                n = JOB[job]
                if n >= 4:
                    pe.wait_ge(proj_read, n - 3)
                return n % 4

            def in_cols(c):
                for (kind, a), n in load_at.items():
                    if kind == "in" and a <= c < a + LOADS[n][2]:
                        return n, c - a, LOADS[n][2]

            def project(job, c, width, lo, hi, part=0, last=False):
                n, o, w = in_cols(c)
                wait_load(n)
                b = begin(job)
                wv = ring[:, slot_of(n), 0:KT * w].rearrange("p (k n) -> p k n", k=KT)
                for k in range(KT):
                    ins = nc.tensor.matmul(ps[part:part + width, b, 0:hi - lo], wv[:, k, o:o + width],
                                           xnT[:, k, lo:hi], start=(k == 0), stop=(k == KT - 1))
                    if k == 0:
                        settle(ins)
                ins.then_inc(proj_done, 1)
                if last:
                    owed[0] += 1

            pe.wait_ge(vec_in_s, 16)
            pe.wait_ge(const_in, 16)
            nc.tensor.transpose(ps[:, 7, 0:NVEC], vec_rows, ident[0:NVEC, 0:NVEC]).then_inc(vecT_done, 1)

            pe.wait_ge(xs_ready, 3)
            for i in range(KT):
                b = begin(("xT", i))
                c = slice(P * i, P * i + P)
                nc.tensor.transpose(ps[:, b, 0:N_META], xs[0:N_META, 2, c], ident[0:N_META, 0:N_META])
                nc.tensor.transpose(ps[:, b, N_META:N_META + P], xs[:, 0, c], ident)
                nc.tensor.transpose(ps[:, b, N_META + P:T], xs[:, 1, c], ident).then_inc(proj_done, 1)
            pe.wait_ge(proj_read, KT)

            for i in range(QT):
                project(("cq", i), OFF_CQ + P * i, P, N_META, T, last=(i == 1))
            for i in range(KVT):
                project(("ckv", i), OFF_CKV + P * i, P, 0, T, last=(i == 0))
            project(("kr", 0), OFF_KR, ROPE, 0, T, part=NOPE, last=True)
            project(("rx", 0), OFF_RX, P, 0, T)
            project(("rx", 1), OFF_RX + P, P, 0, T, last=True)

            pe.wait_ge(lora_sq, 2)
            for k in range(QT):
                ins = nc.tensor.matmul(ps[:, 4, 0:SEQ], ones, sqq[:, k, :], start=(k == 0), stop=(k == QT - 1))
            ins.then_inc(lora_sum, 1)
            for k in range(KVT):
                ins = nc.tensor.matmul(ps[:, 5, 0:T], ones, sqk[:, k, :], start=(k == 0), stop=(k == KVT - 1))
            ins.then_inc(lora_sum, 1)
            pe.wait_ge(proj_read, JOB[("kr", 0)] + 1)
            nc.tensor.matmul(ps[NOPE:QD, 6, 0:T], rotm, kh[NOPE:QD, 0, :], start=True, stop=True).then_inc(krot_done, 1)

            pe.wait_ge(lora_ready, 1)
            for h in range(HEADS):
                n = load_at[("uq", 384 * (h // 4))]
                wait_load(n)
                b = begin(("q", h))
                wv = ring[:, slot_of(n), 0:QT * 384].rearrange("p (k n) -> p k n", k=QT)
                for k in range(QT):
                    ins = nc.tensor.matmul(ps[0:QD, b, 0:SEQ], wv[:, k, QD * (h % 4):QD * (h % 4) + QD], cq[:, k, :],
                                           start=(k == 0), stop=(k == QT - 1))
                    if k == 0:
                        settle(ins)
                ins.then_inc(proj_done, 1)
                if h % 4 == 3:
                    owed[0] += 1
            pe.wait_ge(lora_ready, 2)
            n = load_at[("ukv", 0)]
            wait_load(n)
            wv = wslot(n, KVT)
            for h in range(HEADS):
                b = begin(("k", h))
                for k in range(KVT):
                    ins = nc.tensor.matmul(ps[0:NOPE, b, 0:T], wv[:, k, P * h:P * h + NOPE], ckv[:, k, :],
                                           start=(k == 0), stop=(k == KVT - 1))
                    if k == 0:
                        settle(ins)
                ins.then_inc(proj_done, 1)
            for t in range(3):
                b = begin(("v", t))
                m = min(P, T - P * t)
                for k in range(KVT):
                    ins = nc.tensor.matmul(ps[0:m, b, :].rearrange("p (h d) -> p h d", h=HEADS),
                                           ckv[:, k, P * t:P * t + m],
                                           wv[:, k, :].rearrange("p (h d) -> p h d", h=HEADS)[:, :, NOPE:P],
                                           start=(k == 0), stop=(k == KVT - 1))
                ins.then_inc(proj_done, 1)
            owed[0] += 1

            project(("rg", 0), OFF_RG, P, N_META, T)
            project(("rg", 1), OFF_RG + P, P, N_META, T, last=True)

            pe.wait_ge(proj_read, JOB[("q", HEADS - 1)] + 1)
            pe.wait_ge(rope_ready, 1)
            pe.wait_ge(lora_var, 2)
            for g in range(4):
                nc.tensor.matmul(ps[NOPE:QD, 4 + g, :].rearrange("p (h t) -> p h t", h=2), rotm,
                                 qh[NOPE:QD, 2 * g:2 * g + 2, :], start=True, stop=True).then_inc(qrot_done, 1)

            def attention_step(s):
                if s < NU:
                    h, b = UNITS[s]
                    if s == 0:
                        pe.wait_ge(rope_ready, 5)
                        pe.wait_ge(proj_read, JOB[("v", 2)] + 1)
                    if s >= 2:
                        pe.wait_ge(scores_read, s - 1)
                    nc.tensor.matmul(ps[:, 4 + s % 2, 0:nk(b)], qh[0:QD, h, P * b:P * b + P], kh[0:QD, h, 0:nk(b)],
                                     start=True, stop=True).then_inc(scores_done, 1)
                if 1 <= s <= NU:
                    r = s - 1
                    b = UNITS[r][1]
                    pe.wait_ge(probs_ready, r + 1)
                    if r >= 1:
                        pe.wait_ge(probsT_ready, r)
                    for t, m in ktiles(b):
                        ins = nc.tensor.transpose(ps[0:m, 6, P * t:P * t + P], S[:, r % 2, P * t:P * t + m], ident)
                    ins.then_inc(probsT_done, 1)
                if s >= 2:
                    r = s - 2
                    h, b = UNITS[r]
                    pe.wait_ge(probsT_ready, r + 1)
                    if r >= 1:
                        pe.wait_ge(attn_ready, r)
                    o = VD * (h % 2)
                    kts = ktiles(b)
                    for t, m in kts:
                        ins = nc.tensor.matmul(ps[o:o + VD, 7, 0:P], vtok[0:m, t, VD * h:VD * h + VD],
                                               PT[0:m, r % 2, t, :], start=(t == 0), stop=(t == kts[-1][0]))
                    ins.then_inc(attn_done, 1)

            def lru_gates(p):
                n = load_at[("gates", 2 * p)]
                wait_load(n)
                wv = ring[:, slot_of(n), 0:4 * P].rearrange("p (g k n) -> p g k n", g=2, k=2)
                for g, name in ((0, "ra"), (1, "ri")):
                    for k in range(2):
                        i = 2 * p + k
                        b = begin((name, i))
                        pe.wait_ge(conv_ready, i + 1)
                        ins = nc.tensor.matmul(ps[:, b, 0:T], wv[:, g, k, :], xc[:, k, :], start=True, stop=True)
                        ins.then_inc(proj_done, 1)
                        if g == 1 and k == 1:
                            owed[0] += 1
                        if (name, i) in step_after:
                            attention_step(step_after[(name, i)])

            lru_gates(0)
            for p in range(1, 4):
                for name, off, lo in (("rx", OFF_RX, 0), ("rg", OFF_RG, N_META)):
                    for k in range(2):
                        i = 2 * p + k
                        project((name, i), off + P * i, P, lo, T, last=(k == 1))
                        if (name, i) in step_after:
                            attention_step(step_after[(name, i)])
                lru_gates(p)

            n_out = [0]

            def branch_begin():
                d = n_out[0]
                n_out[0] += 1
                if d >= 4:
                    pe.wait_ge(branch_read, d - 3)
                return 4 + d % 4

            pe.wait_ge(attn_ready, NU)
            for g in range(2):
                for i in range(4 * g, 4 * g + 4):
                    project(("ga", i), OFF_GATE + P * i, P, N_META, T, last=(i % 2 == 1))
                n = load_at[("ao", 512 * g)]
                wait_load(n)
                wv = wslot(n, 4)
                for i in range(4):
                    b = branch_begin()
                    for k in range(4):
                        ins = nc.tensor.matmul(ps[:, b, 0:SEQ], wv[:, k, P * i:P * i + P], oT[:, k, :],
                                               start=(k == 0), stop=(k == 3))
                        if k == 0:
                            settle(ins)
                    ins.then_inc(branch_done, 1)
                owed[0] += 1
            for p in range(4):
                for i in (2 * p, 2 * p + 1):
                    project(("gr", i), OFF_GATE + D + P * i, P, N_META, T, last=(i % 2 == 1))
                n = load_at[("ro", 256 * p)]
                wait_load(n)
                wv = wslot(n, KT)
                if p == 0:
                    pe.wait_ge(y_ready_s, 4)
                for i in range(2):
                    b = branch_begin()
                    for k in range(KT):
                        ins = nc.tensor.matmul(ps[:, b, 0:SEQ], wv[:, k, P * i:P * i + P], gel[:, k, :],
                                               start=(k == 0), stop=(k == KT - 1))
                        if k == 0:
                            settle(ins)
                    ins.then_inc(branch_done, 1)
                owed[0] += 1

            pe.wait_ge(proj_read, len(jobs))
            for r in range(4):
                n = load_at[("out", 2 * r)]
                wait_load(n)
                wv = wslot(n, 2)
                pe.wait_ge(branch_read, 8 + 2 * r + 2)
                for k in range(2):
                    for i in range(TT):
                        for c in range(2):
                            ins = nc.tensor.matmul(ps[:, 2 * i + c, :], mT[:, 2 * r + k, P * i:P * i + P],
                                                   wv[:, k, 512 * c:512 * c + 512],
                                                   start=(r == 0 and k == 0), stop=(r == 3 and k == 1))
                            if k == 0:
                                settle(ins)
                ins.then_inc(weights_used, 1)

            for i in range(TT):
                pe.wait_ge(xn2_ready, i + 1)
                for k in range(KT):
                    ins = nc.tensor.transpose(ps[:, 4 + k // 2, SEQ * (k % 2) + P * i:SEQ * (k % 2) + P * i + P],
                                              xn2[:, i, P * k:P * k + P], ident)
            ins.then_inc(xn2T_done, 1)

            pe.wait_ge(xn2T_ready, 1)
            for i in range(TT):
                for k in range(KT):
                    nc.tensor.matmul(ps[:, i, 0:E], xn2T[:, k, P * i:P * i + P], wr[:, k, :], start=(k == 0), stop=False)
                ins = nc.tensor.matmul(ps[:, i, 0:E], ones[0:1, :], brt[0:1, :], start=False, stop=True)
            ins.then_inc(logits_done, 1)

            pe.wait_ge(mask_ready, TT)
            nc.tensor.matmul(ps[:, 2, 0:E], upper, selm[:, 0, :], start=True, stop=True)
            nc.tensor.matmul(ps[:, 2, E:2 * E], ones, selm[:, 0, :], start=True, stop=False, skip_group_check=True)
            nc.tensor.matmul(ps[:, 2, E:2 * E], upper, selm[:, 1, :], start=False, stop=True, skip_group_check=True)
            nc.tensor.matmul(ps[:, 3, 0:E], ones, selm[:, 0, :], start=True, stop=False)
            nc.tensor.matmul(ps[:, 3, 0:E], ones, selm[:, 1, :], start=False, stop=True).then_inc(pos_done, 1)

            pe.wait_ge(gate_ready, 1)
            nc.tensor.transpose(ps[0:E, 4, 0:P], gate[:, 0, 0:E], ident)
            nc.tensor.transpose(ps[0:E, 4, P:2 * P], gate[:, 1, 0:E], ident).then_inc(gateT_done, 1)
            pe.wait_ge(gateT_ready, 1)
            for i in range(TT):
                for c in range(2):
                    nc.tensor.matmul(ps[:, 6 + c, :], gateT[0:E, P * i:P * i + P], bdn[0:E, 512 * c:512 * c + 512],
                                     start=True, stop=True).then_inc(bdn_done, 1)
                pe.wait_ge(scat_added, i + 1)

            def gather():
                for c in range(2):
                    for i in range(TT):
                        ins = nc.tensor.matmul(ps[CAP * c:CAP * c + CAP, 2, :], pick[:, i, :],
                                               xn2[:, i, 512 * c:512 * c + 512], start=(i == 0), stop=(i == TT - 1))
                ins.then_inc(gather_done, 1)

            def turn_route():
                for i in range(TT):
                    ins = nc.tensor.transpose(ps[:, 5, P * i:P * i + P], gpick[:, i, :], ident)
                ins.then_inc(gpickT_done, 1)

            def turn_gathered():
                for j in range(4):
                    ins = nc.tensor.transpose(ps[:, 3, P * j:P * j + P], xe[:, P * j:P * j + P], ident)
                ins.then_inc(xeT_done, 1)

            def scatter(u, i, it):
                pe.wait_ge(scat_added, (it * UNROLL + u) * TT + i + TT)
                for c in range(2):
                    ins = nc.tensor.matmul(ps[:, 6 + c, :], gpickT[CAP * c:CAP * c + CAP, (u + 1) % 2, i, :],
                                           y[CAP * c:CAP * c + CAP, :], start=True, stop=True)
                ins.then_inc(scat_done, 1)

            pe.wait_ge(route_ready, 1)
            gather()
            turn_route()
            pe.wait_ge(xe_ready, 1)
            turn_gathered()

            def experts(it):
                for u in range(UNROLL):
                    n = it * UNROLL + u
                    w0 = u * PER_EXPERT
                    def loaded(m):
                        s = (M0 + m) % SLOTS
                        before = sum(32 if LOADS[q][0] == "gates" else 16 for q in range(s, M0, SLOTS))
                        pe.wait_ge(slot_loaded[s], it * (16 * UNROLL * PER_EXPERT // SLOTS) + (before + 16 * (m // SLOTS + 1)))
                        return s
                    pe.wait_ge(hidden_read, n + 1)
                    pe.wait_ge(xeT_ready, n + 1)
                    for q in range(4):
                        c, b = q % 2, q // 2
                        nc.tensor.matmul(ps[CAP * c:CAP * c + CAP, b, :], sel[0:E, u % 2, :],
                                         bup[0:E, 512 * q:512 * q + 512], start=True, stop=False)
                    for k in range(KT):
                        s = loaded(w0 + k)
                        g, j = k // 4, k % 4
                        for q in range(4):
                            c, b = q % 2, q // 2
                            ins = nc.tensor.matmul(ps[CAP * c:CAP * c + CAP, b, :], xeT[:, j, CAP * g:CAP * g + CAP],
                                                   ring[:, s, 512 * q:512 * q + 512], start=False, stop=(k == KT - 1))
                        ins.then_inc(weights_used, 1)
                        if k == 1:
                            pe.wait_ge(y_ready, n + 1)
                            scatter(u, 0, it)
                        if k == 4:
                            scatter(u, 1, it)
                    pe.wait_ge(route_ready, n + 2)
                    pe.wait_ge(xe_ready, n + 1)
                    gather()
                    pe.wait_ge(gpickT_ready, n + 1)
                    turn_route()
                    pe.wait_ge(act_ready, n + 1)
                    for j in range(4):
                        ins = nc.tensor.transpose(ps[:, 4, P * j:P * j + P], act_h[:, P * j:P * j + P], ident)
                    ins.then_inc(actT_done, 1)
                    pe.wait_ge(xe_ready, n + 2)
                    turn_gathered()
                    pe.wait_ge(actT_ready, n + 1)
                    pe.wait_ge(gpickT_ready, n + 2)
                    for t in range(4):
                        s = loaded(w0 + KT + t)
                        wv = ring[:, s, :].rearrange("p (k n) -> p k n", k=2)
                        for k in range(2):
                            f = 2 * t + k
                            g, j = f // 4, f % 4
                            for c in range(2):
                                ins = nc.tensor.matmul(ps[CAP * c:CAP * c + CAP, 5, :], actT[:, j, CAP * g:CAP * g + CAP],
                                                       wv[:, k, 512 * c:512 * c + 512], start=(f == 0), stop=(f == 7))
                        ins.then_inc(weights_used, 1)

            with pe.Fori(0, GROUPS) as it:
                experts(it)
            pe.wait_ge(y_ready, E + 1)
            pe.wait_ge(scat_added, TT * (E + 1))
            pe.wait_ge(flag_ready, 1)
            over = pe.value_load(flag_i[0:1, 0:1], min_val=0, max_val=1)
            with pe.If(over > 0):
                with pe.Fori(1, BLOCKS) as j:
                    with pe.Fori(0, GROUPS) as i:
                        experts(j * GROUPS + i)
                pe.wait_ge(y_ready, BLOCKS * E + 1)
                pe.wait_ge(scat_added, TT * (BLOCKS * E + 1))
            for i in range(TT):
                if i:
                    pe.wait_ge(last_added, i)
                for c in range(2):
                    ins = nc.tensor.matmul(ps[:, 6 + c, :], gpickT[CAP * c:CAP * c + CAP, 1, i, :],
                                           y[CAP * c:CAP * c + CAP, :], start=True, stop=True)
                ins.then_inc(last_scat, 1)

        @block.scalar
        def _(act):
            chain = [0]

            def link(ins):
                chain[0] += 1
                ins.then_inc(act_chain, 1)
                act.wait_ge(act_chain, chain[0])

            act.wait_ge(x_in_s, 32)
            for i in range(TT):
                nc.scalar.activation(xs[:, i, :], X[:, i, :], ACT.Square, accum_out=ssx[:, i:i + 1]).then_inc(x_sumsq, 1)
            act.wait_ge(meta_in_s, 16)
            act.wait_ge(ssx_set, 1)
            nc.scalar.activation(xs[0:N_META, 2, :], metab[0:N_META, :], ACT.Square,
                                 accum_out=ssx[0:N_META, 2:3]).then_inc(x_sumsq, 1)
            act.wait_ge(x_var, 1)
            nc.scalar.activation(rsx, ssx, ACT.Sqrt).then_inc(x_std, 1)
            act.wait_ge(softplus_in, 1)
            nc.scalar.activation(sp[:, 0:8], sp[:, 0:8], ACT.Exp, scale=-1.0).then_inc(sp_exp, 1)
            act.wait_ge(vec_ready, 1)

            def read(job):
                n = JOB[job]
                kind, i = job
                b = n % 4
                act.wait_ge(proj_done, n + 1)
                if kind == "xT":
                    ins = nc.scalar.activation(xnT[:, i, :], ps[:, b, 0:T], ACT.Copy, scale=v("norm_mix_g", i))
                elif kind == "cq":
                    ins = nc.scalar.activation(cq[:, i, :], ps[:, b, 0:SEQ], ACT.Copy)
                elif kind == "ckv":
                    ins = nc.scalar.activation(ckv[:, i, :], ps[:, b, 0:T], ACT.Copy)
                elif kind == "kr":
                    ins = nc.scalar.activation(kh[NOPE:QD, 0, :], ps[NOPE:QD, b, 0:T], ACT.Copy)
                elif kind == "rx":
                    if i == 0:
                        act.wait_ge(xs_read, 1)
                    if i >= 2:
                        act.wait_ge(conv_ready, i - 1)
                    ins = nc.scalar.activation(rxp[:, i % 2, CONV - 1:], ps[:, b, 0:T], ACT.Copy)
                elif kind == "q":
                    ins = nc.scalar.activation(qh[0:QD, i, :], ps[0:QD, b, 0:SEQ], ACT.Copy)
                elif kind == "k":
                    ins = nc.scalar.activation(kh[0:NOPE, i, :], ps[0:NOPE, b, 0:T], ACT.Copy)
                elif kind == "v":
                    m = min(P, T - P * i)
                    ins = nc.scalar.activation(vtok[0:m, i, :], ps[0:m, b, :], ACT.Copy)
                elif kind == "rg":
                    if i >= 2:
                        act.wait_ge(gelu_free, i // 2)
                    ins = nc.scalar.activation(xg[:, i % 2, :], ps[:, b, 0:SEQ], ACT.Copy)
                elif kind == "ra":
                    if i >= 2:
                        act.wait_ge(y_ready_s, i // 2)
                    ins = nc.scalar.activation(tr[:, i % 2, :], ps[:, b, 0:T], ACT.Tanh, bias=hba[:, i:i + 1], scale=0.5)
                elif kind == "ri":
                    ins = nc.scalar.activation(ti[:, i % 2, :], ps[:, b, 0:T], ACT.Tanh, bias=hbx[:, i:i + 1], scale=0.5)
                elif kind == "ga":
                    if i == 0:
                        act.wait_ge(attn_ready, NU)
                    if i >= 4:
                        act.wait_ge(branch_read, i - 3)
                    ins = nc.scalar.activation(ta[:, i % 4, :], ps[:, b, 0:SEQ], ACT.Tanh, bias=hbg[:, i:i + 1], scale=0.5)
                else:
                    act.wait_ge(branch_read, 4 + i + 1)
                    ins = nc.scalar.activation(ta[:, i % 4, :], ps[:, b, 0:SEQ], ACT.Tanh, bias=hbg[:, 8 + i:9 + i], scale=0.5)
                ins.then_inc(proj_read, 1)

            def attention_exp(s):
                if s >= NU:
                    return
                b = UNITS[s][1]
                act.wait_ge(rowmax_ready, s + 1)
                nc.scalar.activation(S[:, s % 2, 0:nk(b)], S[:, s % 2, 0:nk(b)], ACT.Exp, bias=nmx[:, s % 2:s % 2 + 1],
                                     accum_out=sm[:, s % 2:s % 2 + 1]).then_inc(exp_done, 1)

            def gelu(p):
                act.wait_ge(gelu_arg, p + 1)
                nc.scalar.activation(ug, ug, ACT.Tanh, scale=GELU_C).then_inc(gelu_tanh, 1)

            def decay(p):
                if p == 0:
                    act.wait_ge(hc_ready, 1)
                act.wait_ge(proj_read, JOB[("ra", 2 * p + 1)] + 1)
                for k in range(2):
                    i = 2 * p + k
                    nc.scalar.activation(av[:, k, :], tr[:, k, :], ACT.Exp, bias=hc[:, i:i + 1], scale=hc[:, i:i + 1])
                    ins = nc.scalar.activation(th[:, k, :], tr[:, k, :], ACT.Tanh, bias=nhc[:, i:i + 1],
                                               scale=nhc[:, i:i + 1])
                ins.then_inc(lru_tanh, 1)
                act.wait_ge(lru_arg, p + 1)
                nc.scalar.activation(th, th, ACT.Sqrt, scale=0.25).then_inc(lru_sqrt, 1)

            for job in jobs:
                read(job)
                if job == ("rx", 1):
                    act.wait_ge(lora_var, 2)
                    nc.scalar.activation(rq, rq, ACT.Sqrt).then_inc(lora_std, 1)
                    nc.scalar.activation(rk, rk, ACT.Sqrt).then_inc(lora_std, 1)
                if job[0] == "rg" and job[1] % 2 == 1:
                    gelu(job[1] // 2)
                if job in step_after:
                    attention_exp(step_after[job])
                if job[0] == "ri" and job[1] % 2 == 1:
                    decay(job[1] // 2)

            for i in range(TT):
                act.wait_ge(h_ready, i + 1)
                nc.scalar.activation(sqx[:, i, :], X[:, i, :], ACT.Square, accum_out=ss2[:, i:i + 1]).then_inc(h_sumsq, 1)
            act.wait_ge(h_var, 1)
            nc.scalar.activation(rs2, ss2, ACT.Sqrt).then_inc(h_std, 1)

            act.wait_ge(xn2T_done, 1)
            for b in range(4):
                ins = nc.scalar.activation(xn2T[:, 2 * b:2 * b + 2, :],
                                           ps[:, 4 + b, :].rearrange("p (k t) -> p k t", k=2), ACT.Copy)
            ins.then_inc(xn2T_ready, 1)

            for i in range(TT):
                act.wait_ge(mask_ready, i + 1)
                nc.scalar.activation(lg[:, i, :], lg[:, i, :], ACT.Exp, bias=nm1[:, i:i + 1]).then_inc(gexp_done, 1)
            act.wait_ge(gateT_done, 1)
            nc.scalar.activation(gateT[0:E, :], ps[0:E, 4, 0:SEQ], ACT.Copy).then_inc(gateT_ready, 1)

            act.wait_ge(gather_done, 1)
            nc.scalar.activation(xe, ps[:, 2, :], ACT.Copy).then_inc(xe_ready, 1)
            act.wait_ge(gpickT_done, 1)
            nc.scalar.activation(gpickT[:, 0, :, :], ps[:, 5, 0:SEQ].rearrange("p (i t) -> p i t", i=TT),
                                 ACT.Copy).then_inc(gpickT_ready, 1)

            def experts(it):
                for u in range(UNROLL):
                    n = it * UNROLL + u
                    act.wait_ge(glu_ready, n + 1)
                    nc.scalar.activation(sg, hg, ACT.Sigmoid, scale=ALPHA).then_inc(sig_done, 1)
                    act.wait_ge(gather_done, n + 2)
                    act.wait_ge(xeT_done, n + 1)
                    nc.scalar.activation(xe, ps[:, 2, :], ACT.Copy).then_inc(xe_ready, 1)
                    act.wait_ge(gpickT_done, n + 2)
                    nc.scalar.activation(gpickT[:, (u + 1) % 2, :, :], ps[:, 5, 0:SEQ].rearrange("p (i t) -> p i t", i=TT),
                                         ACT.Copy).then_inc(gpickT_ready, 1)
                    act.wait_ge(actT_done, n + 1)
                    nc.scalar.activation(actT, ps[:, 4, :].rearrange("p (j t) -> p j t", j=4), ACT.Copy)\
                      .then_inc(actT_ready, 1)
                    act.wait_ge(weights_used, n * PER_EXPERT + (M0 + PER_EXPERT))
                    nc.scalar.activation(y, ps[:, 5, :], ACT.Copy).then_inc(y_ready, 1)

            with act.Fori(0, GROUPS) as it:
                experts(it)
            act.wait_ge(flag_ready, 1)
            over = act.value_load(flag_i[0:1, 0:1], min_val=0, max_val=1)
            with act.If(over > 0):
                with act.Fori(1, BLOCKS) as j:
                    with act.Fori(0, GROUPS) as i:
                        experts(j * GROUPS + i)

            for i in range(TT):
                act.wait_ge(last_added, i + 1)
                nc.scalar.activation(sqf[:, i, :], X[:, i, :], ACT.Square, accum_out=ssf[:, i:i + 1]).then_inc(f_sumsq, 1)
                act.wait_ge(f_var, i + 1)
                nc.scalar.activation(rsf[:, i:i + 1], ssf[:, i:i + 1], ACT.Sqrt).then_inc(f_std, 1)

        @block.vector
        def _(dve):
            chain = [0]

            def link(ins):
                chain[0] += 1
                ins.then_inc(dve_chain, 1)
                dve.wait_ge(dve_chain, chain[0])

            V = nc.vector
            V.memset(ssx[:, 2:3], 1.0).then_inc(ssx_set, 1)
            dve.wait_ge(vecT_done, 1)
            link(V.tensor_copy(vec[:, :], ps[:, 7, 0:NVEC]))
            lam = vec[:, VEC_AT["rg_lambda"]:VEC_AT["rg_lambda"] + 8]
            link(V.tensor_scalar(sp[:, 8:16], lam, -1.0, None, ALU.mult))
            V.tensor_tensor(sp[:, 0:8], sp[:, 8:16], lam, ALU.max).then_inc(softplus_in, 1)
            V.tensor_scalar(hba, vec[:, VEC_AT["b_rg_a"]:VEC_AT["b_rg_a"] + 8], 0.5, None, ALU.mult)
            V.tensor_scalar(hbx, vec[:, VEC_AT["b_rg_x"]:VEC_AT["b_rg_x"] + 8], 0.5, None, ALU.mult)
            V.tensor_scalar(hbg, vec[:, VEC_AT["b_gate"]:VEC_AT["b_gate"] + 16], 0.5, None, ALU.mult).then_inc(vec_ready, 1)
            dve.wait_ge(x_sumsq, 3)
            V.tensor_scalar(ssx, ssx, 1.0 / D, EPS, ALU.mult, ALU.add).then_inc(x_var, 1)
            dve.wait_ge(x_std, 1)
            link(V.reciprocal(rsx, rsx))
            for i in range(TT):
                V.tensor_scalar(xs[:, i, :], X[:, i, :], rsx[:, i:i + 1], None, ALU.mult).then_inc(xs_ready, 1)
            V.tensor_scalar(xs[0:N_META, 2, :], metab[0:N_META, :], rsx[0:N_META, 2:3], None, ALU.mult).then_inc(xs_ready, 1)

            dve.wait_ge(sp_exp, 1)
            link(V.tensor_scalar(sp[:, 16:24], sp[:, 0:8], 2.0, None, ALU.add))
            link(V.reciprocal(sp[:, 16:24], sp[:, 16:24]))
            link(V.tensor_tensor(sp[:, 16:24], sp[:, 0:8], sp[:, 16:24], ALU.mult))
            link(V.tensor_tensor(sp[:, 0:8], sp[:, 16:24], sp[:, 16:24], ALU.mult))
            link(V.tensor_scalar(sp[:, 24:32], sp[:, 0:8], 1.0 / 17, 1.0 / 15, ALU.mult, ALU.add))
            for d in (13, 11, 9, 7, 5, 3, 1):
                link(V.tensor_tensor(sp[:, 24:32], sp[:, 24:32], sp[:, 0:8], ALU.mult))
                link(V.tensor_scalar(sp[:, 24:32], sp[:, 24:32], 1.0 / d, None, ALU.add))
            link(V.tensor_tensor(sp[:, 24:32], sp[:, 24:32], sp[:, 16:24], ALU.mult))
            link(V.tensor_scalar(sp[:, 8:16], sp[:, 8:16], 0.0, None, ALU.max))
            link(V.scalar_tensor_tensor(out=sp[:, 24:32], in0=sp[:, 24:32], scalar=2.0, in1=sp[:, 8:16],
                                        op0=ALU.mult, op1=ALU.add))
            V.tensor_scalar(hc, sp[:, 24:32], -LRU_C / 2, None, ALU.mult)
            V.tensor_scalar(nhc, sp[:, 24:32], LRU_C / 2, None, ALU.mult).then_inc(hc_ready, 1)

            dve.wait_ge(proj_done, KT)
            V.memset(rxp[:, :, 0:CONV - 1], 0.0).then_inc(xs_read, 1)
            dve.wait_ge(proj_read, JOB[("cq", QT - 1)] + 1)
            V.tensor_tensor(sqq, cq, cq, ALU.mult).then_inc(lora_sq, 1)
            dve.wait_ge(proj_read, JOB[("ckv", KVT - 1)] + 1)
            V.tensor_tensor(sqk, ckv, ckv, ALU.mult).then_inc(lora_sq, 1)

            def conv(i):
                k = i % 2
                dve.wait_ge(proj_read, JOB[("rx", i)] + 1)
                if k == 0 and i >= 2:
                    dve.wait_ge(proj_done, JOB[("ri", i - 1)] + 1)
                link(V.tensor_scalar(xc[:, k, :], rxp[:, k, 3:3 + T], v("conv_w", 8 * 3 + i), v("conv_b", i),
                                     ALU.mult, ALU.add))
                for w in (2, 1, 0):
                    ins = V.scalar_tensor_tensor(out=xc[:, k, :], in0=rxp[:, k, w:w + T], scalar=v("conv_w", 8 * w + i),
                                                 in1=xc[:, k, :], op0=ALU.mult, op1=ALU.add)
                    if w:
                        link(ins)
                ins.then_inc(conv_ready, 1)

            dve.wait_ge(xs_read, 1)
            dve.wait_ge(lora_sum, 2)
            V.tensor_scalar(rq, ps[:, 4, 0:SEQ], 1.0 / Q_LORA, EPS, ALU.mult, ALU.add).then_inc(lora_var, 1)
            V.tensor_scalar(rk, ps[:, 5, 0:T], 1.0 / KV_LORA, EPS, ALU.mult, ALU.add).then_inc(lora_var, 1)
            dve.wait_ge(lora_std, 2)
            link(V.reciprocal(rq, rq))
            for k in range(QT):
                ins = V.scalar_tensor_tensor(out=cq[:, k, :], in0=cq[:, k, :], scalar=v("q_norm_g", k), in1=rq,
                                             op0=ALU.mult, op1=ALU.mult)
            ins.then_inc(lora_ready, 1)
            link(V.reciprocal(rk, rk))
            for k in range(KVT):
                ins = V.scalar_tensor_tensor(out=ckv[:, k, :], in0=ckv[:, k, :], scalar=v("kv_norm_g", k), in1=rk,
                                             op0=ALU.mult, op1=ALU.mult)
            ins.then_inc(lora_ready, 1)
            conv(0)
            conv(1)

            dve.wait_ge(krot_done, 1)
            ku = ropeu[NOPE:QD, :, :].rearrange("p k t -> p (k t)")[:, 0:T]
            V.tensor_tensor(ku, ps[NOPE:QD, 6, 0:T], sinT, ALU.mult)
            link(V.tensor_tensor(kh[NOPE:QD, 0, :], kh[NOPE:QD, 0, :], cosT, ALU.mult))
            link(V.tensor_tensor(kh[NOPE:QD, 0, :], kh[NOPE:QD, 0, :], ku, ALU.add))
            V.tensor_copy(kh[NOPE:QD, 1:HEADS, :], kh[NOPE:QD, 0:1, :].broadcast_to([ROPE, HEADS - 1, T]))\
             .then_inc(rope_ready, 1)
            cos2 = ca[NOPE:QD, CA["cos"][0] + N_META:CA["cos"][1]].rearrange("p (a t) -> p a t", a=1).broadcast_to([ROPE, 2, SEQ])
            sin2 = ca[NOPE:QD, CA["sin"][0] + N_META:CA["sin"][1]].rearrange("p (a t) -> p a t", a=1).broadcast_to([ROPE, 2, SEQ])
            for g in range(4):
                dve.wait_ge(qrot_done, g + 1)
                q2 = qh[NOPE:QD, 2 * g:2 * g + 2, :]
                V.tensor_tensor(ropeu[NOPE:QD, :, :], ps[NOPE:QD, 4 + g, :].rearrange("p (h t) -> p h t", h=2), sin2, ALU.mult)
                link(V.tensor_tensor(q2, q2, cos2, ALU.mult))
                ins = V.tensor_tensor(q2, q2, ropeu[NOPE:QD, :, :], ALU.add)
                if g < 3:
                    ins.then_inc(rope_ready, 1)
                    dve.wait_ge(rope_ready, g + 2)
                else:
                    ins.then_inc(rope_ready, 1)

            def gelu_arg_of(p):
                dve.wait_ge(proj_read, JOB[("rg", 2 * p + 1)] + 1)
                link(V.tensor_tensor(ug, xg, xg, ALU.mult))
                link(V.tensor_scalar(ug, ug, 0.044715, 1.0, ALU.mult, ALU.add))
                V.tensor_tensor(ug, ug, xg, ALU.mult).then_inc(gelu_arg, 1)

            def gelu_end(p):
                dve.wait_ge(gelu_tanh, p + 1)
                V.scalar_tensor_tensor(out=gel[:, 2 * p:2 * p + 2, :], in0=ug, scalar=1.0, in1=xg,
                                       op0=ALU.add, op1=ALU.mult).then_inc(gelu_free, 1)

            def recur_arg(p):
                dve.wait_ge(proj_read, JOB[("ri", 2 * p + 1)] + 1)
                V.scalar_tensor_tensor(out=ti, in0=ti, scalar=1.0, in1=xc, op0=ALU.add, op1=ALU.mult)
                dve.wait_ge(lru_tanh, p + 1)
                link(V.tensor_tensor(tr, av, av, ALU.mult))
                V.scalar_tensor_tensor(out=th, in0=tr, scalar=1.0, in1=th, op0=ALU.add, op1=ALU.mult).then_inc(lru_arg, 1)

            def recur(p):
                dve.wait_ge(lru_sqrt, p + 1)
                dve.wait_ge(gelu_free, p + 1)
                link(V.tensor_tensor(ti, ti, th, ALU.mult))
                V.tensor_tensor_scan(tr[:, 0, :], av[:, 0, :], ti[:, 0, :], 0.0, ALU.mult, ALU.add)
                link(V.tensor_tensor_scan(tr[:, 1, :], av[:, 1, :], ti[:, 1, :], 0.0, ALU.mult, ALU.add))
                g2 = gel[:, 2 * p:2 * p + 2, :]
                V.scalar_tensor_tensor(out=g2, in0=g2, scalar=0.5, in1=tr[:, :, N_META:T], op0=ALU.mult, op1=ALU.mult)\
                 .then_inc(y_ready_s, 1)

            def softmax_in(s):
                b = UNITS[s][1]
                k = s % 2
                w = nk(b)
                dve.wait_ge(scores_done, s + 1)
                if s >= 2:
                    dve.wait_ge(probsT_done, s - 1)
                ins = V.scalar_tensor_tensor(out=S[:, k, 0:w], in0=ps[:, 4 + k, 0:w], scalar=SCALE,
                                             in1=maskc[:, T - w:T], op0=ALU.mult, op1=ALU.add)
                ins.then_inc(scores_read, 1)
                dve.wait_ge(scores_read, s + 1)
                link(V.tensor_reduce(mx[:, k:k + 1], S[:, k, 0:w], AX_X, ALU.max))
                V.tensor_scalar(nmx[:, k:k + 1], mx[:, k:k + 1], -1.0, None, ALU.mult).then_inc(rowmax_ready, 1)

            def softmax_out(s):
                b = UNITS[s][1]
                k = s % 2
                dve.wait_ge(exp_done, s + 1)
                link(V.reciprocal(rsm[:, k:k + 1], sm[:, k:k + 1]))
                V.tensor_scalar(S[:, k, 0:nk(b)], S[:, k, 0:nk(b)], rsm[:, k:k + 1], None, ALU.mult).then_inc(probs_ready, 1)

            def attention_step(s):
                if s < NU:
                    softmax_in(s)
                if 1 <= s <= NU:
                    r = s - 1
                    kts = ktiles(UNITS[r][1])
                    dve.wait_ge(probsT_done, r + 1)
                    if r >= 2:
                        dve.wait_ge(attn_done, r - 1)
                    full = [t for t, m in kts if m == P]
                    V.tensor_copy(PT[:, r % 2, 0:len(full), :],
                                  ps[:, 6, 0:P * len(full)].rearrange("p (k q) -> p k q", k=len(full)))
                    t, m = kts[-1]
                    V.tensor_copy(PT[0:m, r % 2, t, :], ps[0:m, 6, P * t:P * t + P]).then_inc(probsT_ready, 1)
                if s >= 2:
                    r = s - 2
                    h, b = UNITS[r]
                    o = VD * (h % 2)
                    dve.wait_ge(attn_done, r + 1)
                    V.tensor_copy(oT[o:o + VD, h // 2, P * b:P * b + P], ps[o:o + VD, 7, 0:P]).then_inc(attn_ready, 1)
                if s < NU:
                    softmax_out(s)

            for job in jobs[JOB[("rg", 0)]:]:
                kind, i = job
                if kind == "rx":
                    conv(i)
                if kind == "rg" and i % 2 == 1:
                    gelu_arg_of(i // 2)
                if job in step_after:
                    attention_step(step_after[job])
                if kind == "rg" and i % 2 == 1:
                    gelu_end(i // 2)
                if kind == "ri" and i % 2 == 1:
                    recur_arg(i // 2)
                    recur(i // 2)

            d = 0
            for g in range(2):
                for i in range(4 * g, 4 * g + 4):
                    dve.wait_ge(proj_read, JOB[("ga", i)] + 1)
                    dve.wait_ge(branch_done, d + 1)
                    V.scalar_tensor_tensor(out=mT[:, i, :], in0=ta[:, i % 4, :], scalar=1.0, in1=ps[:, 4 + d % 4, 0:SEQ],
                                           op0=ALU.add, op1=ALU.mult).then_inc(branch_read, 1)
                    d += 1
            for i in range(KT):
                dve.wait_ge(proj_read, JOB[("gr", i)] + 1)
                dve.wait_ge(branch_done, d + 1)
                link(V.scalar_tensor_tensor(out=ta[:, i % 4, :], in0=ta[:, i % 4, :], scalar=1.0,
                                            in1=ps[:, 4 + d % 4, 0:SEQ], op0=ALU.add, op1=ALU.mult))
                V.tensor_tensor(mT[:, i, :], mT[:, i, :], ta[:, i % 4, :], ALU.add).then_inc(branch_read, 1)
                d += 1

            dve.wait_ge(weights_used, M0)
            for i in range(TT):
                V.scalar_tensor_tensor(out=X[:, i, :].rearrange("p (c n) -> p c n", c=2), in0=ps[:, 2 * i:2 * i + 2, :],
                                       scalar=0.5, in1=X[:, i, :].rearrange("p (c n) -> p c n", c=2),
                                       op0=ALU.mult, op1=ALU.add).then_inc(h_ready, 1)
            dve.wait_ge(h_sumsq, 2)
            V.tensor_scalar(ss2, ss2, 1.0 / D, EPS, ALU.mult, ALU.add).then_inc(h_var, 1)
            dve.wait_ge(h_std, 1)
            link(V.reciprocal(rs2, rs2))
            dve.wait_ge(moe_in, 16 * 7)
            for i in range(TT):
                V.scalar_tensor_tensor(out=xn2[:, i, :], in0=X[:, i, :], scalar=rs2[:, i:i + 1], in1=gffn,
                                       op0=ALU.mult, op1=ALU.mult).then_inc(xn2_ready, 1)

            dve.wait_ge(logits_done, 1)
            link(V.tensor_copy(lg, ps[:, 0:2, 0:E]))
            for i in range(TT):
                t8 = top8[:, 8 * i:8 * i + 8]
                link(V.max(t8, lg[:, i, :]))
                V.tensor_scalar(nm1[:, i:i + 1], t8[:, 0:1], -1.0, None, ALU.mult)
                k4 = t8[:, TOP_K - 1:TOP_K]
                link(V.tensor_scalar(tmp[:, 0, :], lg[:, i, :], k4, None, ALU.is_gt))
                link(V.tensor_scalar(tmp[:, 1, :], lg[:, i, :], k4, None, ALU.is_equal))
                link(V.tensor_reduce(ngt[:, i:i + 1], tmp[:, 0, :], AX_X, ALU.add))
                link(V.tensor_tensor_scan(tmp[:, 2, :], ones[:, 0:E], tmp[:, 1, :], 0.0, ALU.mult, ALU.add))
                link(V.tensor_scalar(tmp[:, 2, :], tmp[:, 2, :], ngt[:, i:i + 1], TOP_K + 0.5, ALU.add, ALU.is_lt))
                link(V.tensor_tensor(tmp[:, 1, :], tmp[:, 1, :], tmp[:, 2, :], ALU.mult))
                ins = V.tensor_tensor(selm[:, i, :], tmp[:, 0, :], tmp[:, 1, :], ALU.add)
                ins.then_inc(mask_ready, 1)
            dve.wait_ge(mask_ready, TT)
            V.memset(gpickT[:, 1, :, :], 0.0)
            V.memset(y, 0.0).then_inc(y_ready, 1)
            dve.wait_ge(gexp_done, TT)
            for i in range(TT):
                link(V.tensor_tensor(lg[:, i, :], lg[:, i, :], selm[:, i, :], ALU.mult))
                link(V.tensor_reduce(esum[:, i:i + 1], lg[:, i, :], AX_X, ALU.add))
                link(V.reciprocal(esum[:, i:i + 1], esum[:, i:i + 1]))
                link(V.tensor_scalar(gate[:, i, 0:E], lg[:, i, :], esum[:, i:i + 1], None, ALU.mult))
                for j in range(1, BLOCKS):
                    V.tensor_copy(gate[:, i, E * j:E * j + E], gate[:, i, 0:E])
                ins = V.tensor_copy(gate[:, i, E * BLOCKS:NCOL], gate[:, i, 0:NCOL - E * BLOCKS])
            ins.then_inc(gate_ready, 1)
            dve.wait_ge(pos_done, 1)
            for i in range(TT):
                link(V.scalar_tensor_tensor(out=tmp[:, 3 + i, :], in0=ps[:, 2, E * i:E * i + E], scalar=1.0,
                                            in1=selm[:, i, :], op0=ALU.add, op1=ALU.mult))
                for j in range(BLOCKS + 1):
                    w = E if j < BLOCKS else NCOL - E * BLOCKS
                    ins = V.scalar_tensor_tensor(out=posm[:, i, E * j:E * j + w], in0=tmp[:, 3 + i, 0:w], scalar=-1.0,
                                                 in1=block_base[:, E * j:E * j + w], op0=ALU.add, op1=ALU.subtract)
            link(ins)
            link(V.tensor_reduce(cmax[:, 0:1], ps[:, 3, 0:E], AX_X, ALU.max))
            link(V.tensor_scalar(cmax[:, 1:2], cmax[:, 0:1], CAP + 0.5, None, ALU.is_gt))
            V.tensor_copy(flag_i[0:1, 0:1], cmax[0:1, 1:2]).then_inc(flag_ready, 1)

            def route(n, par):
                for i in range(TT):
                    V.tensor_scalar(pick[:, i, :], slot_id[:, 0:CAP], posm[:, i, bass.ds(n, 1)], None, ALU.is_equal)
                    V.tensor_scalar(gpick[:, i, :], slot_id, posm[:, i, bass.ds(n, 1)], gate[:, i, bass.ds(n, 1)],
                                    ALU.is_equal, ALU.mult)
                V.tensor_scalar(sel[0:E, par, :], ones[0:E, 0:CAP], pick_e[0:E, bass.ds(n, 1)], None, ALU.mult)\
                 .then_inc(route_ready, 1)

            dve.wait_ge(gate_ready, 1)
            route(0, 0)
            for i in range(TT):
                dve.wait_ge(bdn_done, 2 * i + 2)
                V.tensor_tensor(X[:, i, :].rearrange("p (c n) -> p c n", c=2), ps[:, 6:8, :],
                                X[:, i, :].rearrange("p (c n) -> p c n", c=2), ALU.add).then_inc(scat_added, 1)
            dve.sem_inc(hidden_read, 1)
            dve.wait_ge(xeT_done, 1)
            V.tensor_copy(xeT, ps[:, 3, :].rearrange("p (j t) -> p j t", j=4)).then_inc(xeT_ready, 1)

            def experts(it):
                for u in range(UNROLL):
                    n = it * UNROLL + u
                    dve.wait_ge(gpickT_done, n + 1)
                    route(n + 1, (u + 1) % 2)
                    for i in range(TT):
                        dve.wait_ge(scat_done, n * TT + (i + 1))
                        xi = X[:, i, :].rearrange("p (c n) -> p c n", c=2)
                        V.tensor_tensor(xi, ps[:, 6:8, :], xi, ALU.add).then_inc(scat_added, 1)
                    dve.wait_ge(weights_used, n * PER_EXPERT + (M0 + KT))
                    V.tensor_scalar(hg, ps[:, 0, :], LIMIT, None, ALU.min).then_inc(glu_ready, 1)
                    V.tensor_scalar(hl, ps[:, 1, :], LIMIT, -LIMIT, ALU.min, ALU.max).then_inc(hidden_read, 1)
                    dve.wait_ge(hidden_read, n + 2)
                    V.scalar_tensor_tensor(out=hl, in0=hl, scalar=1.0, in1=hg, op0=ALU.add, op1=ALU.mult)\
                     .then_inc(lin_ready, 1)
                    dve.wait_ge(lin_ready, n + 1)
                    dve.wait_ge(sig_done, n + 1)
                    V.tensor_tensor(act_h, hl, sg, ALU.mult).then_inc(act_ready, 1)
                    dve.wait_ge(xeT_done, n + 2)
                    V.tensor_copy(xeT, ps[:, 3, :].rearrange("p (j t) -> p j t", j=4)).then_inc(xeT_ready, 1)

            with dve.Fori(0, GROUPS) as it:
                experts(it)
            dve.wait_ge(flag_ready, 1)
            over = dve.value_load(flag_i[0:1, 0:1], min_val=0, max_val=1)
            with dve.If(over > 0):
                with dve.Fori(1, BLOCKS) as j:
                    with dve.Fori(0, GROUPS) as i:
                        experts(j * GROUPS + i)
            for i in range(TT):
                dve.wait_ge(last_scat, i + 1)
                xi = X[:, i, :].rearrange("p (c n) -> p c n", c=2)
                V.tensor_tensor(xi, ps[:, 6:8, :], xi, ALU.add).then_inc(last_added, 1)
            for i in range(TT):
                dve.wait_ge(f_sumsq, i + 1)
                V.tensor_scalar(ssf[:, i:i + 1], ssf[:, i:i + 1], 1.0 / D, EPS, ALU.mult, ALU.add).then_inc(f_var, 1)
                dve.wait_ge(f_std, i + 1)
                link(V.reciprocal(rsf[:, i:i + 1], rsf[:, i:i + 1]))
                V.scalar_tensor_tensor(out=X[:, i, :], in0=X[:, i, :], scalar=rsf[:, i:i + 1], in1=gfin,
                                       op0=ALU.mult, op1=ALU.mult).then_inc(fin_ready, 1)


_INS = ["x", "meta_tokens", "vec", "ca", "cb", "w_in", "w_uq", "w_ukv", "w_ao", "w_rg_a", "w_rg_x", "w_ro", "w_out",
        "norm_ffn_g", "w_router", "b_router", "w_up", "b_up", "w_down", "b_down", "norm_final_g"]


def kernel(**inputs):
    import concourse.bacc as _bacc
    from concourse.bass_utils import run_bass_kernel_spmd as _run

    arrays = {k: np.ascontiguousarray(np.asarray(a)) for k, a in inputs.items()}
    arrays["vec"] = np.concatenate([arrays[name].reshape(rows, P) for name, rows in VEC_ROWS], axis=0)
    arrays["ca"], arrays["cb"] = constants()
    nc = _bacc.Bacc("TRN2", target_bir_lowering=False, num_devices=1)
    feed, args = {}, []
    for name in _INS:
        a = arrays[name]
        feed[f"in_{name}_dram"] = a
        args.append(nc.dram_tensor(f"in_{name}_dram", a.shape, mybir.dt.from_np(a.dtype), kind="ExternalInput").ap())
    args.append(nc.dram_tensor("out_0_dram", (1, SEQ, D), F32, kind="ExternalOutput").ap())
    layer(nc, *args)
    r = _run(nc, [feed], core_ids=[0])
    return r.results[0]["out_0_dram"]
```

```python
import math
from contextlib import ExitStack

import numpy as np

import concourse.bass as bass
from concourse import mybir

F32 = mybir.dt.float32
I32 = mybir.dt.int32
ALU = mybir.AluOpType
ACT = mybir.ActivationFunctionType
AX_X = mybir.AxisListType.X

P = 128
D = 1024
N_META = 16
SEQ = 256
T = SEQ + N_META
EPS = 1e-6
HEADS = 8
Q_LORA, KV_LORA = 384, 256
NOPE, ROPE, VD = 64, 32, 64
QD = NOPE + ROPE
ROPE_BASE = 10000.0
CONV = 4
LRU_C = 8.0
E = 32
TOP_K = 4
F = 1024
ALPHA, LIMIT = 1.702, 7.0
OFF_CQ = 0
OFF_CKV = OFF_CQ + Q_LORA
OFF_KR = OFF_CKV + KV_LORA
OFF_RX = OFF_KR + ROPE
OFF_RG = OFF_RX + D
OFF_GATE = OFF_RG + D
KT = D // P
QT = Q_LORA // P
KVT = KV_LORA // P
TT = SEQ // P
SCALE = (NOPE + ROPE) ** -0.5
GELU_C = math.sqrt(2.0 / math.pi)
MASKED = -3.0e38

SLOTS = 16
SLOT = 2048
CAP = 64
BLOCKS = SEQ // CAP
UNROLL = 4
GROUPS = E // UNROLL
PER_EXPERT = 12
NCOL = E * BLOCKS + UNROLL

VEC_ROWS = [("norm_mix_g", 8), ("q_norm_g", 3), ("kv_norm_g", 2), ("b_gate", 16), ("conv_w", 32),
            ("conv_b", 8), ("b_rg_a", 8), ("b_rg_x", 8), ("rg_lambda", 8)]
VEC_AT = {}
_n = 0
for _name, _rows in VEC_ROWS:
    VEC_AT[_name] = _n
    _n += _rows
NVEC = _n

CA = {}
_n = 0
for _name, _w in (("ident", 128), ("ones", 128), ("mask", 272), ("rot", 32), ("cos", T), ("sin", T)):
    CA[_name] = (_n, _n + _w)
    _n += _w
NCA = _n
CB = {}
_n = 0
for _name, _w in (("upper", 128), ("slot_id", 128), ("pick", NCOL), ("block_base", NCOL)):
    CB[_name] = (_n, _n + _w)
    _n += _w
NCB = _n


def constants():
    a = np.zeros((P, NCA), np.float32)
    a[:, slice(*CA["ident"])] = np.eye(P, dtype=np.float32)
    a[:, slice(*CA["ones"])] = 1.0
    q, k = np.arange(P)[:, None], np.arange(P)[None, :]
    a[:, CA["mask"][0] + 144:CA["mask"][1]] = np.where(k <= q, 0.0, MASKED)
    half = ROPE // 2
    rot = np.zeros((ROPE, ROPE), np.float32)
    for r in range(half):
        rot[r + half, r] = -1.0
        rot[r, r + half] = 1.0
    a[NOPE:QD, slice(*CA["rot"])] = rot
    inv = (np.float32(ROPE_BASE) ** (-np.arange(0, ROPE, 2, dtype=np.float32) / np.float32(ROPE))).astype(np.float32)
    ang = np.arange(T, dtype=np.float32)[:, None] * inv[None, :]
    a[NOPE:QD, slice(*CA["cos"])] = np.tile(np.cos(ang).astype(np.float32).T, (2, 1))
    a[NOPE:QD, slice(*CA["sin"])] = np.tile(np.sin(ang).astype(np.float32).T, (2, 1))
    b = np.zeros((P, NCB), np.float32)
    b[:, slice(*CB["upper"])] = np.triu(np.ones((P, P), np.float32), 1)
    b[:, slice(*CB["slot_id"])] = np.arange(P) % CAP
    n = np.arange(NCOL)
    b[:E, slice(*CB["pick"])] = (n[None, :] % E == np.arange(E)[:, None])
    b[:, slice(*CB["block_base"])] = CAP * (n // E)
    return a, b


def mixer_loads():
    loads = [("in", 0, 256), ("in", 256, 256), ("in", 512, 160), ("in", OFF_RX, 256), ("in", OFF_RG, 256),
             ("uq", 0, 384), ("uq", 384, 384), ("ukv", 0, 1024), ("gates", 0, 2)]
    for p in range(1, 4):
        loads += [("in", OFF_RX + 256 * p, 256), ("in", OFF_RG + 256 * p, 256), ("gates", 2 * p, 2)]
    for p in range(4):
        loads += [("in", OFF_GATE + D + 256 * p, 256), ("ro", 256 * p, 256)]
    for h in range(2):
        loads += [("in", OFF_GATE + 512 * h, 256), ("in", OFF_GATE + 512 * h + 256, 256), ("ao", 512 * h, 512)]
    loads += [("out", 2 * r, 2) for r in range(4)]
    return loads


LOADS = mixer_loads()
M0 = len(LOADS)


def layer(nc, x_in, meta_in, vec_in, ca_in, cb_in, w_in, w_uq, w_ukv, w_ao, w_rg_a, w_rg_x, w_ro, w_out,
          norm_ffn_g, w_router, b_router, w_up, b_up, w_down, b_down, norm_final_g, out):
    with ExitStack() as ctx:
        def sb(name, shape, dt=F32):
            return ctx.enter_context(nc.sbuf_tensor(name, shape, dt))

        def sem(name):
            return ctx.enter_context(nc.semaphore(name))

        ring = sb("ring", [P, SLOTS, SLOT])
        X = sb("X", [P, TT, D])
        ca = sb("ca", [P, NCA])
        vec = sb("vec", [P, NVEC])
        small = sb("small", [P, 160])
        WORK = 16800
        work = sb("work", [P, WORK])
        ps = ctx.enter_context(nc.psum_tensor("ps", [P, 8, 512], F32))

        at = [0]

        def view(n, start=None):
            a = at[0] if start is None else start
            if start is None:
                at[0] += n
            assert a + n <= WORK, (a, n)
            return work[:, a:a + n]

        xnT = view(KT * T).rearrange("p (k t) -> p k t", k=KT)
        qh = view(HEADS * SEQ).rearrange("p (h t) -> p h t", h=HEADS)
        kh = view(HEADS * T).rearrange("p (h t) -> p h t", h=HEADS)
        vtok = view(3 * 512).rearrange("p (k n) -> p k n", k=3)
        cq_at = at[0]
        cq = view(QT * SEQ).rearrange("p (k t) -> p k t", k=QT)
        ckv_at = at[0]
        ckv = view(KVT * T).rearrange("p (k t) -> p k t", k=KVT)
        oT = view(4 * SEQ).rearrange("p (k t) -> p k t", k=4)
        rg_at = at[0]
        rxp = view(2 * (T + 3)).rearrange("p (k t) -> p k t", k=2)
        xc = view(2 * T).rearrange("p (k t) -> p k t", k=2)
        tr = view(2 * T).rearrange("p (k t) -> p k t", k=2)
        ti = view(2 * T).rearrange("p (k t) -> p k t", k=2)
        av = view(2 * T).rearrange("p (k t) -> p k t", k=2)
        th = view(2 * T).rearrange("p (k t) -> p k t", k=2)
        xg = view(2 * SEQ).rearrange("p (k t) -> p k t", k=2)
        ug = view(2 * SEQ).rearrange("p (k t) -> p k t", k=2)
        gel_at = at[0]
        gel = view(KT * SEQ).rearrange("p (k t) -> p k t", k=KT)
        PT = view(2 * 384, cq_at).rearrange("p (b k q) -> p b k q", b=2, k=3)
        S = view(2 * T, ckv_at).rearrange("p (b t) -> p b t", b=2)
        xs = view(3 * D, rg_at).rearrange("p (k d) -> p k d", k=3)
        metab = view(D, rg_at + 3 * D)
        sqq = view(QT * SEQ, rg_at + 4 * D - 768).rearrange("p (k t) -> p k t", k=QT)
        sqk = view(KVT * T, cq_at + 1312).rearrange("p (k t) -> p k t", k=KVT)
        rq = view(SEQ, rg_at + 1100)
        rk = view(T, rg_at + 1100 + SEQ)
        ropeu = view(2 * SEQ, gel_at + 6 * SEQ).rearrange("p (k t) -> p k t", k=2)
        q_at = KT * T
        vec_rows = view(P, q_at)[0:NVEC, :]
        mT = view(KT * SEQ, rg_at).rearrange("p (k t) -> p k t", k=KT)
        ta = view(4 * SEQ, rg_at + 2 * (T + 3) + 10 * T).rearrange("p (k t) -> p k t", k=4)

        at[0] = 0
        xn2 = view(TT * D).rearrange("p (i d) -> p i d", i=TT)
        gfin = view(D)
        posm = view(TT * NCOL).rearrange("p (i n) -> p i n", i=TT)
        gate = view(TT * NCOL).rearrange("p (i n) -> p i n", i=TT)
        lg = view(TT * E).rearrange("p (i e) -> p i e", i=TT)
        selm = view(TT * E).rearrange("p (i e) -> p i e", i=TT)
        tmp = view(6 * E).rearrange("p (k e) -> p k e", k=6)
        assert at[0] <= q_at + HEADS * SEQ
        at[0] = q_at + HEADS * SEQ
        gffn = view(D)
        wr = view(KT * E).rearrange("p (k e) -> p k e", k=KT)
        brt = view(E)
        cb = view(NCB)
        bup = view(2 * F)
        assert at[0] <= ckv_at + KVT * T
        at[0] = ckv_at + KVT * T
        sel = view(2 * CAP).rearrange("p (b t) -> p b t", b=2)
        pick = view(TT * CAP).rearrange("p (i t) -> p i t", i=TT)
        gpick = view(TT * P).rearrange("p (i t) -> p i t", i=TT)
        gpickT = view(2 * TT * P).rearrange("p (b i t) -> p b i t", b=2, i=TT)
        xe = view(512)
        xeT = view(512).rearrange("p (j t) -> p j t", j=4)
        hg = view(512)
        hl = view(512)
        sg = view(512)
        act_h = view(512)
        actT = view(512).rearrange("p (j t) -> p j t", j=4)
        y = view(512)
        assert at[0] <= gel_at
        xn2T_at = gel_at
        xn2T = view(KT * SEQ, xn2T_at).rearrange("p (i k t) -> p i k t", i=TT, k=KT)
        sqx = view(TT * D, xn2T_at).rearrange("p (i d) -> p i d", i=TT)
        sqf = sqx
        flag_i = sb("flag_i", [1, 1], I32)

        ident = ca[:, slice(*CA["ident"])]
        ones = ca[:, slice(*CA["ones"])]
        maskc = ca[:, slice(*CA["mask"])]
        rotm = ca[NOPE:QD, slice(*CA["rot"])]
        cosT = ca[NOPE:QD, slice(*CA["cos"])]
        sinT = ca[NOPE:QD, slice(*CA["sin"])]
        upper = cb[:, slice(*CB["upper"])]
        slot_id = cb[:, slice(*CB["slot_id"])]
        pick_e = cb[:, slice(*CB["pick"])]
        block_base = cb[:, slice(*CB["block_base"])]

        def v(name, i):
            c = VEC_AT[name] + i
            return vec[:, c:c + 1]

        sm_n = [0]

        def col(n):
            a = sm_n[0]
            sm_n[0] += n
            assert sm_n[0] <= 160
            return small[:, a:a + n]

        hc2 = col(8)
        hc = col(8)
        nhc = col(8)
        hba = col(8)
        hbx = col(8)
        hbg = col(16)
        sp = col(32)
        dummy = col(1)
        ssx = col(3)
        rsx = col(3)
        mx = col(2)
        nmx = col(2)
        sm = col(2)
        rsm = col(2)
        ss2 = col(2)
        rs2 = col(2)
        top8 = col(16)
        nm1 = col(2)
        ngt = col(2)
        esum = col(2)
        cmax = col(2)
        ssf = col(2)
        rsf = col(2)

        const_in, vec_in_s, x_in0, x_in1, meta_in_s, moe_in = (sem(n) for n in
                                                         ("const_in", "vec_in_s", "x_in0", "x_in1", "meta_in_s", "moe_in"))
        slot_loaded = [sem(f"slot_loaded{s}") for s in range(SLOTS)]
        weights_used = sem("weights_used")
        dve_chain, act_chain = sem("dve_chain"), sem("act_chain")
        vecT_done, vec_ready, softplus_in, sp_exp = sem("vecT_done"), sem("vec_ready"), sem("softplus_in"), sem("sp_exp")
        x_sumsq, x_var, x_std, x0_sumsq, x0_var, x0_std, x0s_ready, x1s_ready, ms_ready, ident_in = (sem(n) for n in
            ("x_sumsq", "x_var", "x_std", "x0_sumsq", "x0_var", "x0_std", "x0s_ready", "x1s_ready", "ms_ready", "ident_in"))
        vec_read, ms_rs, xT_done, xT_read, xT_read_dve = sem("vec_read"), sem("ms_rs"), sem("xT_done"), sem("xT_read"), sem("xT_read_dve")
        proj_done, proj_read = sem("proj_done"), sem("proj_read")
        lora_sq, lora_sum, lora_var, lora_std, lora_ready = (sem(n) for n in
                                                             ("lora_sq", "lora_sum", "lora_var", "lora_std", "lora_ready"))
        krot_done, qrot_done, rope_ready, rope_read = (sem(n) for n in
                                                       ("krot_done", "qrot_done", "rope_ready", "rope_read"))
        scores_done, rowmax_ready, exp_done, probs_ready = (sem(n) for n in
                                                            ("scores_done", "rowmax_ready", "exp_done", "probs_ready"))
        scores_read, probsT_done, probsT_ready, attn_done, attn_ready = (sem(n) for n in
            ("scores_read", "probsT_done", "probsT_ready", "attn_done", "attn_ready"))
        conv_ready, gelu_arg, gelu_tanh, lru_arg, lru_sqrt, gelu_free, y_ready_s, gates_used = (sem(n) for n in
            ("conv_ready", "gelu_arg", "gelu_tanh", "lru_arg", "lru_sqrt", "gelu_free", "y_ready_s", "gates_used"))
        branch_done, branch_read, h_ready = (sem(n) for n in
                                                       ("branch_done", "branch_read", "h_ready"))
        h_sumsq, h_var, h_std, xn2_ready, xn2T_done, xn2T_ready = (sem(n) for n in
            ("h_sumsq", "h_var", "h_std", "xn2_ready", "xn2T_done", "xn2T_ready"))
        logits_done, gexp_done, mask_ready, pos_done, gate_ready, gateT_done, pick_ready, pos_done_read = (
            sem(n) for n in ("logits_done", "gexp_done", "mask_ready", "pos_done", "gate_ready",
                             "gateT_done", "pick_ready", "pos_done_read"))
        flag_ready = sem("flag_ready")
        route_ready, gather_done, xe_ready, xeT_done, xeT_ready = (sem(n) for n in
            ("route_ready", "gather_done", "xe_ready", "xeT_done", "xeT_ready"))
        gpickT_done, gpickT_ready, hidden_read, glu_ready, sig_done, act_ready = (sem(n) for n in
            ("gpickT_done", "gpickT_ready", "hidden_read", "glu_ready", "sig_done", "act_ready"))
        actT_done, actT_ready, y_ready, scat_done, scat_added = (sem(n) for n in
            ("actT_done", "actT_ready", "y_ready", "scat_done", "scat_added"))
        f_sumsq, f_var, f_std, fin_ready, out_stored = (sem(n) for n in
                                                        ("f_sumsq", "f_var", "f_std", "fin_ready", "out_stored"))

        xn2T_ready2, y_zeroed, bdn_in, gfin_in, out_done, lru_tanh, last_added, last_scat, xs_read, ssx_set, hc_ready, lin_ready = (sem(n) for n in
            ("xn2T_ready2", "y_zeroed", "bdn_in", "gfin_in", "out_done", "lru_tanh", "last_added", "last_scat", "xs_read", "ssx_set", "hc_ready", "lin_ready"))

        block = ctx.enter_context(nc.Block())

        jobs = []
        jobs += [("cq", i) for i in range(QT)] + [("ckv", i) for i in range(KVT)] + [("kr", 0)]
        jobs += [("rx", 0), ("rx", 1), ("rg", 0), ("rg", 1)]
        jobs += [("q", h) for h in range(HEADS)] + [("k", h) for h in range(HEADS)] + [("v", i) for i in range(3)]
        jobs += [("ra", 0), ("ra", 1), ("ri", 0), ("ri", 1)]
        for p in range(1, 4):
            for kinds in (("rx", "rg"), ("ra", "ri")):
                jobs += [(kind, i) for kind in kinds for i in (2 * p, 2 * p + 1)]
        jobs += [("gr", i) for i in range(8)] + [("ga", i) for i in range(8)]
        JOB = {job: n for n, job in enumerate(jobs)}

        UNITS = [(h, b) for h in range(HEADS) for b in range(TT)]
        NU = len(UNITS)
        step_after = {}
        hosts = [host for p in range(1, 4)
                 for host in (("rx", 2 * p), ("rx", 2 * p + 1), ("rg", 2 * p), ("ri", 2 * p + 1))]
        hosts = hosts[2:] + [("gr", i) for i in range(KT)]
        for s in range(NU + 2):
            step_after[hosts[s]] = s

        def nk(b):
            return N_META + P * (b + 1)

        def ktiles(b):
            return [(t, min(P, nk(b) - P * t)) for t in range(3) if nk(b) > P * t]

        @block.sync
        def _(spe):
            for k in range(3):
                src = x_in[0, P * k:P * k + P, :] if k < 2 else meta_in[:, :]
                if k < 2:
                    spe.dma_start(X[:, k, :], src).then_inc((x_in0, x_in1)[k], 16)
                else:
                    spe.dma_start(metab[0:N_META, :], src).then_inc(meta_in_s, 16)
            kview = w_in[0].rearrange("(k p) n -> p k n", p=P)
            for n, (kind, a, w) in enumerate(LOADS):
                s = n % SLOTS
                if n >= SLOTS:
                    spe.wait_ge(weights_used, n - SLOTS + 1)
                if kind == "in":
                    parts = [(KT * w, kview[:, :, a:a + w], KT)]
                elif kind == "ro":
                    parts = [(KT * w, w_ro[0].rearrange("(k p) n -> p k n", p=P)[:, :, a:a + w], KT)]
                elif kind == "uq":
                    parts = [(QT * w, w_uq[0].rearrange("(k p) n -> p k n", p=P)[:, :, a:a + w], QT)]
                elif kind == "ukv":
                    parts = [(KVT * w, w_ukv[0].rearrange("(k p) n -> p k n", p=P), KVT)]
                elif kind == "ao":
                    parts = [(4 * w, w_ao[0].rearrange("(k p) n -> p k n", p=P)[:, :, a:a + w], 4)]
                elif kind == "out":
                    parts = [(2 * D, w_out[0].rearrange("(k p) n -> p k n", p=P)[:, a:a + w, :], 2)]
                else:
                    parts = [(2 * P, w_rg_a[0].rearrange("b i j -> i b j")[:, a:a + w, :], 2),
                             (2 * P, w_rg_x[0].rearrange("b i j -> i b j")[:, a:a + w, :], 2)]
                o = 0
                for width, src, k in parts:
                    spe.dma_start(ring[:, s, o:o + width].rearrange("p (k n) -> p k n", k=k), src)\
                       .then_inc(slot_loaded[s], 16)
                    o += width

            def expert_loads(it, i):
                for u in range(UNROLL):
                    for c in range(PER_EXPERT):
                        m = u * PER_EXPERT + c
                        s = (M0 + m) % SLOTS
                        spe.wait_ge(weights_used, it * (UNROLL * PER_EXPERT) + (M0 + m - SLOTS + 1))
                        if c < KT:
                            src = w_up[0, i * UNROLL + u, P * c:P * c + P, :]
                            dst = ring[:, s, :]
                        else:
                            r = 2 * P * (c - KT)
                            src = w_down[0, i * UNROLL + u, r:r + 2 * P, :].rearrange("(k p) n -> p k n", p=P)
                            dst = ring[:, s, :].rearrange("p (k n) -> p k n", k=2)
                        spe.dma_start(dst, src).then_inc(slot_loaded[s], 16)

            with spe.Fori(0, GROUPS) as it:
                expert_loads(it, it)
            spe.wait_ge(flag_ready, 1)
            over = spe.value_load(flag_i[0:1, 0:1], min_val=0, max_val=1)
            with spe.If(over > 0):
                with spe.Fori(1, BLOCKS) as j:
                    with spe.Fori(0, GROUPS) as i:
                        expert_loads(j * GROUPS + i, i)
            for i in range(TT):
                spe.wait_ge(fin_ready, i + 1)
                spe.dma_start(out[0, P * i:P * i + P, :], X[:, i, :]).then_inc(out_stored, 16)
            spe.wait_ge(out_stored, 16 * TT)

        @block.gpsimd
        def _(pool):
            pool.wait_ge(attn_ready, NU)
            pool.dma_start(gffn, norm_ffn_g[0:1, :].broadcast_to([P, D])).then_inc(moe_in, 16)
            pool.dma_start(wr, w_router[0].rearrange("(k p) e -> p k e", p=P)).then_inc(moe_in, 16)
            pool.dma_start(brt[0:1, :], b_router[0:1, :]).then_inc(moe_in, 16)
            pool.dma_start(cb, cb_in[:, :]).then_inc(moe_in, 16)
            pool.dma_start(bup[0:E, :], b_up[0]).then_inc(moe_in, 16)
            pool.wait_ge(y_zeroed, 1)
            for c in range(2):
                pool.dma_start(y[CAP * c:CAP * c + E, :], b_down[0, :, 512 * c:512 * c + 512]).then_inc(bdn_in, 16)
            pool.wait_ge(h_ready, TT)
            pool.dma_start(gfin, norm_final_g.rearrange("(a d) -> a d", a=1).broadcast_to([P, D])).then_inc(gfin_in, 16)

        @block.tensor
        def _(pe):
            owed = [0]

            def settle(ins):
                if owed[0]:
                    ins.then_inc(weights_used, owed[0])
                    owed[0] = 0

            def slot_of(n):
                return n % SLOTS

            def wait_load(n):
                s = slot_of(n)
                total = sum(32 if LOADS[m][0] == "gates" else 16 for m in range(s, n + 1, SLOTS))
                pe.wait_ge(slot_loaded[s], total)

            def wslot(n, k):
                return ring[:, slot_of(n), :].rearrange("p (k n) -> p k n", k=k)

            load_at = {}
            for n, (kind, a, w) in enumerate(LOADS):
                load_at[(kind, a)] = n

            def begin(job):
                n = JOB[job]
                if n >= 3:
                    pe.wait_ge(proj_read, n - 2)
                return n % 3

            def in_cols(c):
                for (kind, a), n in load_at.items():
                    if kind == "in" and a <= c < a + LOADS[n][2]:
                        return n, c - a, LOADS[n][2]

            def project(job, c, width, lo, hi, part=0, last=False):
                n, o, w = in_cols(c)
                wait_load(n)
                b = begin(job)
                wv = ring[:, slot_of(n), 0:KT * w].rearrange("p (k n) -> p k n", k=KT)
                for k in range(KT):
                    ins = nc.tensor.matmul(ps[part:part + width, b, 0:hi - lo], wv[:, k, o:o + width],
                                           xnT[:, k, lo:hi], start=(k == 0), stop=(k == KT - 1))
                    if k == 0:
                        settle(ins)
                ins.then_inc(proj_done, 1)
                if last:
                    owed[0] += 1

            pe.wait_ge(vec_in_s, 16)
            pe.wait_ge(ident_in, 16)
            nc.tensor.transpose(ps[:, 7, 0:NVEC], vec_rows, ident[0:NVEC, 0:NVEC]).then_inc(vecT_done, 1)

            for t in (0, 2, 1):
                pe.wait_ge((x0s_ready, x1s_ready, ms_ready)[t], 1)
                for i in range(KT):
                    c = slice(P * i, P * i + P)
                    if t == 0 and i == 7:
                        pe.wait_ge(vec_read, 1)
                    if t < 2:
                        ins = nc.tensor.transpose(ps[:, i, N_META + P * t:N_META + P * t + P], xs[:, t, c], ident)
                    else:
                        nc.tensor.transpose(ps[:, i, 0:N_META], xs[0:N_META, 2, c], ident[0:N_META, 0:N_META])
                    if t == 1:
                        ins.then_inc(xT_done, 1)
            pe.wait_ge(xT_read, KT // 2)
            pe.wait_ge(xT_read_dve, KT // 2)

            for i in range(QT):
                project(("cq", i), OFF_CQ + P * i, P, N_META, T, last=(i == 1))
            for i in range(KVT):
                project(("ckv", i), OFF_CKV + P * i, P, 0, T, last=(i == 0))
            project(("kr", 0), OFF_KR, ROPE, 0, T, part=NOPE, last=True)
            project(("rx", 0), OFF_RX, P, 0, T)
            project(("rx", 1), OFF_RX + P, P, 0, T, last=True)

            pe.wait_ge(const_in, 16)
            pe.wait_ge(lora_sq, 2)
            for k in range(QT):
                ins = nc.tensor.matmul(ps[:, 4, 0:SEQ], ones, sqq[:, k, :], start=(k == 0), stop=(k == QT - 1))
            ins.then_inc(lora_sum, 1)
            for k in range(KVT):
                ins = nc.tensor.matmul(ps[:, 5, 0:T], ones, sqk[:, k, :], start=(k == 0), stop=(k == KVT - 1))
            ins.then_inc(lora_sum, 1)
            pe.wait_ge(proj_read, JOB[("kr", 0)] + 1)
            nc.tensor.matmul(ps[NOPE:QD, 6, 0:T], rotm, kh[NOPE:QD, 0, :], start=True, stop=True).then_inc(krot_done, 1)
            project(("rg", 0), OFF_RG, P, N_META, T)
            project(("rg", 1), OFF_RG + P, P, N_META, T, last=True)

            pe.wait_ge(lora_ready, 1)
            for h in range(HEADS):
                n = load_at[("uq", 384 * (h // 4))]
                wait_load(n)
                b = begin(("q", h))
                wv = ring[:, slot_of(n), 0:QT * 384].rearrange("p (k n) -> p k n", k=QT)
                for k in range(QT):
                    ins = nc.tensor.matmul(ps[0:QD, b, 0:SEQ], wv[:, k, QD * (h % 4):QD * (h % 4) + QD], cq[:, k, :],
                                           start=(k == 0), stop=(k == QT - 1))
                    if k == 0:
                        settle(ins)
                ins.then_inc(proj_done, 1)
                if h % 4 == 3:
                    owed[0] += 1
            pe.wait_ge(lora_ready, 2)
            n = load_at[("ukv", 0)]
            wait_load(n)
            wv = wslot(n, KVT)
            for h in range(HEADS):
                b = begin(("k", h))
                for k in range(KVT):
                    ins = nc.tensor.matmul(ps[0:NOPE, b, 0:T], wv[:, k, P * h:P * h + NOPE], ckv[:, k, :],
                                           start=(k == 0), stop=(k == KVT - 1))
                    if k == 0:
                        settle(ins)
                ins.then_inc(proj_done, 1)
                if 2 <= h < 6:
                    g = h - 2
                    if g == 0:
                        pe.wait_ge(proj_read, JOB[("q", HEADS - 1)] + 1)
                        pe.wait_ge(rope_ready, 1)
                        pe.wait_ge(lora_var, 2)
                    nc.tensor.matmul(ps[NOPE:QD, 4 + g, :].rearrange("p (h t) -> p h t", h=2), rotm,
                                     qh[NOPE:QD, 2 * g:2 * g + 2, :], start=True, stop=True).then_inc(qrot_done, 1)
            for t in range(3):
                b = begin(("v", t))
                m = min(P, T - P * t)
                for k in range(KVT):
                    ins = nc.tensor.matmul(ps[0:m, b, :].rearrange("p (h d) -> p h d", h=HEADS),
                                           ckv[:, k, P * t:P * t + m],
                                           wv[:, k, :].rearrange("p (h d) -> p h d", h=HEADS)[:, :, NOPE:P],
                                           start=(k == 0), stop=(k == KVT - 1))
                ins.then_inc(proj_done, 1)
            owed[0] += 1

            def attention_step(s):
                if s < NU:
                    h, b = UNITS[s]
                    if s == 0:
                        pe.wait_ge(rope_ready, 5)
                        pe.wait_ge(proj_read, JOB[("v", 2)] + 1)
                    if s >= 2:
                        pe.wait_ge(scores_read, s - 1)
                    nc.tensor.matmul(ps[:, 4 + s % 2, 0:nk(b)], qh[0:QD, h, P * b:P * b + P], kh[0:QD, h, 0:nk(b)],
                                     start=True, stop=True).then_inc(scores_done, 1)
                if s >= 2:
                    r = s - 2
                    h, b = UNITS[r]
                    pe.wait_ge(probsT_ready, r + 1)
                    if r >= 1:
                        pe.wait_ge(attn_ready, r)
                    o = VD * (h % 2)
                    kts = ktiles(b)
                    for t, m in kts:
                        ins = nc.tensor.matmul(ps[o:o + VD, 6, 3 * P:4 * P], vtok[0:m, t, VD * h:VD * h + VD],
                                               PT[0:m, r % 2, t, :], start=(t == 0), stop=(t == kts[-1][0]))
                    ins.then_inc(attn_done, 1)
                if 1 <= s <= NU:
                    r = s - 1
                    b = UNITS[r][1]
                    pe.wait_ge(probs_ready, r + 1)
                    for t, m in ktiles(b):
                        ins = nc.tensor.transpose(ps[0:m, 6, P * t:P * t + P], S[:, r % 2, P * t:P * t + m], ident)
                    ins.then_inc(probsT_done, 1)

            def lru_gates(p):
                n = load_at[("gates", 2 * p)]
                wait_load(n)
                wv = ring[:, slot_of(n), 0:4 * P].rearrange("p (g k n) -> p g k n", g=2, k=2)
                for g, name in ((0, "ra"), (1, "ri")):
                    for k in range(2):
                        i = 2 * p + k
                        b = begin((name, i))
                        pe.wait_ge(conv_ready, i + 1)
                        ins = nc.tensor.matmul(ps[:, b, 0:T], wv[:, g, k, :], xc[:, k, :], start=True, stop=True)
                        ins.then_inc(proj_done, 1)
                        if g == 1 and k == 1:
                            owed[0] += 1
                        if (name, i) in step_after:
                            attention_step(step_after[(name, i)])

            lru_gates(0)
            for p in range(1, 4):
                for name, off, lo in (("rx", OFF_RX, 0), ("rg", OFF_RG, N_META)):
                    for k in range(2):
                        i = 2 * p + k
                        project((name, i), off + P * i, P, lo, T, last=(k == 1))
                        if (name, i) in step_after:
                            attention_step(step_after[(name, i)])
                lru_gates(p)

            n_out = [0]

            def branch_begin():
                d = n_out[0]
                n_out[0] += 1
                if d >= 2:
                    pe.wait_ge(branch_read, d - 1)
                return (3, 7)[d % 2]

            for p in range(4):
                for i in (2 * p, 2 * p + 1):
                    project(("gr", i), OFF_GATE + D + P * i, P, N_META, T, last=(i % 2 == 1))
                    if ("gr", i) in step_after:
                        attention_step(step_after[("gr", i)])
                n = load_at[("ro", 256 * p)]
                wait_load(n)
                wv = wslot(n, KT)
                if p == 0:
                    pe.wait_ge(y_ready_s, 4)
                for i in range(2):
                    b = branch_begin()
                    for k in range(KT):
                        ins = nc.tensor.matmul(ps[:, b, 0:SEQ], wv[:, k, P * i:P * i + P], gel[:, k, :],
                                               start=(k == 0), stop=(k == KT - 1))
                        if k == 0:
                            settle(ins)
                    ins.then_inc(branch_done, 1)
                owed[0] += 1
            for g in range(2):
                for i in range(4 * g, 4 * g + 4):
                    project(("ga", i), OFF_GATE + P * i, P, N_META, T, last=(i % 2 == 1))
                n = load_at[("ao", 512 * g)]
                wait_load(n)
                wv = wslot(n, 4)
                pe.wait_ge(attn_ready, NU)
                for i in range(4):
                    b = branch_begin()
                    for k in range(4):
                        ins = nc.tensor.matmul(ps[:, b, 0:SEQ], wv[:, k, P * i:P * i + P], oT[:, k, :],
                                               start=(k == 0), stop=(k == 3))
                        if k == 0:
                            settle(ins)
                    ins.then_inc(branch_done, 1)
                owed[0] += 1

            pe.wait_ge(proj_read, len(jobs))
            pe.wait_ge(branch_read, 15)
            for i in range(TT):
                for r in range(4):
                    n = load_at[("out", 2 * r)]
                    if i == 0:
                        wait_load(n)
                        if r == 3:
                            pe.wait_ge(branch_read, 16)
                    wv = wslot(n, 2)
                    for k in range(2):
                        for c in range(2):
                            ins = nc.tensor.matmul(ps[:, 2 * i + c, :], mT[:, 2 * r + k, P * i:P * i + P],
                                                   wv[:, k, 512 * c:512 * c + 512],
                                                   start=(r == 0 and k == 0), stop=(r == 3 and k == 1))
                            if i == 0 and k == 0 and c == 0:
                                settle(ins)
                    if i == 1:
                        ins.then_inc(weights_used, 1)
                if i == 0:
                    ins.then_inc(out_done, 1)

            pe.wait_ge(moe_in, 16 * 5)
            for i in range(TT):
                pe.wait_ge(xn2_ready, i + 1)
                for k in range(KT):
                    ins = nc.tensor.transpose(ps[:, 4 + 2 * i + k // 4, P * (k % 4):P * (k % 4) + P],
                                              xn2[:, i, P * k:P * k + P], ident)
                ins.then_inc(xn2T_done, 1)
            for i in range(TT):
                pe.wait_ge(xn2T_ready, i + 1)
                pe.wait_ge(xn2T_ready2, i + 1)
                for k in range(KT):
                    nc.tensor.matmul(ps[:, i, 0:E], xn2T[:, i, k, :], wr[:, k, :], start=(k == 0), stop=False)
                nc.tensor.matmul(ps[:, i, 0:E], ones[0:1, :], brt[0:1, :], start=False, stop=True)\
                  .then_inc(logits_done, 1)

            pe.wait_ge(mask_ready, 1)
            nc.tensor.matmul(ps[:, 2, 0:E], upper, selm[:, 0, :], start=True, stop=True)
            nc.tensor.matmul(ps[:, 2, E:2 * E], ones, selm[:, 0, :], start=True, stop=False, skip_group_check=True)
            nc.tensor.matmul(ps[:, 2, E:2 * E], upper, selm[:, 1, :], start=False, stop=True, skip_group_check=True)\
              .then_inc(pos_done, 1)
            nc.tensor.matmul(ps[:, 3, 0:E], ones, selm[:, 0, :], start=True, stop=False)
            nc.tensor.matmul(ps[:, 3, 0:E], ones, selm[:, 1, :], start=False, stop=True).then_inc(pos_done, 1)

            def gather():
                for c in range(2):
                    for i in range(TT):
                        ins = nc.tensor.matmul(ps[CAP * c:CAP * c + CAP, 2, :], pick[:, i, :],
                                               xn2[:, i, 512 * c:512 * c + 512], start=(i == 0), stop=(i == TT - 1))
                ins.then_inc(gather_done, 1)

            def turn_route():
                for i in range(TT):
                    ins = nc.tensor.transpose(ps[:, 5, P * i:P * i + P], gpick[:, i, :], ident)
                ins.then_inc(gpickT_done, 1)

            def turn_gathered():
                for j in range(4):
                    ins = nc.tensor.transpose(ps[:, 3, P * j:P * j + P], xe[:, P * j:P * j + P], ident)
                ins.then_inc(xeT_done, 1)

            def scatter(u, i, it):
                pe.wait_ge(scat_added, (it * UNROLL + u) * TT + (i + 1))
                for c in range(2):
                    ins = nc.tensor.matmul(ps[:, 6 + c, :], gpickT[CAP * c:CAP * c + CAP, (u + 1) % 2, i, :],
                                           y[CAP * c:CAP * c + CAP, :], start=True, stop=True)
                ins.then_inc(scat_done, 1)

            pe.wait_ge(pick_ready, 1)
            gather()
            pe.wait_ge(gate_ready, 1)
            for i in range(TT):
                ins = nc.tensor.transpose(ps[:, 4, P * i:P * i + P], gate[:, i, 0:P], ident)
            ins.then_inc(gateT_done, 1)
            pe.wait_ge(xe_ready, 1)
            pe.wait_ge(pos_done_read, 1)
            turn_gathered()
            pe.wait_ge(route_ready, 1)
            turn_route()
            pe.wait_ge(bdn_in, 32)

            def experts(it):
                for u in range(UNROLL):
                    n = it * UNROLL + u
                    w0 = u * PER_EXPERT
                    def loaded(m):
                        s = (M0 + m) % SLOTS
                        before = sum(32 if LOADS[q][0] == "gates" else 16 for q in range(s, M0, SLOTS))
                        pe.wait_ge(slot_loaded[s], it * (16 * UNROLL * PER_EXPERT // SLOTS) + (before + 16 * (m // SLOTS + 1)))
                        return s
                    pe.wait_ge(hidden_read, n + 1)
                    for q in range(4):
                        c, b = q % 2, q // 2
                        nc.tensor.matmul(ps[CAP * c:CAP * c + CAP, b, :], sel[0:E, u % 2, :],
                                         bup[0:E, 512 * q:512 * q + 512], start=True, stop=False)
                    pe.wait_ge(xeT_ready, n + 1)
                    for k in range(KT):
                        s = loaded(w0 + k)
                        g, j = k // 4, k % 4
                        for q in range(4):
                            c, b = q % 2, q // 2
                            ins = nc.tensor.matmul(ps[CAP * c:CAP * c + CAP, b, :], xeT[:, j, CAP * g:CAP * g + CAP],
                                                   ring[:, s, 512 * q:512 * q + 512], start=False, stop=(k == KT - 1))
                        ins.then_inc(weights_used, 1)
                        if k == 1:
                            pe.wait_ge(y_ready, n + 1)
                            scatter(u, 0, it)
                        if k == 4:
                            scatter(u, 1, it)
                    pe.wait_ge(route_ready, n + 2)
                    pe.wait_ge(xe_ready, n + 1)
                    gather()
                    pe.wait_ge(gpickT_ready, n + 1)
                    turn_route()
                    pe.wait_ge(act_ready, n + 1)
                    for j in range(4):
                        ins = nc.tensor.transpose(ps[:, 4, P * j:P * j + P], act_h[:, P * j:P * j + P], ident)
                    ins.then_inc(actT_done, 1)
                    pe.wait_ge(xe_ready, n + 2)
                    turn_gathered()
                    pe.wait_ge(actT_ready, n + 1)
                    pe.wait_ge(gpickT_ready, n + 2)
                    for t in range(4):
                        s = loaded(w0 + KT + t)
                        wv = ring[:, s, :].rearrange("p (k n) -> p k n", k=2)
                        for k in range(2):
                            f = 2 * t + k
                            g, j = f // 4, f % 4
                            for c in range(2):
                                ins = nc.tensor.matmul(ps[CAP * c:CAP * c + CAP, 5, :], actT[:, j, CAP * g:CAP * g + CAP],
                                                       wv[:, k, 512 * c:512 * c + 512], start=(f == 0), stop=(f == 7))
                        ins.then_inc(weights_used, 1)

            with pe.Fori(0, GROUPS) as it:
                experts(it)
            pe.wait_ge(y_ready, E + 1)
            pe.wait_ge(scat_added, TT * E + 1)
            pe.wait_ge(flag_ready, 1)
            over = pe.value_load(flag_i[0:1, 0:1], min_val=0, max_val=1)
            with pe.If(over > 0):
                with pe.Fori(1, BLOCKS) as j:
                    with pe.Fori(0, GROUPS) as i:
                        experts(j * GROUPS + i)
                pe.wait_ge(y_ready, BLOCKS * E + 1)
                pe.wait_ge(scat_added, TT * BLOCKS * E + 1)
            for i in range(TT):
                for c in range(2):
                    ins = nc.tensor.matmul(ps[:, (6 if i == 0 else 0) + c, :], gpickT[CAP * c:CAP * c + CAP, 1, i, :],
                                           y[CAP * c:CAP * c + CAP, :], start=True, stop=True)
                ins.then_inc(last_scat, 1)

        @block.scalar
        def _(act):
            chain = [0]

            def link(ins):
                chain[0] += 1
                ins.then_inc(act_chain, 1)
                act.wait_ge(act_chain, chain[0])

            act.dma_start(vec_rows, vec_in[:, :]).then_inc(vec_in_s, 16)
            act.dma_start(ca[:, 0:P], ca_in[:, 0:P]).then_inc(ident_in, 16)
            act.dma_start(ca[:, P:], ca_in[:, P:]).then_inc(const_in, 16)
            act.wait_ge(ssx_set, 1)
            nc.scalar.activation(dummy, dummy, ACT.Sqrt)
            act.wait_ge(x_in0, 16)
            nc.scalar.activation(xs[:, 0, :], X[:, 0, :], ACT.Square, accum_out=ssx[:, 0:1]).then_inc(x0_sumsq, 1)
            act.wait_ge(meta_in_s, 16)
            nc.scalar.activation(xs[0:N_META, 2, :], metab[0:N_META, :], ACT.Square,
                                 accum_out=ssx[0:N_META, 2:3]).then_inc(x_sumsq, 1)
            act.wait_ge(x0_var, 1)
            nc.scalar.activation(rsx[:, 0:1], ssx[:, 0:1], ACT.Sqrt).then_inc(x0_std, 1)
            act.wait_ge(x_var, 1)
            nc.scalar.activation(rsx[:, 1:3], ssx[:, 1:3], ACT.Sqrt).then_inc(x_std, 1)
            act.wait_ge(ms_rs, 1)
            nc.scalar.activation(xs[0:N_META, 2, :], metab[0:N_META, :], ACT.Copy, scale=rsx[0:N_META, 2:3])\
              .then_inc(ms_ready, 1)
            act.wait_ge(vec_ready, 1)
            for i in range(0, KT, 2):
                act.wait_ge(xT_done, i + 1)
                nc.scalar.activation(xnT[:, i, :], ps[:, i, 0:T], ACT.Copy, scale=v("norm_mix_g", i)).then_inc(xT_read, 1)
            act.wait_ge(softplus_in, 1)
            nc.scalar.activation(sp[:, 0:8], sp[:, 0:8], ACT.Exp, scale=-1.0).then_inc(sp_exp, 1)

            def read(job):
                n = JOB[job]
                kind, i = job
                b = n % 3
                act.wait_ge(proj_done, n + 1)
                if kind == "cq":
                    ins = nc.scalar.activation(cq[:, i, :], ps[:, b, 0:SEQ], ACT.Copy)
                elif kind == "ckv":
                    ins = nc.scalar.activation(ckv[:, i, :], ps[:, b, 0:T], ACT.Copy)
                elif kind == "kr":
                    ins = nc.scalar.activation(kh[NOPE:QD, 0, :], ps[NOPE:QD, b, 0:T], ACT.Copy)
                elif kind == "rx":
                    if i == 0:
                        act.wait_ge(xs_read, 1)
                    if i >= 2:
                        act.wait_ge(conv_ready, i - 1)
                    ins = nc.scalar.activation(rxp[:, i % 2, CONV - 1:], ps[:, b, 0:T], ACT.Copy)
                elif kind == "q":
                    ins = nc.scalar.activation(qh[0:QD, i, :], ps[0:QD, b, 0:SEQ], ACT.Copy)
                elif kind == "k":
                    ins = nc.scalar.activation(kh[0:NOPE, i, :], ps[0:NOPE, b, 0:T], ACT.Copy)
                elif kind == "v":
                    m = min(P, T - P * i)
                    ins = nc.scalar.activation(vtok[0:m, i, :], ps[0:m, b, :], ACT.Copy)
                elif kind == "rg":
                    if i >= 2:
                        act.wait_ge(gelu_free, i // 2)
                    nc.scalar.activation(ug[:, i % 2, :], ps[:, b, 0:SEQ], ACT.Square)
                    ins = nc.scalar.activation(xg[:, i % 2, :], ps[:, b, 0:SEQ], ACT.Copy)
                elif kind == "ra":
                    if i >= 2:
                        act.wait_ge(y_ready_s, i // 2)
                    ins = nc.scalar.activation(tr[:, i % 2, :], ps[:, b, 0:T], ACT.Tanh, bias=hba[:, i:i + 1], scale=0.5)
                elif kind == "ri":
                    ins = nc.scalar.activation(ti[:, i % 2, :], ps[:, b, 0:T], ACT.Tanh, bias=hbx[:, i:i + 1], scale=0.5)
                elif kind == "gr":
                    if i == 0:
                        act.wait_ge(gelu_free, 4)
                    if i >= 4:
                        act.wait_ge(branch_read, i - 3)
                    ins = nc.scalar.activation(ta[:, i % 4, :], ps[:, b, 0:SEQ], ACT.Tanh, bias=hbg[:, 8 + i:9 + i], scale=0.5)
                else:
                    act.wait_ge(branch_read, 4 + i + 1)
                    ins = nc.scalar.activation(ta[:, i % 4, :], ps[:, b, 0:SEQ], ACT.Tanh, bias=hbg[:, i:i + 1], scale=0.5)
                ins.then_inc(proj_read, 1)

            def attention_read(s):
                if 1 <= s <= NU:
                    r = s - 1
                    kts = ktiles(UNITS[r][1])
                    act.wait_ge(probsT_done, r + 1)
                    full = len(kts) - 1
                    nc.scalar.activation(PT[:, r % 2, 0:full, :],
                                         ps[:, 6, 0:P * full].rearrange("p (k q) -> p k q", k=full), ACT.Copy)
                    t, m = kts[-1]
                    nc.scalar.activation(PT[0:m, r % 2, t, :], ps[0:m, 6, P * t:P * t + P], ACT.Copy)\
                      .then_inc(probsT_ready, 1)
                if s >= 2:
                    r = s - 2
                    h, b = UNITS[r]
                    o = VD * (h % 2)
                    act.wait_ge(attn_done, r + 1)
                    nc.scalar.activation(oT[o:o + VD, h // 2, P * b:P * b + P], ps[o:o + VD, 6, 3 * P:4 * P], ACT.Copy)\
                      .then_inc(attn_ready, 1)

            def attention_exp(s):
                if s >= NU:
                    return
                b = UNITS[s][1]
                act.wait_ge(rowmax_ready, s + 1)
                nc.scalar.activation(S[:, s % 2, 0:nk(b)], S[:, s % 2, 0:nk(b)], ACT.Exp, bias=nmx[:, s % 2:s % 2 + 1],
                                     accum_out=sm[:, s % 2:s % 2 + 1]).then_inc(exp_done, 1)

            def gelu(p):
                act.wait_ge(gelu_arg, p + 1)
                nc.scalar.activation(ug, ug, ACT.Tanh, scale=GELU_C).then_inc(gelu_tanh, 1)

            def decay(p):
                if p == 0:
                    act.wait_ge(hc_ready, 1)
                act.wait_ge(proj_read, JOB[("ra", 2 * p + 1)] + 1)
                for k in range(2):
                    i = 2 * p + k
                    nc.scalar.activation(av[:, k, :], tr[:, k, :], ACT.Exp, bias=hc[:, i:i + 1], scale=hc[:, i:i + 1])
                    nc.scalar.activation(th[:, k, :], tr[:, k, :], ACT.Tanh, bias=nhc[:, i:i + 1],
                                         scale=nhc[:, i:i + 1])
                    ins = nc.scalar.activation(tr[:, k, :], tr[:, k, :], ACT.Exp, bias=hc2[:, i:i + 1],
                                               scale=hc2[:, i:i + 1])
                ins.then_inc(lru_tanh, 1)
                act.wait_ge(lru_arg, p + 1)
                nc.scalar.activation(th, th, ACT.Sqrt, scale=0.25).then_inc(lru_sqrt, 1)

            for job in jobs:
                read(job)
                if job == ("rx", 1):
                    act.wait_ge(lora_var, 2)
                    nc.scalar.activation(rq, rq, ACT.Sqrt).then_inc(lora_std, 1)
                    nc.scalar.activation(rk, rk, ACT.Sqrt).then_inc(lora_std, 1)
                if (job[0] == "rg" and job[1] % 2 == 1 and job[1] > 1) or job == ("k", 0):
                    gelu(max(job[1], 0) // 2)
                if job in step_after:
                    attention_read(step_after[job])
                    attention_exp(step_after[job])
                if job[0] == "ri" and job[1] % 2 == 1:
                    decay(job[1] // 2)

            for i in range(TT):
                act.wait_ge(h_ready, i + 1)
                nc.scalar.activation(sqx[:, i, :], X[:, i, :], ACT.Square, accum_out=ss2[:, i:i + 1]).then_inc(h_sumsq, 1)
                act.wait_ge(h_var, i + 1)
                nc.scalar.activation(rs2[:, i:i + 1], ss2[:, i:i + 1], ACT.Sqrt).then_inc(h_std, 1)

            for i in range(TT):
                act.wait_ge(xn2T_done, i + 1)
                nc.scalar.activation(xn2T[:, i, 0:4, :], ps[:, 4 + 2 * i, :].rearrange("p (k t) -> p k t", k=4),
                                     ACT.Copy).then_inc(xn2T_ready, 1)

            act.wait_ge(mask_ready, 1)
            for i in range(TT):
                nc.scalar.activation(lg[:, i, :], lg[:, i, :], ACT.Exp, bias=nm1[:, i:i + 1]).then_inc(gexp_done, 1)

            act.wait_ge(gather_done, 1)
            nc.scalar.activation(xe, ps[:, 2, :], ACT.Copy).then_inc(xe_ready, 1)
            act.wait_ge(gateT_done, 1)
            nc.scalar.activation(gpickT[:, 1, :, :], ps[:, 4, 0:SEQ].rearrange("p (i t) -> p i t", i=TT),
                                 ACT.Copy).then_inc(y_ready, 1)
            act.wait_ge(gpickT_done, 1)
            nc.scalar.activation(gpickT[:, 0, :, :], ps[:, 5, 0:SEQ].rearrange("p (i t) -> p i t", i=TT),
                                 ACT.Copy).then_inc(gpickT_ready, 1)

            def experts(it):
                for u in range(UNROLL):
                    n = it * UNROLL + u
                    act.wait_ge(glu_ready, n + 1)
                    nc.scalar.activation(sg, hg, ACT.Sigmoid, scale=ALPHA).then_inc(sig_done, 1)
                    act.wait_ge(gather_done, n + 2)
                    act.wait_ge(xeT_done, n + 1)
                    nc.scalar.activation(xe, ps[:, 2, :], ACT.Copy).then_inc(xe_ready, 1)
                    act.wait_ge(gpickT_done, n + 2)
                    nc.scalar.activation(gpickT[:, (u + 1) % 2, :, :], ps[:, 5, 0:SEQ].rearrange("p (i t) -> p i t", i=TT),
                                         ACT.Copy).then_inc(gpickT_ready, 1)
                    act.wait_ge(actT_done, n + 1)
                    nc.scalar.activation(actT, ps[:, 4, :].rearrange("p (j t) -> p j t", j=4), ACT.Copy)\
                      .then_inc(actT_ready, 1)
                    act.wait_ge(weights_used, n * PER_EXPERT + (M0 + PER_EXPERT))
                    nc.scalar.activation(y, ps[:, 5, :], ACT.Copy).then_inc(y_ready, 1)

            with act.Fori(0, GROUPS) as it:
                experts(it)
            act.wait_ge(flag_ready, 1)
            over = act.value_load(flag_i[0:1, 0:1], min_val=0, max_val=1)
            with act.If(over > 0):
                with act.Fori(1, BLOCKS) as j:
                    with act.Fori(0, GROUPS) as i:
                        experts(j * GROUPS + i)

            nc.scalar.activation(rs2[:, 0:1], rs2[:, 0:1], ACT.Sqrt)
            for i in range(TT):
                act.wait_ge(last_added, i + 1)
                nc.scalar.activation(sqf[:, i, :], X[:, i, :], ACT.Square, accum_out=ssf[:, i:i + 1]).then_inc(f_sumsq, 1)
                act.wait_ge(f_var, i + 1)
                nc.scalar.activation(rsf[:, i:i + 1], ssf[:, i:i + 1], ACT.Sqrt).then_inc(f_std, 1)

        @block.vector
        def _(dve):
            chain = [0]

            def link(ins):
                chain[0] += 1
                ins.then_inc(dve_chain, 1)
                dve.wait_ge(dve_chain, chain[0])

            V = nc.vector
            V.memset(dummy, 1.0)
            V.memset(ssx[:, 2:3], 1.0).then_inc(ssx_set, 1)
            dve.wait_ge(x_in1, 16)
            V.tensor_tensor_reduce(xs[:, 1, :], X[:, 1, :], X[:, 1, :], 1.0, 0.0, ALU.mult, ALU.add, ssx[:, 1:2])\
             .then_inc(x_sumsq, 1)
            dve.wait_ge(x0_sumsq, 1)
            V.tensor_scalar(ssx[:, 0:1], ssx[:, 0:1], 1.0 / D, EPS, ALU.mult, ALU.add).then_inc(x0_var, 1)
            dve.wait_ge(x_sumsq, 2)
            V.tensor_scalar(ssx[:, 1:3], ssx[:, 1:3], 1.0 / D, EPS, ALU.mult, ALU.add).then_inc(x_var, 1)
            dve.wait_ge(vecT_done, 1)
            V.tensor_copy(vec[:, :], ps[:, 7, 0:NVEC]).then_inc(vec_read, 1)
            dve.wait_ge(x0_std, 1)
            link(V.reciprocal(rsx[:, 0:1], rsx[:, 0:1]))
            V.tensor_scalar(xs[:, 0, :], X[:, 0, :], rsx[:, 0:1], None, ALU.mult).then_inc(x0s_ready, 1)
            dve.wait_ge(x_std, 1)
            V.reciprocal(rsx[:, 1:3], rsx[:, 1:3]).then_inc(ms_rs, 1)
            dve.wait_ge(ms_rs, 1)
            V.tensor_scalar(xs[:, 1, :], X[:, 1, :], rsx[:, 1:2], None, ALU.mult).then_inc(x1s_ready, 1)
            dve.wait_ge(vec_read, 1)
            lam = vec[:, VEC_AT["rg_lambda"]:VEC_AT["rg_lambda"] + 8]
            V.tensor_scalar(hba, vec[:, VEC_AT["b_rg_a"]:VEC_AT["b_rg_a"] + 8], 0.5, None, ALU.mult)
            V.tensor_scalar(hbx, vec[:, VEC_AT["b_rg_x"]:VEC_AT["b_rg_x"] + 8], 0.5, None, ALU.mult)
            V.tensor_scalar(hbg, vec[:, VEC_AT["b_gate"]:VEC_AT["b_gate"] + 16], 0.5, None, ALU.mult).then_inc(vec_ready, 1)
            for i in range(1, KT, 2):
                dve.wait_ge(xT_done, i + 1)
                V.tensor_scalar(xnT[:, i, :], ps[:, i, 0:T], v("norm_mix_g", i), None, ALU.mult).then_inc(xT_read_dve, 1)
            link(V.tensor_scalar(sp[:, 8:16], lam, -1.0, None, ALU.mult))
            V.tensor_tensor(sp[:, 0:8], sp[:, 8:16], lam, ALU.max).then_inc(softplus_in, 1)
            dve.wait_ge(sp_exp, 1)
            link(V.tensor_scalar(sp[:, 16:24], sp[:, 0:8], 2.0, None, ALU.add))
            link(V.reciprocal(sp[:, 16:24], sp[:, 16:24]))
            link(V.tensor_tensor(sp[:, 16:24], sp[:, 0:8], sp[:, 16:24], ALU.mult))
            link(V.tensor_tensor(sp[:, 0:8], sp[:, 16:24], sp[:, 16:24], ALU.mult))
            link(V.tensor_scalar(sp[:, 24:32], sp[:, 0:8], 1.0 / 17, 1.0 / 15, ALU.mult, ALU.add))
            for d in (13, 11, 9, 7, 5, 3, 1):
                link(V.tensor_tensor(sp[:, 24:32], sp[:, 24:32], sp[:, 0:8], ALU.mult))
                link(V.tensor_scalar(sp[:, 24:32], sp[:, 24:32], 1.0 / d, None, ALU.add))
            link(V.tensor_tensor(sp[:, 24:32], sp[:, 24:32], sp[:, 16:24], ALU.mult))
            link(V.tensor_scalar(sp[:, 8:16], sp[:, 8:16], 0.0, None, ALU.max))
            link(V.scalar_tensor_tensor(out=sp[:, 24:32], in0=sp[:, 24:32], scalar=2.0, in1=sp[:, 8:16],
                                        op0=ALU.mult, op1=ALU.add))
            V.tensor_scalar(hc, sp[:, 24:32], -LRU_C / 2, None, ALU.mult)
            V.tensor_scalar(hc2, sp[:, 24:32], -LRU_C, None, ALU.mult)
            V.tensor_scalar(nhc, sp[:, 24:32], LRU_C / 2, None, ALU.mult).then_inc(hc_ready, 1)

            dve.wait_ge(xT_done, KT)
            V.memset(rxp[:, :, 0:CONV - 1], 0.0).then_inc(xs_read, 1)
            dve.wait_ge(proj_read, JOB[("cq", QT - 1)] + 1)
            V.tensor_tensor(sqq, cq, cq, ALU.mult).then_inc(lora_sq, 1)
            dve.wait_ge(proj_read, JOB[("ckv", KVT - 1)] + 1)
            V.tensor_tensor(sqk, ckv, ckv, ALU.mult).then_inc(lora_sq, 1)

            def conv(i):
                k = i % 2
                dve.wait_ge(proj_read, JOB[("rx", i)] + 1)
                if k == 0 and i >= 2:
                    dve.wait_ge(proj_done, JOB[("ri", i - 1)] + 1)
                link(V.tensor_scalar(xc[:, k, :], rxp[:, k, 3:3 + T], v("conv_w", 8 * 3 + i), v("conv_b", i),
                                     ALU.mult, ALU.add))
                for w in (2, 1, 0):
                    ins = V.scalar_tensor_tensor(out=xc[:, k, :], in0=rxp[:, k, w:w + T], scalar=v("conv_w", 8 * w + i),
                                                 in1=xc[:, k, :], op0=ALU.mult, op1=ALU.add)
                    if w:
                        link(ins)
                ins.then_inc(conv_ready, 1)

            dve.wait_ge(xs_read, 1)
            dve.wait_ge(lora_sum, 2)
            V.tensor_scalar(rq, ps[:, 4, 0:SEQ], 1.0 / Q_LORA, EPS, ALU.mult, ALU.add).then_inc(lora_var, 1)
            V.tensor_scalar(rk, ps[:, 5, 0:T], 1.0 / KV_LORA, EPS, ALU.mult, ALU.add).then_inc(lora_var, 1)
            dve.wait_ge(lora_std, 2)
            link(V.reciprocal(rq, rq))
            for k in range(QT):
                ins = V.scalar_tensor_tensor(out=cq[:, k, :], in0=cq[:, k, :], scalar=v("q_norm_g", k), in1=rq,
                                             op0=ALU.mult, op1=ALU.mult)
            ins.then_inc(lora_ready, 1)
            link(V.reciprocal(rk, rk))
            for k in range(KVT):
                ins = V.scalar_tensor_tensor(out=ckv[:, k, :], in0=ckv[:, k, :], scalar=v("kv_norm_g", k), in1=rk,
                                             op0=ALU.mult, op1=ALU.mult)
            ins.then_inc(lora_ready, 1)
            conv(0)
            conv(1)

            dve.wait_ge(krot_done, 1)
            ku = ropeu[NOPE:QD, :, :].rearrange("p k t -> p (k t)")[:, 0:T]
            V.tensor_tensor(ku, ps[NOPE:QD, 6, 0:T], sinT, ALU.mult)
            link(V.tensor_tensor(kh[NOPE:QD, 0, :], kh[NOPE:QD, 0, :], cosT, ALU.mult))
            link(V.tensor_tensor(kh[NOPE:QD, 0, :], kh[NOPE:QD, 0, :], ku, ALU.add))
            V.tensor_copy(kh[NOPE:QD, 1:HEADS, :], kh[NOPE:QD, 0:1, :].broadcast_to([ROPE, HEADS - 1, T]))\
             .then_inc(rope_ready, 1)
            def gelu_arg_of(p):
                dve.wait_ge(proj_read, JOB[("rg", 2 * p + 1)] + 1)
                link(V.tensor_scalar(ug, ug, 0.044715, 1.0, ALU.mult, ALU.add))
                V.tensor_tensor(ug, ug, xg, ALU.mult).then_inc(gelu_arg, 1)

            gelu_arg_of(0)
            cos2 = ca[NOPE:QD, CA["cos"][0] + N_META:CA["cos"][1]].rearrange("p (a t) -> p a t", a=1).broadcast_to([ROPE, 2, SEQ])
            sin2 = ca[NOPE:QD, CA["sin"][0] + N_META:CA["sin"][1]].rearrange("p (a t) -> p a t", a=1).broadcast_to([ROPE, 2, SEQ])
            for g in range(4):
                dve.wait_ge(qrot_done, g + 1)
                q2 = qh[NOPE:QD, 2 * g:2 * g + 2, :]
                V.tensor_tensor(ropeu[NOPE:QD, :, :], ps[NOPE:QD, 4 + g, :].rearrange("p (h t) -> p h t", h=2), sin2, ALU.mult)
                link(V.tensor_tensor(q2, q2, cos2, ALU.mult))
                ins = V.tensor_tensor(q2, q2, ropeu[NOPE:QD, :, :], ALU.add)
                if g < 3:
                    ins.then_inc(rope_ready, 1)
                    dve.wait_ge(rope_ready, g + 2)
                else:
                    ins.then_inc(rope_ready, 1)

            def gelu_end(p):
                dve.wait_ge(gelu_tanh, p + 1)
                V.scalar_tensor_tensor(out=gel[:, 2 * p:2 * p + 2, :], in0=ug, scalar=1.0, in1=xg,
                                       op0=ALU.add, op1=ALU.mult).then_inc(gelu_free, 1)

            def recur_arg(p):
                dve.wait_ge(proj_read, JOB[("ri", 2 * p + 1)] + 1)
                V.scalar_tensor_tensor(out=ti, in0=ti, scalar=1.0, in1=xc, op0=ALU.add, op1=ALU.mult)
                dve.wait_ge(lru_tanh, p + 1)
                V.scalar_tensor_tensor(out=th, in0=tr, scalar=1.0, in1=th, op0=ALU.add, op1=ALU.mult).then_inc(lru_arg, 1)

            def recur(p):
                dve.wait_ge(lru_sqrt, p + 1)
                dve.wait_ge(gelu_free, p + 1)
                link(V.tensor_tensor(ti, ti, th, ALU.mult))
                V.tensor_tensor_scan(tr[:, 0, :], av[:, 0, :], ti[:, 0, :], 0.0, ALU.mult, ALU.add)
                link(V.tensor_tensor_scan(tr[:, 1, :], av[:, 1, :], ti[:, 1, :], 0.0, ALU.mult, ALU.add))
                g2 = gel[:, 2 * p:2 * p + 2, :]
                V.scalar_tensor_tensor(out=g2, in0=g2, scalar=0.5, in1=tr[:, :, N_META:T], op0=ALU.mult, op1=ALU.mult)\
                 .then_inc(y_ready_s, 1)

            def softmax_in(s):
                b = UNITS[s][1]
                k = s % 2
                w = nk(b)
                dve.wait_ge(scores_done, s + 1)
                if s >= 2:
                    dve.wait_ge(probsT_done, s - 1)
                ins = V.scalar_tensor_tensor(out=S[:, k, 0:w], in0=ps[:, 4 + k, 0:w], scalar=SCALE,
                                             in1=maskc[:, T - w:T], op0=ALU.mult, op1=ALU.add)
                ins.then_inc(scores_read, 1)
                dve.wait_ge(scores_read, s + 1)
                link(V.tensor_reduce(mx[:, k:k + 1], S[:, k, 0:w], AX_X, ALU.max))
                V.tensor_scalar(nmx[:, k:k + 1], mx[:, k:k + 1], -1.0, None, ALU.mult).then_inc(rowmax_ready, 1)

            def softmax_out(s):
                b = UNITS[s][1]
                k = s % 2
                dve.wait_ge(exp_done, s + 1)
                link(V.reciprocal(rsm[:, k:k + 1], sm[:, k:k + 1]))
                V.tensor_scalar(S[:, k, 0:nk(b)], S[:, k, 0:nk(b)], rsm[:, k:k + 1], None, ALU.mult).then_inc(probs_ready, 1)

            def attention_step(s):
                if s < NU:
                    softmax_in(s)
                if s < NU:
                    softmax_out(s)

            def merge_rec(i):
                dve.wait_ge(proj_read, JOB[("gr", i)] + 1)
                dve.wait_ge(branch_done, i + 1)
                V.scalar_tensor_tensor(out=mT[:, i, :], in0=ta[:, i % 4, :], scalar=1.0, in1=ps[:, (3, 7)[i % 2], 0:SEQ],
                                       op0=ALU.add, op1=ALU.mult).then_inc(branch_read, 1)

            def merge_attn(i):
                dve.wait_ge(proj_read, JOB[("ga", i)] + 1)
                dve.wait_ge(branch_done, KT + i + 1)
                link(V.scalar_tensor_tensor(out=ta[:, i % 4, :], in0=ta[:, i % 4, :], scalar=1.0,
                                            in1=ps[:, (3, 7)[i % 2], 0:SEQ], op0=ALU.add, op1=ALU.mult))
                V.tensor_tensor(mT[:, i, :], mT[:, i, :], ta[:, i % 4, :], ALU.add).then_inc(branch_read, 1)

            gelu_end(0)
            for job in jobs[JOB[("ra", 0)]:JOB[("ga", 0)]]:
                kind, i = job
                if job in step_after:
                    attention_step(step_after[job])
                if kind == "rx":
                    if i % 2 == 0:
                        recur(i // 2 - 1)
                    conv(i)
                if kind == "rg" and i % 2 == 1:
                    gelu_arg_of(i // 2)
                    gelu_end(i // 2)
                if kind == "ri" and i % 2 == 1:
                    recur_arg(i // 2)
                if job == ("gr", 0):
                    recur(3)
                if kind == "gr" and i % 2 == 1:
                    merge_rec(i - 1)
                    merge_rec(i)

            for i in range(KT):
                merge_attn(i)

            def pick_tokens(n):
                for i in range(TT):
                    ins = V.tensor_scalar(pick[:, i, :], slot_id[:, 0:CAP], posm[:, i, bass.ds(n, 1)], None, ALU.is_equal)
                ins.then_inc(pick_ready, 1)

            def route(n, par):
                for i in range(TT):
                    V.tensor_scalar(gpick[:, i, :], slot_id, posm[:, i, bass.ds(n, 1)], gate[:, i, bass.ds(n, 1)],
                                    ALU.is_equal, ALU.mult)
                V.tensor_scalar(sel[0:E, par, :], ones[0:E, 0:CAP], pick_e[0:E, bass.ds(n, 1)], None, ALU.mult)\
                 .then_inc(route_ready, 1)

            for i in range(TT):
                if i == 0:
                    dve.wait_ge(out_done, 1)
                else:
                    dve.wait_ge(weights_used, M0)
                V.scalar_tensor_tensor(out=X[:, i, :].rearrange("p (c n) -> p c n", c=2), in0=ps[:, 2 * i:2 * i + 2, :],
                                       scalar=0.5, in1=X[:, i, :].rearrange("p (c n) -> p c n", c=2),
                                       op0=ALU.mult, op1=ALU.add).then_inc(h_ready, 1)
                if i == 0:
                    V.memset(y, 0.0).then_inc(y_zeroed, 1)
                dve.wait_ge(h_sumsq, i + 1)
                V.tensor_scalar(ss2[:, i:i + 1], ss2[:, i:i + 1], 1.0 / D, EPS, ALU.mult, ALU.add).then_inc(h_var, 1)
                dve.wait_ge(h_std, i + 1)
                link(V.reciprocal(rs2[:, i:i + 1], rs2[:, i:i + 1]))
                if i == 0:
                    dve.wait_ge(moe_in, 16 * 5)
                V.scalar_tensor_tensor(out=xn2[:, i, :], in0=X[:, i, :], scalar=rs2[:, i:i + 1], in1=gffn,
                                       op0=ALU.mult, op1=ALU.mult).then_inc(xn2_ready, 1)
            for i in range(TT):
                dve.wait_ge(xn2T_done, i + 1)
                V.tensor_copy(xn2T[:, i, 4:8, :], ps[:, 5 + 2 * i, :].rearrange("p (k t) -> p k t", k=4))\
                 .then_inc(xn2T_ready2, 1)

            t8 = top8.rearrange("p (i k) -> p i k", i=TT)
            for i in range(TT):
                dve.wait_ge(logits_done, i + 1)
                link(V.tensor_copy(lg[:, i, :], ps[:, i, 0:E]))
                ins = V.max(t8[:, i, :], lg[:, i, :])
            link(ins)
            V.tensor_scalar(nm1.rearrange("p (i k) -> p i k", k=1), t8[:, :, 0:1], -1.0, None, ALU.mult)
            k4 = t8[:, :, TOP_K - 1:TOP_K].broadcast_to([P, TT, E])
            gt, eq, rank = (tmp[:, 2 * q:2 * q + 2, :] for q in range(3))
            V.tensor_tensor(eq, lg, k4, ALU.is_equal)
            link(V.tensor_tensor(gt, lg, k4, ALU.is_gt))
            link(V.tensor_reduce(ngt, gt, AX_X, ALU.add))
            for i in range(TT):
                ins = V.tensor_tensor_scan(rank[:, i, :], ones[:, 0:E], eq[:, i, :], ngt[:, i:i + 1], ALU.mult, ALU.add)
            link(ins)
            link(V.scalar_tensor_tensor(out=eq, in0=rank, scalar=TOP_K + 0.5, in1=eq, op0=ALU.is_lt, op1=ALU.mult))
            V.tensor_tensor(selm, gt, eq, ALU.add).then_inc(mask_ready, 1)
            dve.wait_ge(mask_ready, 1)
            dve.wait_ge(pos_done, 1)
            link(V.scalar_tensor_tensor(out=rank, in0=ps[:, 2, 0:TT * E].rearrange("p (i e) -> p i e", i=TT), scalar=1.0,
                                        in1=selm, op0=ALU.add, op1=ALU.mult))
            for j in range(BLOCKS + 1):
                w = min(E, NCOL - E * j)
                bb = block_base[:, E * j:E * j + w].rearrange("p (a n) -> p a n", a=1).broadcast_to([P, TT, w])
                ins = V.scalar_tensor_tensor(out=posm[:, :, E * j:E * j + w], in0=rank[:, :, 0:w], scalar=-1.0,
                                             in1=bb, op0=ALU.add, op1=ALU.subtract)
                if j == 0:
                    link(ins)
                    pick_tokens(0)
            dve.wait_ge(gexp_done, TT)
            link(V.tensor_tensor(lg, lg, selm, ALU.mult))
            link(V.tensor_reduce(esum, lg, AX_X, ALU.add))
            link(V.reciprocal(esum, esum))
            for i in range(TT):
                for j in range(BLOCKS + 1):
                    w = min(E, NCOL - E * j)
                    ins = V.tensor_scalar(gate[:, i, E * j:E * j + w], lg[:, i, 0:w], esum[:, i:i + 1], None, ALU.mult)
            ins.then_inc(gate_ready, 1)
            dve.wait_ge(gate_ready, 1)
            route(0, 0)
            dve.wait_ge(pos_done, 2)
            V.tensor_reduce(cmax[:, 0:1], ps[:, 3, 0:E], AX_X, ALU.max).then_inc(pos_done_read, 1)
            dve.wait_ge(pos_done_read, 1)
            link(V.tensor_scalar(cmax[:, 1:2], cmax[:, 0:1], CAP + 0.5, None, ALU.is_gt))
            V.tensor_copy(flag_i[0:1, 0:1], cmax[0:1, 1:2]).then_inc(flag_ready, 1)
            dve.sem_inc(hidden_read, 1)
            dve.sem_inc(scat_added, 1)
            dve.wait_ge(xeT_done, 1)
            V.tensor_copy(xeT, ps[:, 3, :].rearrange("p (j t) -> p j t", j=4)).then_inc(xeT_ready, 1)

            def experts(it):
                for u in range(UNROLL):
                    n = it * UNROLL + u
                    dve.wait_ge(gpickT_done, n + 1)
                    pick_tokens(n + 1)
                    route(n + 1, (u + 1) % 2)
                    for i in range(TT):
                        dve.wait_ge(scat_done, n * TT + (i + 1))
                        xi = X[:, i, :].rearrange("p (c n) -> p c n", c=2)
                        V.tensor_tensor(xi, ps[:, 6:8, :], xi, ALU.add).then_inc(scat_added, 1)
                    dve.wait_ge(weights_used, n * PER_EXPERT + (M0 + KT))
                    V.tensor_scalar(hg, ps[:, 0, :], LIMIT, None, ALU.min).then_inc(glu_ready, 1)
                    V.tensor_scalar(hl, ps[:, 1, :], LIMIT, -LIMIT, ALU.min, ALU.max).then_inc(hidden_read, 1)
                    dve.wait_ge(hidden_read, n + 2)
                    V.scalar_tensor_tensor(out=hl, in0=hl, scalar=1.0, in1=hg, op0=ALU.add, op1=ALU.mult)\
                     .then_inc(lin_ready, 1)
                    dve.wait_ge(lin_ready, n + 1)
                    dve.wait_ge(sig_done, n + 1)
                    V.tensor_tensor(act_h, hl, sg, ALU.mult).then_inc(act_ready, 1)
                    dve.wait_ge(xeT_done, n + 2)
                    V.tensor_copy(xeT, ps[:, 3, :].rearrange("p (j t) -> p j t", j=4)).then_inc(xeT_ready, 1)

            with dve.Fori(0, GROUPS) as it:
                experts(it)
            dve.wait_ge(flag_ready, 1)
            over = dve.value_load(flag_i[0:1, 0:1], min_val=0, max_val=1)
            with dve.If(over > 0):
                with dve.Fori(1, BLOCKS) as j:
                    with dve.Fori(0, GROUPS) as i:
                        experts(j * GROUPS + i)
            for i in range(TT):
                dve.wait_ge(last_scat, i + 1)
                xi = X[:, i, :].rearrange("p (c n) -> p c n", c=2)
                V.tensor_tensor(xi, ps[:, 6:8, :] if i == 0 else ps[:, 0:2, :], xi, ALU.add).then_inc(last_added, 1)
            dve.wait_ge(gfin_in, 16)
            for i in range(TT):
                dve.wait_ge(f_sumsq, i + 1)
                V.tensor_scalar(ssf[:, i:i + 1], ssf[:, i:i + 1], 1.0 / D, EPS, ALU.mult, ALU.add).then_inc(f_var, 1)
                dve.wait_ge(f_std, i + 1)
                link(V.reciprocal(rsf[:, i:i + 1], rsf[:, i:i + 1]))
                V.scalar_tensor_tensor(out=X[:, i, :], in0=X[:, i, :], scalar=rsf[:, i:i + 1], in1=gfin,
                                       op0=ALU.mult, op1=ALU.mult).then_inc(fin_ready, 1)


_INS = ["x", "meta_tokens", "vec", "ca", "cb", "w_in", "w_uq", "w_ukv", "w_ao", "w_rg_a", "w_rg_x", "w_ro", "w_out",
        "norm_ffn_g", "w_router", "b_router", "w_up", "b_up", "w_down", "b_down", "norm_final_g"]


def kernel(**inputs):
    import concourse.bacc as _bacc
    from concourse.bass_utils import run_bass_kernel_spmd as _run

    arrays = {k: np.ascontiguousarray(np.asarray(a)) for k, a in inputs.items()}
    arrays["vec"] = np.concatenate([arrays[name].reshape(rows, P) for name, rows in VEC_ROWS], axis=0)
    arrays["ca"], arrays["cb"] = constants()
    nc = _bacc.Bacc("TRN2", target_bir_lowering=False, num_devices=1)
    feed, args = {}, []
    for name in _INS:
        a = arrays[name]
        feed[f"in_{name}_dram"] = a
        args.append(nc.dram_tensor(f"in_{name}_dram", a.shape, mybir.dt.from_np(a.dtype), kind="ExternalInput").ap())
    args.append(nc.dram_tensor("out_0_dram", (1, SEQ, D), F32, kind="ExternalOutput").ap())
    layer(nc, *args)
    r = _run(nc, [feed], core_ids=[0])
    return r.results[0]["out_0_dram"]
```

```python
import math
from contextlib import ExitStack

import numpy as np

import concourse.bass as bass
from concourse import mybir

F32 = mybir.dt.float32
I32 = mybir.dt.int32
ALU = mybir.AluOpType
ACT = mybir.ActivationFunctionType
AX_X = mybir.AxisListType.X

P = 128
D = 1024
N_META = 16
SEQ = 256
T = SEQ + N_META
EPS = 1e-6
HEADS = 8
Q_LORA, KV_LORA = 384, 256
NOPE, ROPE, VD = 64, 32, 64
QD = NOPE + ROPE
ROPE_BASE = 10000.0
CONV = 4
LRU_C = 8.0
E = 32
TOP_K = 4
F = 1024
ALPHA, LIMIT = 1.702, 7.0
OFF_CQ = 0
OFF_CKV = OFF_CQ + Q_LORA
OFF_KR = OFF_CKV + KV_LORA
OFF_RX = OFF_KR + ROPE
OFF_RG = OFF_RX + D
OFF_GATE = OFF_RG + D
KT = D // P
QT = Q_LORA // P
KVT = KV_LORA // P
TT = SEQ // P
SCALE = (NOPE + ROPE) ** -0.5
GELU_C = math.sqrt(2.0 / math.pi)
MASKED = -3.0e38

SLOTS = 16
SLOT = 2048
CAP = 64
BLOCKS = SEQ // CAP
UNROLL = 4
GROUPS = E // UNROLL
PER_EXPERT = 12
NCOL = E * BLOCKS + UNROLL

VEC_ROWS = [("norm_mix_g", 8), ("q_norm_g", 3), ("kv_norm_g", 2), ("b_gate", 16), ("conv_w", 32),
            ("conv_b", 8), ("b_rg_a", 8), ("b_rg_x", 8), ("rg_lambda", 8), ("norm_ffn_g", 8)]
VEC_AT = {}
_n = 0
for _name, _rows in VEC_ROWS:
    VEC_AT[_name] = _n
    _n += _rows
NVEC = _n

CA = {}
_n = 0
for _name, _w in (("ident", 128), ("ones", 128), ("mask", 272), ("rot", 32), ("cos", T), ("sin", T)):
    CA[_name] = (_n, _n + _w)
    _n += _w
NCA = _n
CB = {}
_n = 0
for _name, _w in (("upper", 128), ("slot_id", 128), ("pick", NCOL), ("block_base", NCOL)):
    CB[_name] = (_n, _n + _w)
    _n += _w
NCB = _n


def constants():
    a = np.zeros((P, NCA), np.float32)
    a[:, slice(*CA["ident"])] = np.eye(P, dtype=np.float32)
    a[:, slice(*CA["ones"])] = 1.0
    q, k = np.arange(P)[:, None], np.arange(P)[None, :]
    a[:, CA["mask"][0] + 144:CA["mask"][1]] = np.where(k <= q, 0.0, MASKED)
    half = ROPE // 2
    rot = np.zeros((ROPE, ROPE), np.float32)
    for r in range(half):
        rot[r + half, r] = -1.0
        rot[r, r + half] = 1.0
    a[NOPE:QD, slice(*CA["rot"])] = rot
    inv = (np.float32(ROPE_BASE) ** (-np.arange(0, ROPE, 2, dtype=np.float32) / np.float32(ROPE))).astype(np.float32)
    ang = np.arange(T, dtype=np.float32)[:, None] * inv[None, :]
    a[NOPE:QD, slice(*CA["cos"])] = np.tile(np.cos(ang).astype(np.float32).T, (2, 1))
    a[NOPE:QD, slice(*CA["sin"])] = np.tile(np.sin(ang).astype(np.float32).T, (2, 1))
    b = np.zeros((P, NCB), np.float32)
    b[:, slice(*CB["upper"])] = np.triu(np.ones((P, P), np.float32), 1)
    b[:, slice(*CB["slot_id"])] = np.arange(P) % CAP
    n = np.arange(NCOL)
    b[:E, slice(*CB["pick"])] = (n[None, :] % E == np.arange(E)[:, None])
    b[:, slice(*CB["block_base"])] = CAP * (n // E)
    return a, b


def mixer_loads():
    loads = [("in", 0, 256), ("in", 256, 256), ("in", 512, 160), ("in", OFF_RX, 256), ("in", OFF_RG, 256),
             ("uq", 0, 384), ("uq", 384, 384), ("ukv", 0, 1024), ("gates", 0, 2)]
    for p in range(1, 4):
        loads += [("in", OFF_RX + 256 * p, 256), ("in", OFF_RG + 256 * p, 256), ("gates", 2 * p, 2)]
    for p in range(5):
        loads += [("in", OFF_GATE + D + 256 * p, 256)] if p < 4 else []
        loads += [("ro", 256 * (p - 1), 256)] if p else []
    for h in range(2):
        loads += [("in", OFF_GATE + 512 * h, 256), ("in", OFF_GATE + 512 * h + 256, 256), ("ao", 512 * h, 512)]
    loads += [("out", 2 * r, 2) for r in range(4)]
    return loads


LOADS = mixer_loads()
M0 = len(LOADS)


def layer(nc, x_in, meta_in, vec_in, ca_in, cb_in, w_in, w_uq, w_ukv, w_ao, w_rg_a, w_rg_x, w_ro, w_out,
          norm_ffn_g, w_router, b_router, w_up, b_up, w_down, b_down, norm_final_g, out):
    with ExitStack() as ctx:
        def sb(name, shape, dt=F32):
            return ctx.enter_context(nc.sbuf_tensor(name, shape, dt))

        def sem(name):
            return ctx.enter_context(nc.semaphore(name))

        ring = sb("ring", [P, SLOTS, SLOT])
        X = sb("X", [P, TT, D])
        ca = sb("ca", [P, NCA])
        vec = sb("vec", [P, NVEC])
        small = sb("small", [P, 160])
        WORK = 16800
        work = sb("work", [P, WORK])
        ps = ctx.enter_context(nc.psum_tensor("ps", [P, 8, 512], F32))

        at = [0]

        def view(n, start=None):
            a = at[0] if start is None else start
            if start is None:
                at[0] += n
            assert a + n <= WORK, (a, n)
            return work[:, a:a + n]

        xnT = view(KT * T).rearrange("p (k t) -> p k t", k=KT)
        qh = view(HEADS * SEQ).rearrange("p (h t) -> p h t", h=HEADS)
        kh = view(HEADS * T).rearrange("p (h t) -> p h t", h=HEADS)
        vtok = view(3 * 512).rearrange("p (k n) -> p k n", k=3)
        cq_at = at[0]
        cq = view(QT * SEQ).rearrange("p (k t) -> p k t", k=QT)
        ckv_at = at[0]
        ckv = view(KVT * T).rearrange("p (k t) -> p k t", k=KVT)
        oT = view(4 * SEQ).rearrange("p (k t) -> p k t", k=4)
        rg_at = at[0]
        rxp = view(2 * (T + 3)).rearrange("p (k t) -> p k t", k=2)
        xc = view(2 * T).rearrange("p (k t) -> p k t", k=2)
        tr = view(2 * T).rearrange("p (k t) -> p k t", k=2)
        ti = view(2 * T).rearrange("p (k t) -> p k t", k=2)
        av = view(2 * T).rearrange("p (k t) -> p k t", k=2)
        th = view(2 * T).rearrange("p (k t) -> p k t", k=2)
        xg = view(2 * SEQ).rearrange("p (k t) -> p k t", k=2)
        ug = view(2 * SEQ).rearrange("p (k t) -> p k t", k=2)
        gel_at = at[0]
        gel = view(KT * SEQ).rearrange("p (k t) -> p k t", k=KT)
        PT = view(2 * 384, cq_at).rearrange("p (b k q) -> p b k q", b=2, k=3)
        S = view(2 * T, ckv_at).rearrange("p (b t) -> p b t", b=2)
        xs = view(3 * D, rg_at).rearrange("p (k d) -> p k d", k=3)
        metab = view(D, rg_at + 3 * D)
        sqq = view(QT * SEQ, rg_at + 4 * D - 768).rearrange("p (k t) -> p k t", k=QT)
        sqk = view(KVT * T, cq_at + 1312).rearrange("p (k t) -> p k t", k=KVT)
        rq = view(SEQ, rg_at + 1100)
        rk = view(T, rg_at + 1100 + SEQ)
        ropeu = view(2 * SEQ, gel_at + 6 * SEQ).rearrange("p (k t) -> p k t", k=2)
        q_at = KT * T
        vec_rows = view(P, q_at)[0:NVEC, :]
        mT = view(KT * SEQ, rg_at).rearrange("p (k t) -> p k t", k=KT)
        ta = view(4 * SEQ, rg_at + 2 * (T + 3) + 10 * T).rearrange("p (k t) -> p k t", k=4)

        at[0] = 0
        xn2 = view(TT * D).rearrange("p (i d) -> p i d", i=TT)
        gfin = view(D)
        posm = view(TT * NCOL).rearrange("p (i n) -> p i n", i=TT)
        gate = view(TT * NCOL).rearrange("p (i n) -> p i n", i=TT)
        lg = view(TT * E).rearrange("p (i e) -> p i e", i=TT)
        selm = view(TT * E).rearrange("p (i e) -> p i e", i=TT)
        tmp = view(6 * E).rearrange("p (k e) -> p k e", k=6)
        assert at[0] <= q_at + HEADS * SEQ
        at[0] = q_at + HEADS * SEQ
        gffn = view(D)
        wr = view(KT * E).rearrange("p (k e) -> p k e", k=KT)
        brt = view(E)
        cb = view(NCB)
        bup = view(2 * F)
        assert at[0] <= ckv_at + KVT * T
        at[0] = ckv_at + KVT * T
        sel = view(2 * CAP).rearrange("p (b t) -> p b t", b=2)
        pick = view(TT * CAP).rearrange("p (i t) -> p i t", i=TT)
        gpick = view(TT * P).rearrange("p (i t) -> p i t", i=TT)
        gpickT = view(2 * TT * P).rearrange("p (b i t) -> p b i t", b=2, i=TT)
        xe = view(512)
        xeT = view(512).rearrange("p (j t) -> p j t", j=4)
        hg = view(512)
        hl = view(512)
        sg = view(512)
        act_h = view(512)
        actT = view(512).rearrange("p (j t) -> p j t", j=4)
        y = view(512)
        assert at[0] <= gel_at
        hT_at = gel_at
        hT = view(KT * SEQ, hT_at).rearrange("p (i k t) -> p i k t", i=TT, k=KT)
        sqx = xn2
        sqf = view(TT * D, hT_at).rearrange("p (i d) -> p i d", i=TT)
        flag_i = sb("flag_i", [1, 1], I32)

        ident = ca[:, slice(*CA["ident"])]
        ones = ca[:, slice(*CA["ones"])]
        maskc = ca[:, slice(*CA["mask"])]
        rotm = ca[NOPE:QD, slice(*CA["rot"])]
        cosT = ca[NOPE:QD, slice(*CA["cos"])]
        sinT = ca[NOPE:QD, slice(*CA["sin"])]
        upper = cb[:, slice(*CB["upper"])]
        slot_id = cb[:, slice(*CB["slot_id"])]
        pick_e = cb[:, slice(*CB["pick"])]
        block_base = cb[:, slice(*CB["block_base"])]

        def v(name, i):
            c = VEC_AT[name] + i
            return vec[:, c:c + 1]

        sm_n = [0]

        def col(n):
            a = sm_n[0]
            sm_n[0] += n
            assert sm_n[0] <= 160
            return small[:, a:a + n]

        hc2 = col(8)
        hc = col(8)
        nhc = col(8)
        hba = col(8)
        hbx = col(8)
        hbg = col(16)
        sp = col(32)
        dummy = col(1)
        ssx = col(3)
        rsx = col(3)
        mx = col(2)
        nmx = col(2)
        sm = col(2)
        rsm = col(2)
        ss2 = col(2)
        rs2 = col(2)
        top8 = col(16)
        nm1 = col(2)
        ngt = col(2)
        esum = col(2)
        cmax = col(2)
        ssf = col(2)
        ssh = col(4)
        rsf = col(2)

        slot_loaded = [sem(f"slot_loaded{s}") for s in range(SLOTS)]
        weights_used = sem("weights_used")
        const_in, ident_in, vec_in_s, x_in0, x_in1 = (
            sem(n) for n in ("const_in", "ident_in", "vec_in_s", "x_in0", "x_in1"))
        meta_in_s, moe_in, bdn_in, gfin_in = (
            sem(n) for n in ("meta_in_s", "moe_in", "bdn_in", "gfin_in"))
        dve_chain = sem("dve_chain")
        vecT_done, vec_read, vec_ready, softplus_in, sp_exp = (
            sem(n) for n in ("vecT_done", "vec_read", "vec_ready", "softplus_in", "sp_exp"))
        hc_ready, ssx_set, x0_sumsq, x0_var, x0_std = (
            sem(n) for n in ("hc_ready", "ssx_set", "x0_sumsq", "x0_var", "x0_std"))
        x0s_ready, x_sumsq, x_var, x_std, rsx_ready = (
            sem(n) for n in ("x0s_ready", "x_sumsq", "x_var", "x_std", "rsx_ready"))
        x1s_ready, ms_ready, xT_done, xT_read, xT_read_dve = (
            sem(n) for n in ("x1s_ready", "ms_ready", "xT_done", "xT_read", "xT_read_dve"))
        xs_read = sem("xs_read")
        proj_done, proj_read, lora_sq, lora_sum, lora_var = (
            sem(n) for n in ("proj_done", "proj_read", "lora_sq", "lora_sum", "lora_var"))
        lora_std, lora_ready, krot_done, qrot_done, rope_ready = (
            sem(n) for n in ("lora_std", "lora_ready", "krot_done", "qrot_done", "rope_ready"))
        scores_done, scores_read, rowmax_ready, exp_done, probs_ready = (
            sem(n) for n in ("scores_done", "scores_read", "rowmax_ready", "exp_done", "probs_ready"))
        probsT_done, probsT_ready, attn_done, attn_ready = (
            sem(n) for n in ("probsT_done", "probsT_ready", "attn_done", "attn_ready"))
        conv_ready, gelu_arg, gelu_tanh, gelu_free, lru_tanh = (
            sem(n) for n in ("conv_ready", "gelu_arg", "gelu_tanh", "gelu_free", "lru_tanh"))
        lru_arg, lru_sqrt, recurrence_done = (
            sem(n) for n in ("lru_arg", "lru_sqrt", "recurrence_done"))
        branch_done, branch_read, out_done, h_half, h_sumsq = (
            sem(n) for n in ("branch_done", "branch_read", "out_done", "h_half", "h_sumsq"))
        h_var, h_std, xn2_ready = (
            sem(n) for n in ("h_var", "h_std", "xn2_ready"))
        wr_ready, hT_done, hT_ready, hT_ready2, logits_done = (
            sem(n) for n in ("wr_ready", "hT_done", "hT_ready", "hT_ready2", "logits_done"))
        mask_ready, gexp_done, pos_done, pos_done_read, gate_ready = (
            sem(n) for n in ("mask_ready", "gexp_done", "pos_done", "pos_done_read", "gate_ready"))
        gateT_done, flag_ready, pick_ready, route_ready = (
            sem(n) for n in ("gateT_done", "flag_ready", "pick_ready", "route_ready"))
        y_zeroed, gather_done, xe_ready, xeT_done, xeT_ready = (
            sem(n) for n in ("y_zeroed", "gather_done", "xe_ready", "xeT_done", "xeT_ready"))
        gpickT_done, gpickT_ready, hidden_read, glu_ready, sig_done = (
            sem(n) for n in ("gpickT_done", "gpickT_ready", "hidden_read", "glu_ready", "sig_done"))
        lin_ready, act_ready, actT_done, actT_ready, y_ready = (
            sem(n) for n in ("lin_ready", "act_ready", "actT_done", "actT_ready", "y_ready"))
        scat_done, scat_added = (
            sem(n) for n in ("scat_done", "scat_added"))
        last_scat, last_added, f_sumsq, f_var, f_std = (
            sem(n) for n in ("last_scat", "last_added", "f_sumsq", "f_var", "f_std"))
        fin_ready, out_stored = (
            sem(n) for n in ("fin_ready", "out_stored"))

        block = ctx.enter_context(nc.Block())

        jobs = []
        jobs += [("cq", i) for i in range(QT)] + [("ckv", i) for i in range(KVT)] + [("kr", 0)]
        jobs += [("rx", 0), ("rx", 1), ("rg", 0), ("rg", 1)]
        jobs += [("q", h) for h in range(HEADS)] + [("k", g) for g in range(HEADS // 2)] + [("v", i) for i in range(3)]
        jobs += [("ra", 0), ("ra", 1), ("ri", 0), ("ri", 1)]
        for p in range(1, 4):
            for kinds in (("rx", "rg"), ("ra", "ri")):
                jobs += [(kind, i) for kind in kinds for i in (2 * p, 2 * p + 1)]
        jobs += [("gr", i) for i in range(8)] + [("ga", i) for i in range(8)]
        JOB = {job: n for n, job in enumerate(jobs)}

        UNITS = [(h, b) for h in range(HEADS) for b in range(TT)]
        NU = len(UNITS)
        step_after = {}
        hosts = [host for p in range(1, 4)
                 for host in (("rx", 2 * p), ("rx", 2 * p + 1), ("rg", 2 * p), ("ri", 2 * p + 1))]
        hosts = hosts[2:] + [("gr", i) for i in range(KT)]
        for s in range(NU + 2):
            step_after[hosts[s]] = s

        def nk(b):
            return N_META + P * (b + 1)

        def ktiles(b):
            return [(t, min(P, nk(b) - P * t)) for t in range(3) if nk(b) > P * t]

        @block.sync
        def _(spe):
            for k in range(3):
                src = x_in[0, P * k:P * k + P, :] if k < 2 else meta_in[:, :]
                if k < 2:
                    spe.dma_start(X[:, k, :], src).then_inc((x_in0, x_in1)[k], 16)
                else:
                    spe.dma_start(metab[0:N_META, :], src).then_inc(meta_in_s, 16)
            kview = w_in[0].rearrange("(k p) n -> p k n", p=P)
            for n, (kind, a, w) in enumerate(LOADS):
                s = n % SLOTS
                if n >= SLOTS:
                    spe.wait_ge(weights_used, n - SLOTS + 1)
                if kind == "in":
                    parts = [(KT * w, kview[:, :, a:a + w], KT)]
                elif kind == "ro":
                    parts = [(KT * w, w_ro[0].rearrange("(k p) n -> p k n", p=P)[:, :, a:a + w], KT)]
                elif kind == "uq":
                    parts = [(QT * w, w_uq[0].rearrange("(k p) n -> p k n", p=P)[:, :, a:a + w], QT)]
                elif kind == "ukv":
                    parts = [(KVT * w, w_ukv[0].rearrange("(k p) n -> p k n", p=P), KVT)]
                elif kind == "ao":
                    parts = [(4 * w, w_ao[0].rearrange("(k p) n -> p k n", p=P)[:, :, a:a + w], 4)]
                elif kind == "out":
                    parts = [(2 * D, w_out[0].rearrange("(k p) n -> p k n", p=P)[:, a:a + w, :], 2)]
                else:
                    parts = [(2 * P, w_rg_a[0].rearrange("b i j -> i b j")[:, a:a + w, :], 2),
                             (2 * P, w_rg_x[0].rearrange("b i j -> i b j")[:, a:a + w, :], 2)]
                o = 0
                for width, src, k in parts:
                    spe.dma_start(ring[:, s, o:o + width].rearrange("p (k n) -> p k n", k=k), src)\
                       .then_inc(slot_loaded[s], 16)
                    o += width

            def expert_loads(it, i):
                for u in range(UNROLL):
                    for c in range(PER_EXPERT):
                        m = u * PER_EXPERT + c
                        s = (M0 + m) % SLOTS
                        spe.wait_ge(weights_used, it * (UNROLL * PER_EXPERT) + (M0 + m - SLOTS + 1))
                        if c < KT:
                            src = w_up[0, i * UNROLL + u, P * c:P * c + P, :]
                            dst = ring[:, s, :]
                        else:
                            r = 2 * P * (c - KT)
                            src = w_down[0, i * UNROLL + u, r:r + 2 * P, :].rearrange("(k p) n -> p k n", p=P)
                            dst = ring[:, s, :].rearrange("p (k n) -> p k n", k=2)
                        spe.dma_start(dst, src).then_inc(slot_loaded[s], 16)

            with spe.Fori(0, GROUPS) as it:
                expert_loads(it, it)
            spe.wait_ge(flag_ready, 1)
            over = spe.value_load(flag_i[0:1, 0:1], min_val=0, max_val=1)
            with spe.If(over > 0):
                with spe.Fori(1, BLOCKS) as j:
                    with spe.Fori(0, GROUPS) as i:
                        expert_loads(j * GROUPS + i, i)
            for i in range(TT):
                spe.wait_ge(fin_ready, i + 1)
                spe.dma_start(out[0, P * i:P * i + P, :], X[:, i, :]).then_inc(out_stored, 16)
            spe.wait_ge(out_stored, 16 * TT)

        @block.gpsimd
        def _(pool):
            pool.wait_ge(attn_ready, NU)
            pool.dma_start(gffn, norm_ffn_g[0:1, :].broadcast_to([P, D])).then_inc(moe_in, 16)
            pool.dma_start(wr, w_router[0].rearrange("(k p) e -> p k e", p=P)).then_inc(moe_in, 16)
            pool.dma_start(brt, b_router[0:1, :].broadcast_to([P, E])).then_inc(moe_in, 16)
            pool.dma_start(cb, cb_in[:, :]).then_inc(moe_in, 16)
            pool.dma_start(bup[0:E, :], b_up[0]).then_inc(moe_in, 16)
            pool.wait_ge(y_zeroed, 1)
            for c in range(2):
                pool.dma_start(y[CAP * c:CAP * c + E, :], b_down[0, :, 512 * c:512 * c + 512]).then_inc(bdn_in, 16)
            pool.wait_ge(h_half, 2 * TT)
            pool.dma_start(gfin, norm_final_g.rearrange("(a d) -> a d", a=1).broadcast_to([P, D])).then_inc(gfin_in, 16)

        @block.tensor
        def _(pe):
            owed = [0]

            def settle(ins):
                if owed[0]:
                    ins.then_inc(weights_used, owed[0])
                    owed[0] = 0

            def slot_of(n):
                return n % SLOTS

            def wait_load(n):
                s = slot_of(n)
                total = sum(32 if LOADS[m][0] == "gates" else 16 for m in range(s, n + 1, SLOTS))
                pe.wait_ge(slot_loaded[s], total)

            def wslot(n, k):
                return ring[:, slot_of(n), :].rearrange("p (k n) -> p k n", k=k)

            load_at = {}
            for n, (kind, a, w) in enumerate(LOADS):
                load_at[(kind, a)] = n

            def begin(job):
                n = JOB[job]
                if n >= 3:
                    pe.wait_ge(proj_read, n - 2)
                return n % 3

            def in_cols(c):
                for (kind, a), n in load_at.items():
                    if kind == "in" and a <= c < a + LOADS[n][2]:
                        return n, c - a, LOADS[n][2]

            def project(job, c, width, lo, hi, part=0, last=False):
                n, o, w = in_cols(c)
                wait_load(n)
                b = begin(job)
                wv = ring[:, slot_of(n), 0:KT * w].rearrange("p (k n) -> p k n", k=KT)
                for k in range(KT):
                    ins = nc.tensor.matmul(ps[part:part + width, b, 0:hi - lo], wv[:, k, o:o + width],
                                           xnT[:, k, lo:hi], start=(k == 0), stop=(k == KT - 1))
                    if k == 0:
                        settle(ins)
                ins.then_inc(proj_done, 1)
                if last:
                    owed[0] += 1

            pe.wait_ge(vec_in_s, 16)
            pe.wait_ge(ident_in, 16)
            nc.tensor.transpose(ps[:, 7, 0:NVEC], vec_rows, ident[0:NVEC, 0:NVEC]).then_inc(vecT_done, 1)

            for t in range(3):
                pe.wait_ge((x0s_ready, x1s_ready, ms_ready)[t], 1)
                for i in range(KT):
                    c = slice(P * i, P * i + P)
                    if t == 0 and i == 7:
                        pe.wait_ge(vec_read, 1)
                    if t < 2:
                        nc.tensor.transpose(ps[:, i, N_META + P * t:N_META + P * t + P], xs[:, t, c], ident)
                    else:
                        nc.tensor.transpose(ps[:, i, 0:N_META], xs[0:N_META, 2, c], ident[0:N_META, 0:N_META])\
                          .then_inc(xT_done, 1)
            pe.wait_ge(xT_read, KT // 2)
            pe.wait_ge(xT_read_dve, KT // 2)

            for i in range(QT):
                project(("cq", i), OFF_CQ + P * i, P, N_META, T, last=(i == 1))
            for i in range(KVT):
                project(("ckv", i), OFF_CKV + P * i, P, 0, T, last=(i == 0))
            project(("kr", 0), OFF_KR, ROPE, 0, T, part=NOPE, last=True)
            project(("rx", 0), OFF_RX, P, 0, T)
            project(("rx", 1), OFF_RX + P, P, 0, T, last=True)

            pe.wait_ge(const_in, 16)
            pe.wait_ge(lora_sq, 2)
            for k in range(QT):
                ins = nc.tensor.matmul(ps[:, 4, 0:SEQ], ones, sqq[:, k, :], start=(k == 0), stop=(k == QT - 1))
            ins.then_inc(lora_sum, 1)
            for k in range(KVT):
                ins = nc.tensor.matmul(ps[:, 5, 0:T], ones, sqk[:, k, :], start=(k == 0), stop=(k == KVT - 1))
            ins.then_inc(lora_sum, 1)
            pe.wait_ge(proj_read, JOB[("kr", 0)] + 1)
            nc.tensor.matmul(ps[NOPE:QD, 6, 0:T], rotm, kh[NOPE:QD, 0, :], start=True, stop=True).then_inc(krot_done, 1)
            project(("rg", 0), OFF_RG, P, N_META, T)
            project(("rg", 1), OFF_RG + P, P, N_META, T, last=True)

            pe.wait_ge(lora_ready, 1)
            for h in range(HEADS):
                n = load_at[("uq", 384 * (h // 4))]
                wait_load(n)
                b = begin(("q", h))
                wv = ring[:, slot_of(n), 0:QT * 384].rearrange("p (k n) -> p k n", k=QT)
                for k in range(QT):
                    ins = nc.tensor.matmul(ps[0:QD, b, 0:SEQ], wv[:, k, QD * (h % 4):QD * (h % 4) + QD], cq[:, k, :],
                                           start=(k == 0), stop=(k == QT - 1))
                    if k == 0:
                        settle(ins)
                ins.then_inc(proj_done, 1)
                if h % 4 == 3:
                    owed[0] += 1
            pe.wait_ge(lora_ready, 2)
            n = load_at[("ukv", 0)]
            wait_load(n)
            wv = wslot(n, KVT)
            for g in range(HEADS // 2):
                b = begin(("k", g))
                for k in range(KVT):
                    for c in range(2):
                        h = 2 * g + c
                        ins = nc.tensor.matmul(ps[NOPE * c:NOPE * c + NOPE, b, 0:T], wv[:, k, P * h:P * h + NOPE],
                                               ckv[:, k, :], start=(k == 0), stop=(k == KVT - 1))
                    if k == 0:
                        settle(ins)
                ins.then_inc(proj_done, 1)
                if g >= 2:
                    if g == 2:
                        pe.wait_ge(proj_read, JOB[("q", HEADS - 1)] + 1)
                        pe.wait_ge(rope_ready, 1)
                        pe.wait_ge(lora_var, 2)
                    for r in (2 * g - 4, 2 * g - 3):
                        nc.tensor.matmul(ps[NOPE:QD, 4 + r, :].rearrange("p (h t) -> p h t", h=2), rotm,
                                         qh[NOPE:QD, 2 * r:2 * r + 2, :], start=True, stop=True).then_inc(qrot_done, 1)
            for t in range(3):
                b = begin(("v", t))
                m = min(P, T - P * t)
                for k in range(KVT):
                    ins = nc.tensor.matmul(ps[0:m, b, :].rearrange("p (h d) -> p h d", h=HEADS),
                                           ckv[:, k, P * t:P * t + m],
                                           wv[:, k, :].rearrange("p (h d) -> p h d", h=HEADS)[:, :, NOPE:P],
                                           start=(k == 0), stop=(k == KVT - 1))
                ins.then_inc(proj_done, 1)
            owed[0] += 1

            def attention_step(s):
                if s < NU:
                    h, b = UNITS[s]
                    if s == 0:
                        pe.wait_ge(rope_ready, 5)
                        pe.wait_ge(proj_read, JOB[("v", 2)] + 1)
                    if s >= 2:
                        pe.wait_ge(scores_read, s - 1)
                    nc.tensor.matmul(ps[:, 4 + s % 2, 0:nk(b)], qh[0:QD, h, P * b:P * b + P], kh[0:QD, h, 0:nk(b)],
                                     start=True, stop=True).then_inc(scores_done, 1)
                if s >= 2:
                    r = s - 2
                    h, b = UNITS[r]
                    pe.wait_ge(probsT_ready, r + 1)
                    if r >= 1:
                        pe.wait_ge(attn_ready, r)
                    o = VD * (h % 2)
                    kts = ktiles(b)
                    for t, m in kts:
                        ins = nc.tensor.matmul(ps[o:o + VD, 6, 3 * P:4 * P], vtok[0:m, t, VD * h:VD * h + VD],
                                               PT[0:m, r % 2, t, :], start=(t == 0), stop=(t == kts[-1][0]))
                    ins.then_inc(attn_done, 1)
                if 1 <= s <= NU:
                    r = s - 1
                    b = UNITS[r][1]
                    pe.wait_ge(probs_ready, r + 1)
                    for t, m in ktiles(b):
                        ins = nc.tensor.transpose(ps[0:m, 6, P * t:P * t + P], S[:, r % 2, P * t:P * t + m], ident)
                    ins.then_inc(probsT_done, 1)

            def lru_gates(p):
                n = load_at[("gates", 2 * p)]
                wait_load(n)
                wv = ring[:, slot_of(n), 0:4 * P].rearrange("p (g k n) -> p g k n", g=2, k=2)
                for g, name in ((0, "ra"), (1, "ri")):
                    for k in range(2):
                        i = 2 * p + k
                        b = begin((name, i))
                        pe.wait_ge(conv_ready, i + 1)
                        ins = nc.tensor.matmul(ps[:, b, 0:T], wv[:, g, k, :], xc[:, k, :], start=True, stop=True)
                        ins.then_inc(proj_done, 1)
                        if g == 1 and k == 1:
                            owed[0] += 1
                        if (name, i) in step_after:
                            attention_step(step_after[(name, i)])

            lru_gates(0)
            for p in range(1, 4):
                for name, off, lo in (("rx", OFF_RX, 0), ("rg", OFF_RG, N_META)):
                    for k in range(2):
                        i = 2 * p + k
                        project((name, i), off + P * i, P, lo, T, last=(k == 1))
                        if (name, i) in step_after:
                            attention_step(step_after[(name, i)])
                lru_gates(p)

            n_out = [0]

            def branch_begin():
                d = n_out[0]
                n_out[0] += 1
                if d >= 2:
                    pe.wait_ge(branch_read, d - 1)
                return (3, 7)[d % 2]

            def recurrent_output(p):
                n = load_at[("ro", 256 * p)]
                wait_load(n)
                wv = wslot(n, KT)
                if p == 0:
                    pe.wait_ge(recurrence_done, 4)
                for i in range(2):
                    b = branch_begin()
                    for k in range(KT):
                        ins = nc.tensor.matmul(ps[:, b, 0:SEQ], wv[:, k, P * i:P * i + P], gel[:, k, :],
                                               start=(k == 0), stop=(k == KT - 1))
                        if k == 0:
                            settle(ins)
                    ins.then_inc(branch_done, 1)
                owed[0] += 1

            for p in range(4):
                for i in (2 * p, 2 * p + 1):
                    project(("gr", i), OFF_GATE + D + P * i, P, N_META, T, last=(i % 2 == 1))
                    attention_step(step_after[("gr", i)])
                if p > 0:
                    recurrent_output(p - 1)
            recurrent_output(3)
            for g in range(2):
                for i in range(4 * g, 4 * g + 4):
                    project(("ga", i), OFF_GATE + P * i, P, N_META, T, last=(i % 2 == 1))
                n = load_at[("ao", 512 * g)]
                wait_load(n)
                wv = wslot(n, 4)
                pe.wait_ge(attn_ready, NU)
                for i in range(4):
                    b = branch_begin()
                    for k in range(4):
                        ins = nc.tensor.matmul(ps[:, b, 0:SEQ], wv[:, k, P * i:P * i + P], oT[:, k, :],
                                               start=(k == 0), stop=(k == 3))
                        if k == 0:
                            settle(ins)
                    ins.then_inc(branch_done, 1)
                owed[0] += 1

            def turn_h(i):
                for k in range(KT):
                    if k % 4 == 0:
                        pe.wait_ge(h_half, 2 * i + k // 4 + 1)
                    ins = nc.tensor.transpose(ps[:, 4 + 2 * i + k // 4, P * (k % 4):P * (k % 4) + P],
                                              X[:, i, P * k:P * k + P], ident)
                    if k % 4 == 3:
                        ins.then_inc(hT_done, 1)

            def router(i):
                pe.wait_ge(hT_ready, i + 1)
                for k in range(KT):
                    if k == 4:
                        pe.wait_ge(hT_ready2, i + 1)
                    ins = nc.tensor.matmul(ps[:, i, 0:E], hT[:, i, k, :], wr[:, k, :], start=(k == 0), stop=(k == KT - 1))
                ins.then_inc(logits_done, 1)

            pe.wait_ge(proj_read, len(jobs))
            pe.wait_ge(branch_read, 15)
            for i in range(TT):
                for r in range(4):
                    n = load_at[("out", 2 * r)]
                    if i == 0:
                        wait_load(n)
                        if r == 3:
                            pe.wait_ge(branch_read, 16)
                    wv = wslot(n, 2)
                    for k in range(2):
                        for c in range(2):
                            ins = nc.tensor.matmul(ps[:, 2 * i + c, :], mT[:, 2 * r + k, P * i:P * i + P],
                                                   wv[:, k, 512 * c:512 * c + 512],
                                                   start=(r == 0 and k == 0), stop=(r == 3 and k == 1))
                            if i == 0 and k == 0 and c == 0:
                                settle(ins)
                    if i == 1:
                        ins.then_inc(weights_used, 1)
                        if r == 2:
                            turn_h(0)
                if i == 0:
                    ins.then_inc(out_done, 1)
            pe.wait_ge(wr_ready, 1)
            router(0)
            turn_h(1)
            router(1)

            pe.wait_ge(mask_ready, 1)
            nc.tensor.matmul(ps[:, 2, 0:E], upper, selm[:, 0, :], start=True, stop=True)
            nc.tensor.matmul(ps[:, 2, E:2 * E], ones, selm[:, 0, :], start=True, stop=False, skip_group_check=True)
            nc.tensor.matmul(ps[:, 2, E:2 * E], upper, selm[:, 1, :], start=False, stop=True, skip_group_check=True)\
              .then_inc(pos_done, 1)
            nc.tensor.matmul(ps[:, 3, 0:E], ones, selm[:, 0, :], start=True, stop=False)
            nc.tensor.matmul(ps[:, 3, 0:E], ones, selm[:, 1, :], start=False, stop=True).then_inc(pos_done, 1)

            def gather():
                for c in range(2):
                    for i in range(TT):
                        ins = nc.tensor.matmul(ps[CAP * c:CAP * c + CAP, 2, :], pick[:, i, :],
                                               xn2[:, i, 512 * c:512 * c + 512], start=(i == 0), stop=(i == TT - 1))
                ins.then_inc(gather_done, 1)

            def turn_route():
                for i in range(TT):
                    ins = nc.tensor.transpose(ps[:, 5, P * i:P * i + P], gpick[:, i, :], ident)
                ins.then_inc(gpickT_done, 1)

            def turn_gathered():
                for j in range(4):
                    ins = nc.tensor.transpose(ps[:, 3, P * j:P * j + P], xe[:, P * j:P * j + P], ident)
                ins.then_inc(xeT_done, 1)

            def scatter(u, i, it):
                pe.wait_ge(scat_added, (it * UNROLL + u) * TT + (i + 1))
                for c in range(2):
                    ins = nc.tensor.matmul(ps[:, 6 + c, :], gpickT[CAP * c:CAP * c + CAP, (u + 1) % 2, i, :],
                                           y[CAP * c:CAP * c + CAP, :], start=True, stop=True)
                ins.then_inc(scat_done, 1)

            pe.wait_ge(xn2_ready, TT)
            pe.wait_ge(pick_ready, 1)
            gather()
            pe.wait_ge(gate_ready, 1)
            for i in range(TT):
                ins = nc.tensor.transpose(ps[:, 4, P * i:P * i + P], gate[:, i, 0:P], ident)
            ins.then_inc(gateT_done, 1)
            pe.wait_ge(xe_ready, 1)
            pe.wait_ge(pos_done_read, 1)
            turn_gathered()
            pe.wait_ge(route_ready, 1)
            turn_route()
            pe.wait_ge(bdn_in, 32)

            def experts(it):
                for u in range(UNROLL):
                    n = it * UNROLL + u
                    w0 = u * PER_EXPERT
                    def loaded(m):
                        s = (M0 + m) % SLOTS
                        before = sum(32 if LOADS[q][0] == "gates" else 16 for q in range(s, M0, SLOTS))
                        pe.wait_ge(slot_loaded[s], it * (16 * UNROLL * PER_EXPERT // SLOTS) + (before + 16 * (m // SLOTS + 1)))
                        return s
                    pe.wait_ge(hidden_read, n + 1)
                    for q in range(4):
                        c, b = q % 2, q // 2
                        nc.tensor.matmul(ps[CAP * c:CAP * c + CAP, b, :], sel[0:E, u % 2, :],
                                         bup[0:E, 512 * q:512 * q + 512], start=True, stop=False)
                    pe.wait_ge(xeT_ready, n + 1)
                    for k in range(KT):
                        s = loaded(w0 + k)
                        g, j = k // 4, k % 4
                        for q in range(4):
                            c, b = q % 2, q // 2
                            ins = nc.tensor.matmul(ps[CAP * c:CAP * c + CAP, b, :], xeT[:, j, CAP * g:CAP * g + CAP],
                                                   ring[:, s, 512 * q:512 * q + 512], start=False, stop=(k == KT - 1))
                        ins.then_inc(weights_used, 1)
                        if k == 1:
                            pe.wait_ge(y_ready, n + 1)
                            scatter(u, 0, it)
                        if k == 4:
                            scatter(u, 1, it)
                    pe.wait_ge(route_ready, n + 2)
                    pe.wait_ge(xe_ready, n + 1)
                    gather()
                    pe.wait_ge(gpickT_ready, n + 1)
                    turn_route()
                    pe.wait_ge(act_ready, n + 1)
                    for j in range(4):
                        ins = nc.tensor.transpose(ps[:, 4, P * j:P * j + P], act_h[:, P * j:P * j + P], ident)
                    ins.then_inc(actT_done, 1)
                    pe.wait_ge(xe_ready, n + 2)
                    turn_gathered()
                    pe.wait_ge(actT_ready, n + 1)
                    pe.wait_ge(gpickT_ready, n + 2)
                    for t in range(4):
                        s = loaded(w0 + KT + t)
                        wv = ring[:, s, :].rearrange("p (k n) -> p k n", k=2)
                        for k in range(2):
                            f = 2 * t + k
                            g, j = f // 4, f % 4
                            for c in range(2):
                                ins = nc.tensor.matmul(ps[CAP * c:CAP * c + CAP, 5, :], actT[:, j, CAP * g:CAP * g + CAP],
                                                       wv[:, k, 512 * c:512 * c + 512], start=(f == 0), stop=(f == 7))
                        ins.then_inc(weights_used, 1)

            pe.wait_ge(flag_ready, 1)
            over = pe.value_load(flag_i[0:1, 0:1], min_val=0, max_val=1)
            with pe.Fori(0, GROUPS) as it:
                experts(it)
            with pe.If(over > 0):
                with pe.Fori(1, BLOCKS) as j:
                    with pe.Fori(0, GROUPS) as i:
                        experts(j * GROUPS + i)
                pe.wait_ge(y_ready, BLOCKS * E + 1)
                pe.wait_ge(scat_added, TT * BLOCKS * E + 1)
            pe.wait_ge(y_ready, E + 1)
            pe.wait_ge(scat_added, TT * E + 1)
            for i in range(TT):
                for c in range(2):
                    nc.tensor.matmul(ps[:, (6 if i == 0 else 0) + c, :], gpickT[CAP * c:CAP * c + CAP, 1, i, :],
                                     y[CAP * c:CAP * c + CAP, :], start=True, stop=True).then_inc(last_scat, 1)

        @block.scalar
        def _(act):
            act.dma_start(vec_rows, vec_in[:, :]).then_inc(vec_in_s, 16)
            act.dma_start(ca[:, 0:P], ca_in[:, 0:P]).then_inc(ident_in, 16)
            act.dma_start(ca[:, P:], ca_in[:, P:]).then_inc(const_in, 16)
            act.wait_ge(ssx_set, 1)
            nc.scalar.activation(dummy, dummy, ACT.Sqrt)
            act.wait_ge(x_in0, 16)
            nc.scalar.activation(xs[:, 0, :], X[:, 0, :], ACT.Square, accum_out=ssx[:, 0:1]).then_inc(x0_sumsq, 1)
            act.wait_ge(x0_var, 1)
            nc.scalar.activation(rsx[:, 0:1], ssx[:, 0:1], ACT.Sqrt).then_inc(x0_std, 1)
            act.wait_ge(x_in1, 16)
            nc.scalar.activation(xs[:, 1, :], X[:, 1, :], ACT.Square, accum_out=ssx[:, 1:2]).then_inc(x_sumsq, 1)
            act.wait_ge(x_var, 1)
            nc.scalar.activation(rsx[:, 1:2], ssx[:, 1:2], ACT.Sqrt).then_inc(x_std, 1)
            act.wait_ge(meta_in_s, 16)
            nc.scalar.activation(xs[0:N_META, 2, :], metab[0:N_META, :], ACT.Square,
                                 accum_out=ssx[0:N_META, 2:3]).then_inc(x_sumsq, 1)
            act.wait_ge(x_var, 2)
            nc.scalar.activation(rsx[:, 2:3], ssx[:, 2:3], ACT.Sqrt).then_inc(x_std, 1)
            act.wait_ge(rsx_ready, 1)
            nc.scalar.activation(xs[0:N_META, 2, :], metab[0:N_META, :], ACT.Copy, scale=rsx[0:N_META, 2:3])\
              .then_inc(ms_ready, 1)
            act.wait_ge(vec_ready, 1)
            for i in range(0, KT, 2):
                act.wait_ge(xT_done, i + 1)
                nc.scalar.activation(xnT[:, i, :], ps[:, i, 0:T], ACT.Copy, scale=v("norm_mix_g", i)).then_inc(xT_read, 1)
            act.wait_ge(softplus_in, 1)
            nc.scalar.activation(sp[:, 0:8], sp[:, 0:8], ACT.Exp, scale=-1.0).then_inc(sp_exp, 1)

            def read(job):
                n = JOB[job]
                kind, i = job
                b = n % 3
                act.wait_ge(proj_done, n + 1)
                if kind == "cq":
                    ins = nc.scalar.activation(cq[:, i, :], ps[:, b, 0:SEQ], ACT.Copy)
                elif kind == "ckv":
                    ins = nc.scalar.activation(ckv[:, i, :], ps[:, b, 0:T], ACT.Copy)
                elif kind == "kr":
                    ins = nc.scalar.activation(kh[NOPE:QD, 0, :], ps[NOPE:QD, b, 0:T], ACT.Copy)
                elif kind == "rx":
                    if i == 0:
                        act.wait_ge(xs_read, 1)
                    if i >= 2:
                        act.wait_ge(conv_ready, i - 1)
                    ins = nc.scalar.activation(rxp[:, i % 2, CONV - 1:], ps[:, b, 0:T], ACT.Copy)
                elif kind == "q":
                    ins = nc.scalar.activation(qh[0:QD, i, :], ps[0:QD, b, 0:SEQ], ACT.Copy)
                elif kind == "k":
                    nc.scalar.activation(kh[0:NOPE, 2 * i, :], ps[0:NOPE, b, 0:T], ACT.Copy)
                    ins = nc.scalar.activation(kh[0:NOPE, 2 * i + 1, :], ps[NOPE:P, b, 0:T], ACT.Copy)
                elif kind == "v":
                    m = min(P, T - P * i)
                    ins = nc.scalar.activation(vtok[0:m, i, :], ps[0:m, b, :], ACT.Copy)
                elif kind == "rg":
                    if i >= 2:
                        act.wait_ge(gelu_free, i // 2)
                    nc.scalar.activation(ug[:, i % 2, :], ps[:, b, 0:SEQ], ACT.Square)
                    ins = nc.scalar.activation(xg[:, i % 2, :], ps[:, b, 0:SEQ], ACT.Copy)
                elif kind == "ra":
                    if i >= 2:
                        act.wait_ge(recurrence_done, i // 2)
                    ins = nc.scalar.activation(tr[:, i % 2, :], ps[:, b, 0:T], ACT.Tanh, bias=hba[:, i:i + 1], scale=0.5)
                elif kind == "ri":
                    ins = nc.scalar.activation(ti[:, i % 2, :], ps[:, b, 0:T], ACT.Tanh, bias=hbx[:, i:i + 1], scale=0.5)
                elif kind == "gr":
                    if i == 0:
                        act.wait_ge(gelu_free, 4)
                    if i >= 4:
                        act.wait_ge(branch_read, i - 3)
                    ins = nc.scalar.activation(ta[:, i % 4, :], ps[:, b, 0:SEQ], ACT.Tanh, bias=hbg[:, 8 + i:9 + i], scale=0.5)
                else:
                    act.wait_ge(branch_read, 4 + i + 1)
                    ins = nc.scalar.activation(ta[:, i % 4, :], ps[:, b, 0:SEQ], ACT.Tanh, bias=hbg[:, i:i + 1], scale=0.5)
                ins.then_inc(proj_read, 1)

            def attention_read(s):
                if 1 <= s <= NU:
                    r = s - 1
                    kts = ktiles(UNITS[r][1])
                    act.wait_ge(probsT_done, r + 1)
                    full = len(kts) - 1
                    nc.scalar.activation(PT[:, r % 2, 0:full, :],
                                         ps[:, 6, 0:P * full].rearrange("p (k q) -> p k q", k=full), ACT.Copy)
                    t, m = kts[-1]
                    nc.scalar.activation(PT[0:m, r % 2, t, :], ps[0:m, 6, P * t:P * t + P], ACT.Copy)\
                      .then_inc(probsT_ready, 1)
                if s >= 2:
                    r = s - 2
                    h, b = UNITS[r]
                    o = VD * (h % 2)
                    act.wait_ge(attn_done, r + 1)
                    nc.scalar.activation(oT[o:o + VD, h // 2, P * b:P * b + P], ps[o:o + VD, 6, 3 * P:4 * P], ACT.Copy)\
                      .then_inc(attn_ready, 1)

            def attention_exp(s):
                if s >= NU:
                    return
                b = UNITS[s][1]
                act.wait_ge(rowmax_ready, s + 1)
                nc.scalar.activation(S[:, s % 2, 0:nk(b)], S[:, s % 2, 0:nk(b)], ACT.Exp, bias=nmx[:, s % 2:s % 2 + 1],
                                     accum_out=sm[:, s % 2:s % 2 + 1]).then_inc(exp_done, 1)

            def gelu(p):
                act.wait_ge(gelu_arg, p + 1)
                nc.scalar.activation(ug, ug, ACT.Tanh, scale=GELU_C).then_inc(gelu_tanh, 1)

            def decay(p):
                if p == 0:
                    act.wait_ge(hc_ready, 1)
                act.wait_ge(proj_read, JOB[("ra", 2 * p + 1)] + 1)
                for k in range(2):
                    i = 2 * p + k
                    nc.scalar.activation(av[:, k, :], tr[:, k, :], ACT.Exp, bias=hc[:, i:i + 1], scale=hc[:, i:i + 1])
                    nc.scalar.activation(th[:, k, :], tr[:, k, :], ACT.Tanh, bias=nhc[:, i:i + 1],
                                         scale=nhc[:, i:i + 1])
                    ins = nc.scalar.activation(tr[:, k, :], tr[:, k, :], ACT.Exp, bias=hc2[:, i:i + 1],
                                               scale=hc2[:, i:i + 1])
                ins.then_inc(lru_tanh, 1)

            def input_scale(p):
                act.wait_ge(lru_arg, p + 1)
                nc.scalar.activation(th, th, ACT.Sqrt, scale=0.25).then_inc(lru_sqrt, 1)

            for job in jobs:
                read(job)
                if job == ("rx", 1):
                    act.wait_ge(lora_var, 2)
                    nc.scalar.activation(rq, rq, ACT.Sqrt).then_inc(lora_std, 1)
                    nc.scalar.activation(rk, rk, ACT.Sqrt).then_inc(lora_std, 1)
                if job == ("k", 0):
                    gelu(0)
                if job in step_after:
                    attention_read(step_after[job])
                    attention_exp(step_after[job])
                if job[0] == "ri" and job[1] % 2 == 1:
                    decay(job[1] // 2)
                    if job[1] > 1:
                        gelu(job[1] // 2)
                if (job[0] == "rx" and job[1] % 2 == 0 and job[1] > 1) or job == ("gr", 0):
                    input_scale(3 if job[0] == "gr" else job[1] // 2 - 1)

            for i in range(TT):
                act.wait_ge(h_half, 2 * i + 2)
                if i == 0:
                    nc.scalar.activation(sqx[:, i, :], X[:, i, :], ACT.Square, accum_out=ss2[:, i:i + 1])\
                      .then_inc(h_sumsq, 1)
                act.wait_ge(hT_done, 2 * i + 1)
                nc.scalar.activation(hT[:, i, 0:4, :], ps[:, 4 + 2 * i, :].rearrange("p (k t) -> p k t", k=4),
                                     ACT.Copy).then_inc(hT_ready, 1)
                if i == 1:
                    nc.scalar.activation(sqx[:, i, :], X[:, i, :], ACT.Square, accum_out=ss2[:, i:i + 1])\
                      .then_inc(h_sumsq, 1)
                act.wait_ge(h_var, i + 1)
                nc.scalar.activation(rs2[:, i:i + 1], ss2[:, i:i + 1], ACT.Sqrt).then_inc(h_std, 1)

            act.wait_ge(mask_ready, 1)
            for i in range(TT):
                nc.scalar.activation(lg[:, i, :], lg[:, i, :], ACT.Exp, bias=nm1[:, i:i + 1]).then_inc(gexp_done, 1)

            act.wait_ge(gather_done, 1)
            nc.scalar.activation(xe, ps[:, 2, :], ACT.Copy).then_inc(xe_ready, 1)
            act.wait_ge(gateT_done, 1)
            nc.scalar.activation(gpickT[:, 1, :, :], ps[:, 4, 0:SEQ].rearrange("p (i t) -> p i t", i=TT),
                                 ACT.Copy).then_inc(y_ready, 1)
            act.wait_ge(gpickT_done, 1)
            nc.scalar.activation(gpickT[:, 0, :, :], ps[:, 5, 0:SEQ].rearrange("p (i t) -> p i t", i=TT),
                                 ACT.Copy).then_inc(gpickT_ready, 1)

            def experts(it):
                for u in range(UNROLL):
                    n = it * UNROLL + u
                    act.wait_ge(glu_ready, n + 1)
                    nc.scalar.activation(sg, hg, ACT.Sigmoid, scale=ALPHA).then_inc(sig_done, 1)
                    act.wait_ge(gather_done, n + 2)
                    act.wait_ge(xeT_done, n + 1)
                    nc.scalar.activation(xe, ps[:, 2, :], ACT.Copy).then_inc(xe_ready, 1)
                    act.wait_ge(gpickT_done, n + 2)
                    nc.scalar.activation(gpickT[:, (u + 1) % 2, :, :], ps[:, 5, 0:SEQ].rearrange("p (i t) -> p i t", i=TT),
                                         ACT.Copy).then_inc(gpickT_ready, 1)
                    act.wait_ge(actT_done, n + 1)
                    nc.scalar.activation(actT, ps[:, 4, :].rearrange("p (j t) -> p j t", j=4), ACT.Copy)\
                      .then_inc(actT_ready, 1)
                    act.wait_ge(weights_used, n * PER_EXPERT + (M0 + PER_EXPERT))
                    nc.scalar.activation(y, ps[:, 5, :], ACT.Copy).then_inc(y_ready, 1)

            with act.Fori(0, GROUPS) as it:
                experts(it)
            act.wait_ge(flag_ready, 1)
            over = act.value_load(flag_i[0:1, 0:1], min_val=0, max_val=1)
            with act.If(over > 0):
                with act.Fori(1, BLOCKS) as j:
                    with act.Fori(0, GROUPS) as i:
                        experts(j * GROUPS + i)

            nc.scalar.activation(rs2[:, 0:1], rs2[:, 0:1], ACT.Sqrt)
            for i in range(TT):
                for c in range(2):
                    act.wait_ge(last_added, 2 * i + c + 1)
                    nc.scalar.activation(sqf[:, i, 512 * c:512 * c + 512], X[:, i, 512 * c:512 * c + 512], ACT.Square,
                                         accum_out=ssh[:, 2 * i + c:2 * i + c + 1]).then_inc(f_sumsq, 1)
                act.wait_ge(f_var, i + 1)
                nc.scalar.activation(rsf[:, i:i + 1], ssf[:, i:i + 1], ACT.Sqrt).then_inc(f_std, 1)

        @block.vector
        def _(dve):
            chain = [0]

            def link(ins):
                chain[0] += 1
                ins.then_inc(dve_chain, 1)
                dve.wait_ge(dve_chain, chain[0])

            V = nc.vector
            V.memset(dummy, 1.0)
            V.memset(ssx[:, 2:3], 1.0).then_inc(ssx_set, 1)
            dve.wait_ge(x0_sumsq, 1)
            V.tensor_scalar(ssx[:, 0:1], ssx[:, 0:1], 1.0 / D, EPS, ALU.mult, ALU.add).then_inc(x0_var, 1)
            dve.wait_ge(vecT_done, 1)
            V.tensor_copy(vec[:, :], ps[:, 7, 0:NVEC]).then_inc(vec_read, 1)
            dve.wait_ge(x0_std, 1)
            link(V.reciprocal(rsx[:, 0:1], rsx[:, 0:1]))
            V.tensor_scalar(xs[:, 0, :], X[:, 0, :], rsx[:, 0:1], None, ALU.mult).then_inc(x0s_ready, 1)
            dve.wait_ge(x_sumsq, 1)
            V.tensor_scalar(ssx[:, 1:2], ssx[:, 1:2], 1.0 / D, EPS, ALU.mult, ALU.add).then_inc(x_var, 1)
            dve.wait_ge(x_std, 1)
            link(V.reciprocal(rsx[:, 1:2], rsx[:, 1:2]))
            V.tensor_scalar(xs[:, 1, :], X[:, 1, :], rsx[:, 1:2], None, ALU.mult).then_inc(x1s_ready, 1)
            dve.wait_ge(x_sumsq, 2)
            V.tensor_scalar(ssx[:, 2:3], ssx[:, 2:3], 1.0 / D, EPS, ALU.mult, ALU.add).then_inc(x_var, 1)
            dve.wait_ge(x_std, 2)
            V.reciprocal(rsx[:, 2:3], rsx[:, 2:3]).then_inc(rsx_ready, 1)
            dve.wait_ge(vec_read, 1)
            lam = vec[:, VEC_AT["rg_lambda"]:VEC_AT["rg_lambda"] + 8]
            V.tensor_scalar(hba, vec[:, VEC_AT["b_rg_a"]:VEC_AT["b_rg_a"] + 8], 0.5, None, ALU.mult)
            V.tensor_scalar(hbx, vec[:, VEC_AT["b_rg_x"]:VEC_AT["b_rg_x"] + 8], 0.5, None, ALU.mult)
            V.tensor_scalar(hbg, vec[:, VEC_AT["b_gate"]:VEC_AT["b_gate"] + 16], 0.5, None, ALU.mult).then_inc(vec_ready, 1)
            for i in range(1, KT, 2):
                dve.wait_ge(xT_done, i + 1)
                V.tensor_scalar(xnT[:, i, :], ps[:, i, 0:T], v("norm_mix_g", i), None, ALU.mult).then_inc(xT_read_dve, 1)
            link(V.tensor_scalar(sp[:, 8:16], lam, -1.0, None, ALU.mult))
            V.tensor_tensor(sp[:, 0:8], sp[:, 8:16], lam, ALU.max).then_inc(softplus_in, 1)
            dve.wait_ge(sp_exp, 1)
            link(V.tensor_scalar(sp[:, 16:24], sp[:, 0:8], 2.0, None, ALU.add))
            link(V.reciprocal(sp[:, 16:24], sp[:, 16:24]))
            link(V.tensor_tensor(sp[:, 16:24], sp[:, 0:8], sp[:, 16:24], ALU.mult))
            link(V.tensor_tensor(sp[:, 0:8], sp[:, 16:24], sp[:, 16:24], ALU.mult))
            link(V.tensor_scalar(sp[:, 24:32], sp[:, 0:8], 1.0 / 17, 1.0 / 15, ALU.mult, ALU.add))
            for d in (13, 11, 9, 7, 5, 3, 1):
                link(V.tensor_tensor(sp[:, 24:32], sp[:, 24:32], sp[:, 0:8], ALU.mult))
                link(V.tensor_scalar(sp[:, 24:32], sp[:, 24:32], 1.0 / d, None, ALU.add))
            link(V.tensor_tensor(sp[:, 24:32], sp[:, 24:32], sp[:, 16:24], ALU.mult))
            link(V.tensor_scalar(sp[:, 8:16], sp[:, 8:16], 0.0, None, ALU.max))
            link(V.scalar_tensor_tensor(out=sp[:, 24:32], in0=sp[:, 24:32], scalar=2.0, in1=sp[:, 8:16],
                                        op0=ALU.mult, op1=ALU.add))
            V.tensor_scalar(hc, sp[:, 24:32], -LRU_C / 2, None, ALU.mult)
            V.tensor_scalar(hc2, sp[:, 24:32], -LRU_C, None, ALU.mult)
            V.tensor_scalar(nhc, sp[:, 24:32], LRU_C / 2, None, ALU.mult).then_inc(hc_ready, 1)

            dve.wait_ge(xT_done, KT)
            V.memset(rxp[:, :, 0:CONV - 1], 0.0).then_inc(xs_read, 1)
            dve.wait_ge(proj_read, JOB[("cq", QT - 1)] + 1)
            V.tensor_tensor(sqq, cq, cq, ALU.mult).then_inc(lora_sq, 1)
            dve.wait_ge(proj_read, JOB[("ckv", KVT - 1)] + 1)
            V.tensor_tensor(sqk, ckv, ckv, ALU.mult).then_inc(lora_sq, 1)

            def conv(i):
                k = i % 2
                dve.wait_ge(proj_read, JOB[("rx", i)] + 1)
                if k == 0 and i >= 2:
                    dve.wait_ge(proj_done, JOB[("ri", i - 1)] + 1)
                    dve.wait_ge(lru_arg, i // 2)
                link(V.tensor_scalar(xc[:, k, :], rxp[:, k, 3:3 + T], v("conv_w", 8 * 3 + i), v("conv_b", i),
                                     ALU.mult, ALU.add))
                for w in (2, 1, 0):
                    ins = V.scalar_tensor_tensor(out=xc[:, k, :], in0=rxp[:, k, w:w + T], scalar=v("conv_w", 8 * w + i),
                                                 in1=xc[:, k, :], op0=ALU.mult, op1=ALU.add)
                    if w:
                        link(ins)
                ins.then_inc(conv_ready, 1)

            dve.wait_ge(xs_read, 1)
            dve.wait_ge(lora_sum, 2)
            V.tensor_scalar(rq, ps[:, 4, 0:SEQ], 1.0 / Q_LORA, EPS, ALU.mult, ALU.add).then_inc(lora_var, 1)
            V.tensor_scalar(rk, ps[:, 5, 0:T], 1.0 / KV_LORA, EPS, ALU.mult, ALU.add).then_inc(lora_var, 1)
            dve.wait_ge(lora_std, 2)
            link(V.reciprocal(rq, rq))
            for k in range(QT):
                ins = V.scalar_tensor_tensor(out=cq[:, k, :], in0=cq[:, k, :], scalar=v("q_norm_g", k), in1=rq,
                                             op0=ALU.mult, op1=ALU.mult)
            ins.then_inc(lora_ready, 1)
            link(V.reciprocal(rk, rk))
            for k in range(KVT):
                ins = V.scalar_tensor_tensor(out=ckv[:, k, :], in0=ckv[:, k, :], scalar=v("kv_norm_g", k), in1=rk,
                                             op0=ALU.mult, op1=ALU.mult)
            ins.then_inc(lora_ready, 1)
            conv(0)
            conv(1)

            dve.wait_ge(krot_done, 1)
            ku = ropeu[NOPE:QD, :, :].rearrange("p k t -> p (k t)")[:, 0:T]
            V.tensor_tensor(ku, ps[NOPE:QD, 6, 0:T], sinT, ALU.mult)
            link(V.tensor_tensor(kh[NOPE:QD, 0, :], kh[NOPE:QD, 0, :], cosT, ALU.mult))
            link(V.tensor_tensor(kh[NOPE:QD, 0, :], kh[NOPE:QD, 0, :], ku, ALU.add))
            V.tensor_copy(kh[NOPE:QD, 1:HEADS, :], kh[NOPE:QD, 0:1, :].broadcast_to([ROPE, HEADS - 1, T]))\
             .then_inc(rope_ready, 1)
            def gelu_arg_of(p):
                dve.wait_ge(proj_read, JOB[("rg", 2 * p + 1)] + 1)
                link(V.tensor_scalar(ug, ug, 0.044715, 1.0, ALU.mult, ALU.add))
                V.tensor_tensor(ug, ug, xg, ALU.mult).then_inc(gelu_arg, 1)

            gelu_arg_of(0)
            cos2 = ca[NOPE:QD, CA["cos"][0] + N_META:CA["cos"][1]].rearrange("p (a t) -> p a t", a=1).broadcast_to([ROPE, 2, SEQ])
            sin2 = ca[NOPE:QD, CA["sin"][0] + N_META:CA["sin"][1]].rearrange("p (a t) -> p a t", a=1).broadcast_to([ROPE, 2, SEQ])
            for g in range(4):
                dve.wait_ge(qrot_done, g + 1)
                q2 = qh[NOPE:QD, 2 * g:2 * g + 2, :]
                V.tensor_tensor(ropeu[NOPE:QD, :, :], ps[NOPE:QD, 4 + g, :].rearrange("p (h t) -> p h t", h=2), sin2, ALU.mult)
                link(V.tensor_tensor(q2, q2, cos2, ALU.mult))
                ins = V.tensor_tensor(q2, q2, ropeu[NOPE:QD, :, :], ALU.add)
                if g < 3:
                    ins.then_inc(rope_ready, 1)
                    dve.wait_ge(rope_ready, g + 2)
                else:
                    ins.then_inc(rope_ready, 1)

            def gelu_end(p):
                dve.wait_ge(gelu_tanh, p + 1)
                V.scalar_tensor_tensor(out=gel[:, 2 * p:2 * p + 2, :], in0=ug, scalar=1.0, in1=xg,
                                       op0=ALU.add, op1=ALU.mult).then_inc(gelu_free, 1)

            def recur_arg(p):
                dve.wait_ge(proj_read, JOB[("ri", 2 * p + 1)] + 1)
                V.scalar_tensor_tensor(out=ti, in0=ti, scalar=1.0, in1=xc, op0=ALU.add, op1=ALU.mult)
                dve.wait_ge(lru_tanh, p + 1)
                V.scalar_tensor_tensor(out=th, in0=tr, scalar=1.0, in1=th, op0=ALU.add, op1=ALU.mult).then_inc(lru_arg, 1)

            def recur(p):
                dve.wait_ge(lru_sqrt, p + 1)
                dve.wait_ge(gelu_free, p + 1)
                link(V.tensor_tensor(ti, ti, th, ALU.mult))
                V.tensor_tensor_scan(tr[:, 0, :], av[:, 0, :], ti[:, 0, :], 0.0, ALU.mult, ALU.add)
                link(V.tensor_tensor_scan(tr[:, 1, :], av[:, 1, :], ti[:, 1, :], 0.0, ALU.mult, ALU.add))
                g2 = gel[:, 2 * p:2 * p + 2, :]
                V.scalar_tensor_tensor(out=g2, in0=g2, scalar=0.5, in1=tr[:, :, N_META:T], op0=ALU.mult, op1=ALU.mult)\
                 .then_inc(recurrence_done, 1)

            def softmax_in(s):
                b = UNITS[s][1]
                k = s % 2
                w = nk(b)
                dve.wait_ge(scores_done, s + 1)
                if s >= 2:
                    dve.wait_ge(probsT_done, s - 1)
                ins = V.scalar_tensor_tensor(out=S[:, k, 0:w], in0=ps[:, 4 + k, 0:w], scalar=SCALE,
                                             in1=maskc[:, T - w:T], op0=ALU.mult, op1=ALU.add)
                ins.then_inc(scores_read, 1)
                dve.wait_ge(scores_read, s + 1)
                link(V.tensor_reduce(mx[:, k:k + 1], S[:, k, 0:w], AX_X, ALU.max))
                V.tensor_scalar(nmx[:, k:k + 1], mx[:, k:k + 1], -1.0, None, ALU.mult).then_inc(rowmax_ready, 1)

            def softmax_out(s):
                b = UNITS[s][1]
                k = s % 2
                dve.wait_ge(exp_done, s + 1)
                link(V.reciprocal(rsm[:, k:k + 1], sm[:, k:k + 1]))
                V.tensor_scalar(S[:, k, 0:nk(b)], S[:, k, 0:nk(b)], rsm[:, k:k + 1], None, ALU.mult).then_inc(probs_ready, 1)

            def attention_step(s):
                if s < NU:
                    softmax_in(s)
                if s < NU:
                    softmax_out(s)

            def merge_rec(i):
                dve.wait_ge(proj_read, JOB[("gr", i)] + 1)
                dve.wait_ge(branch_done, i + 1)
                V.scalar_tensor_tensor(out=mT[:, i, :], in0=ta[:, i % 4, :], scalar=1.0, in1=ps[:, (3, 7)[i % 2], 0:SEQ],
                                       op0=ALU.add, op1=ALU.mult).then_inc(branch_read, 1)

            def merge_attn(i):
                dve.wait_ge(proj_read, JOB[("ga", i)] + 1)
                dve.wait_ge(branch_done, KT + i + 1)
                link(V.scalar_tensor_tensor(out=ta[:, i % 4, :], in0=ta[:, i % 4, :], scalar=1.0,
                                            in1=ps[:, (3, 7)[i % 2], 0:SEQ], op0=ALU.add, op1=ALU.mult))
                V.tensor_tensor(mT[:, i, :], mT[:, i, :], ta[:, i % 4, :], ALU.add).then_inc(branch_read, 1)

            gelu_end(0)
            for job in jobs[JOB[("ra", 0)]:JOB[("ga", 0)]]:
                kind, i = job
                if job == ("gr", 0):
                    gelu_end(3)
                if job in step_after:
                    attention_step(step_after[job])
                if kind == "rx":
                    if i % 2 == 0 and i > 2:
                        gelu_end(i // 2 - 1)
                    if i % 2 == 1:
                        recur(i // 2 - 1)
                    conv(i)
                if kind == "rg" and i % 2 == 1:
                    gelu_arg_of(i // 2)
                if kind == "ri" and i % 2 == 1:
                    recur_arg(i // 2)
                if job == ("gr", 1):
                    recur(3)
                if kind == "gr" and i % 2 == 1 and i > 1:
                    merge_rec(i - 3)
                    merge_rec(i - 2)
            merge_rec(KT - 2)
            merge_rec(KT - 1)

            for i in range(KT):
                merge_attn(i)

            def pick_tokens(n):
                for i in range(TT):
                    ins = V.tensor_scalar(pick[:, i, :], slot_id[:, 0:CAP], posm[:, i, bass.ds(n, 1)], None, ALU.is_equal)
                ins.then_inc(pick_ready, 1)

            def route(n, par):
                for i in range(TT):
                    V.tensor_scalar(gpick[:, i, :], slot_id, posm[:, i, bass.ds(n, 1)], gate[:, i, bass.ds(n, 1)],
                                    ALU.is_equal, ALU.mult)
                V.tensor_scalar(sel[0:E, par, :], ones[0:E, 0:CAP], pick_e[0:E, bass.ds(n, 1)], None, ALU.mult)\
                 .then_inc(route_ready, 1)

            t8 = top8.rearrange("p (i k) -> p i k", i=TT)

            def logits(i):
                dve.wait_ge(logits_done, i + 1)
                link(V.scalar_tensor_tensor(out=lg[:, i, :], in0=ps[:, i, 0:E], scalar=rs2[:, i:i + 1], in1=brt,
                                            op0=ALU.mult, op1=ALU.add))
                return V.max(t8[:, i, :], lg[:, i, :])

            def normed(i):
                V.scalar_tensor_tensor(out=xn2[:, i, :], in0=X[:, i, :], scalar=rs2[:, i:i + 1], in1=gffn,
                                       op0=ALU.mult, op1=ALU.mult).then_inc(xn2_ready, 1)

            for i in range(TT):
                if i == 0:
                    dve.wait_ge(out_done, 1)
                else:
                    dve.wait_ge(weights_used, M0)
                for c in range(2):
                    xi = X[:, i, 512 * c:512 * c + 512]
                    ins = V.scalar_tensor_tensor(out=xi, in0=ps[:, 2 * i + c, :], scalar=0.5, in1=xi,
                                                 op0=ALU.mult, op1=ALU.add)
                    ins.then_inc(h_half, 1)
                if i == 0:
                    V.memset(y, 0.0).then_inc(y_zeroed, 1)
                    dve.wait_ge(moe_in, 16 * 5)
                    g8 = vec[:, VEC_AT["norm_ffn_g"]:VEC_AT["norm_ffn_g"] + KT].rearrange("p (k a) -> p k a", a=1)
                    V.tensor_tensor(wr, wr, g8.broadcast_to([P, KT, E]), ALU.mult).then_inc(wr_ready, 1)
                if i == 0:
                    dve.wait_ge(h_sumsq, i + 1)
                    V.tensor_scalar(ss2[:, i:i + 1], ss2[:, i:i + 1], 1.0 / D, EPS, ALU.mult, ALU.add).then_inc(h_var, 1)
                dve.wait_ge(hT_done, 2 * i + 2)
                V.tensor_copy(hT[:, i, 4:8, :], ps[:, 5 + 2 * i, :].rearrange("p (k t) -> p k t", k=4))\
                 .then_inc(hT_ready2, 1)
                if i == 1:
                    logits(0)
                    dve.wait_ge(h_sumsq, i + 1)
                    V.tensor_scalar(ss2[:, i:i + 1], ss2[:, i:i + 1], 1.0 / D, EPS, ALU.mult, ALU.add).then_inc(h_var, 1)
                dve.wait_ge(h_std, i + 1)
                link(V.reciprocal(rs2[:, i:i + 1], rs2[:, i:i + 1]))
                if i == 0:
                    normed(0)

            ins = logits(1)
            link(ins)
            V.tensor_scalar(nm1.rearrange("p (i k) -> p i k", k=1), t8[:, :, 0:1], -1.0, None, ALU.mult)
            k4 = t8[:, :, TOP_K - 1:TOP_K].broadcast_to([P, TT, E])
            gt, eq, rank = (tmp[:, 2 * q:2 * q + 2, :] for q in range(3))
            V.tensor_tensor(eq, lg, k4, ALU.is_equal)
            link(V.tensor_tensor(gt, lg, k4, ALU.is_gt))
            link(V.tensor_reduce(ngt, gt, AX_X, ALU.add))
            for i in range(TT):
                ins = V.tensor_tensor_scan(rank[:, i, :], ones[:, 0:E], eq[:, i, :], ngt[:, i:i + 1], ALU.mult, ALU.add)
            link(ins)
            link(V.scalar_tensor_tensor(out=eq, in0=rank, scalar=TOP_K + 0.5, in1=eq, op0=ALU.is_lt, op1=ALU.mult))
            V.tensor_tensor(selm, gt, eq, ALU.add).then_inc(mask_ready, 1)
            normed(1)
            dve.wait_ge(mask_ready, 1)
            dve.wait_ge(pos_done, 1)
            link(V.scalar_tensor_tensor(out=rank, in0=ps[:, 2, 0:TT * E].rearrange("p (i e) -> p i e", i=TT), scalar=1.0,
                                        in1=selm, op0=ALU.add, op1=ALU.mult))
            for j in range(BLOCKS + 1):
                w = min(E, NCOL - E * j)
                bb = block_base[:, E * j:E * j + w].rearrange("p (a n) -> p a n", a=1).broadcast_to([P, TT, w])
                ins = V.scalar_tensor_tensor(out=posm[:, :, E * j:E * j + w], in0=rank[:, :, 0:w], scalar=-1.0,
                                             in1=bb, op0=ALU.add, op1=ALU.subtract)
                if j == 0:
                    link(ins)
                    pick_tokens(0)
            dve.wait_ge(gexp_done, TT)
            link(V.tensor_tensor(lg, lg, selm, ALU.mult))
            link(V.tensor_reduce(esum, lg, AX_X, ALU.add))
            link(V.reciprocal(esum, esum))
            for i in range(TT):
                for j in range(BLOCKS + 1):
                    w = min(E, NCOL - E * j)
                    ins = V.tensor_scalar(gate[:, i, E * j:E * j + w], lg[:, i, 0:w], esum[:, i:i + 1], None, ALU.mult)
            ins.then_inc(gate_ready, 1)
            dve.wait_ge(gate_ready, 1)
            route(0, 0)
            dve.wait_ge(pos_done, 2)
            V.tensor_reduce(cmax[:, 0:1], ps[:, 3, 0:E], AX_X, ALU.max).then_inc(pos_done_read, 1)
            dve.wait_ge(pos_done_read, 1)
            link(V.tensor_scalar(cmax[:, 1:2], cmax[:, 0:1], CAP + 0.5, None, ALU.is_gt))
            V.tensor_copy(flag_i[0:1, 0:1], cmax[0:1, 1:2]).then_inc(flag_ready, 1)
            dve.sem_inc(hidden_read, 1)
            dve.sem_inc(scat_added, 1)
            dve.wait_ge(xeT_done, 1)
            V.tensor_copy(xeT, ps[:, 3, :].rearrange("p (j t) -> p j t", j=4)).then_inc(xeT_ready, 1)

            def experts(it):
                for u in range(UNROLL):
                    n = it * UNROLL + u
                    dve.wait_ge(gpickT_done, n + 1)
                    pick_tokens(n + 1)
                    route(n + 1, (u + 1) % 2)
                    for i in range(TT):
                        dve.wait_ge(scat_done, n * TT + (i + 1))
                        xi = X[:, i, :].rearrange("p (c n) -> p c n", c=2)
                        V.tensor_tensor(xi, ps[:, 6:8, :], xi, ALU.add).then_inc(scat_added, 1)
                    dve.wait_ge(weights_used, n * PER_EXPERT + (M0 + KT))
                    V.tensor_scalar(hg, ps[:, 0, :], LIMIT, None, ALU.min).then_inc(glu_ready, 1)
                    V.tensor_scalar(hl, ps[:, 1, :], LIMIT, -LIMIT, ALU.min, ALU.max).then_inc(hidden_read, 1)
                    dve.wait_ge(hidden_read, n + 2)
                    V.scalar_tensor_tensor(out=hl, in0=hl, scalar=1.0, in1=hg, op0=ALU.add, op1=ALU.mult)\
                     .then_inc(lin_ready, 1)
                    dve.wait_ge(lin_ready, n + 1)
                    dve.wait_ge(sig_done, n + 1)
                    V.tensor_tensor(act_h, hl, sg, ALU.mult).then_inc(act_ready, 1)
                    dve.wait_ge(xeT_done, n + 2)
                    V.tensor_copy(xeT, ps[:, 3, :].rearrange("p (j t) -> p j t", j=4)).then_inc(xeT_ready, 1)

            with dve.Fori(0, GROUPS) as it:
                experts(it)
            dve.wait_ge(flag_ready, 1)
            over = dve.value_load(flag_i[0:1, 0:1], min_val=0, max_val=1)
            with dve.If(over > 0):
                with dve.Fori(1, BLOCKS) as j:
                    with dve.Fori(0, GROUPS) as i:
                        experts(j * GROUPS + i)
            def add_last(i, c):
                dve.wait_ge(last_scat, 2 * i + c + 1)
                xi = X[:, i, 512 * c:512 * c + 512]
                V.tensor_tensor(xi, ps[:, (6 if i == 0 else 0) + c, :], xi, ALU.add).then_inc(last_added, 1)

            def final_var(i):
                dve.wait_ge(f_sumsq, 2 * i + 2)
                link(V.tensor_tensor(ssf[:, i:i + 1], ssh[:, 2 * i:2 * i + 1], ssh[:, 2 * i + 1:2 * i + 2], ALU.add))
                V.tensor_scalar(ssf[:, i:i + 1], ssf[:, i:i + 1], 1.0 / D, EPS, ALU.mult, ALU.add).then_inc(f_var, 1)

            def final_norm(i):
                dve.wait_ge(f_std, i + 1)
                link(V.reciprocal(rsf[:, i:i + 1], rsf[:, i:i + 1]))
                V.scalar_tensor_tensor(out=X[:, i, :], in0=X[:, i, :], scalar=rsf[:, i:i + 1], in1=gfin,
                                       op0=ALU.mult, op1=ALU.mult).then_inc(fin_ready, 1)

            dve.wait_ge(gfin_in, 16)
            add_last(0, 0)
            add_last(0, 1)
            add_last(1, 0)
            final_var(0)
            add_last(1, 1)
            final_norm(0)
            final_var(1)
            final_norm(1)


_INS = ["x", "meta_tokens", "vec", "ca", "cb", "w_in", "w_uq", "w_ukv", "w_ao", "w_rg_a", "w_rg_x", "w_ro", "w_out",
        "norm_ffn_g", "w_router", "b_router", "w_up", "b_up", "w_down", "b_down", "norm_final_g"]


def kernel(**inputs):
    import concourse.bacc as _bacc
    from concourse.bass_utils import run_bass_kernel_spmd as _run

    arrays = {k: np.ascontiguousarray(np.asarray(a)) for k, a in inputs.items()}
    arrays["vec"] = np.concatenate([arrays[name].reshape(rows, P) for name, rows in VEC_ROWS], axis=0)
    arrays["ca"], arrays["cb"] = constants()
    nc = _bacc.Bacc("TRN2", target_bir_lowering=False, num_devices=1)
    feed, args = {}, []
    for name in _INS:
        a = arrays[name]
        feed[f"in_{name}_dram"] = a
        args.append(nc.dram_tensor(f"in_{name}_dram", a.shape, mybir.dt.from_np(a.dtype), kind="ExternalInput").ap())
    args.append(nc.dram_tensor("out_0_dram", (1, SEQ, D), F32, kind="ExternalOutput").ap())
    layer(nc, *args)
    r = _run(nc, [feed], core_ids=[0])
    return r.results[0]["out_0_dram"]
```
